# Optimizing a Trainium2 kernel written in Bass

```python
import jax
import jax.numpy as jnp
from jax import lax
import numpy as np

D_MODEL = 1024
BATCH = 1
SEQ = 512
DEPTH = 2

HEAD_DIM = 64
ROPE_THETA = 10000.0
NORM_EPS = 1e-6
Q_BLOCK = 128

CONV_CHANNELS = 512
CONV_WIDTH = 3
DSA_HEADS = 8
IDX_HEADS = 4
IDX_DIM = HEAD_DIM
DSA_TOPK_MAX = 256
DIL_HEADS = 16
DIL_KV_HEADS = 4
DIL_PATTERNS = ((128, 1), (512, 4), (2048, 16))
N_GROUPS = 4
EXPERTS_PER_GROUP = 8
N_EXPERTS = N_GROUPS * EXPERTS_PER_GROUP
TOP_K_INNER = 2
D_EXPERT = 512
MOE_BLOCK = 256

EVEN_SPLITS = (CONV_CHANNELS, CONV_CHANNELS, CONV_CHANNELS,
               DSA_HEADS * HEAD_DIM, HEAD_DIM, HEAD_DIM,
               IDX_HEADS * IDX_DIM, IDX_DIM, IDX_HEADS)
ODD_SPLITS = (DIL_HEADS * HEAD_DIM, DIL_KV_HEADS * HEAD_DIM, DIL_KV_HEADS * HEAD_DIM)
EVEN_IN_WIDTH = sum(EVEN_SPLITS)
ODD_IN_WIDTH = sum(ODD_SPLITS)
EVEN_MIX_WIDTH = CONV_CHANNELS + DSA_HEADS * HEAD_DIM
ODD_MIX_WIDTH = DIL_HEADS * HEAD_DIM

kernel_name = 'hybrid_conv_dsa_dilated_hmoe'

def rms_norm(x, gain):
    xf = x.astype(jnp.float32)
    y = xf * lax.rsqrt(jnp.mean(xf * xf, axis=-1, keepdims=True) + NORM_EPS)
    return (y * gain.astype(jnp.float32)).astype(x.dtype)

def rope_tables(seq_len):
    half = HEAD_DIM // 2
    inv_freq = ROPE_THETA ** (-jnp.arange(half, dtype=jnp.float32) / half)
    ang = jnp.arange(seq_len, dtype=jnp.float32)[:, None] * inv_freq[None, :]
    return jnp.cos(ang), jnp.sin(ang)

def apply_rope(x, cos, sin):
    xf = x.astype(jnp.float32)
    x1, x2 = jnp.split(xf, 2, axis=-1)
    c = cos[None, :, None, :]
    s = sin[None, :, None, :]
    return jnp.concatenate([x1 * c - x2 * s, x1 * s + x2 * c], axis=-1).astype(x.dtype)

def split_cols(proj, sizes):
    return jnp.split(proj, np.cumsum(sizes)[:-1].tolist(), axis=-1)

def short_gated_conv(gate_b, gate_c, h, conv_w):
    u = gate_c * h
    seq = u.shape[1]
    u_pad = jnp.pad(u, ((0, 0), (CONV_WIDTH - 1, 0), (0, 0)))
    y = sum(u_pad[:, j:j + seq, :] * conv_w[:, j] for j in range(CONV_WIDTH))
    return gate_b * y

def _gather_rows(table, idx):
    return jax.vmap(lambda t, i: t[i])(table, idx)

def dsa_attention(q, k, v, iq, ik, iw):
    bsz, seq, n_heads, hd = q.shape
    top_k = min(DSA_TOPK_MAX, seq // 4)
    ikf = ik.astype(jnp.float32)
    key_pos = jnp.arange(seq)

    def block(start):
        qb = lax.dynamic_slice_in_dim(q, start, Q_BLOCK, axis=1)
        iqb = lax.dynamic_slice_in_dim(iq, start, Q_BLOCK, axis=1).astype(jnp.float32)
        iwb = lax.dynamic_slice_in_dim(iw, start, Q_BLOCK, axis=1).astype(jnp.float32)
        q_pos = start + jnp.arange(Q_BLOCK)
        rel = jax.nn.relu(jnp.einsum('bqhd,bsd->bqhs', iqb, ikf) * IDX_DIM ** -0.5)
        score = jnp.einsum('bqhs,bqh->bqs', rel, iwb)
        causal = key_pos[None, :] <= q_pos[:, None]
        score = jnp.where(causal[None], score, -jnp.inf)
        _, idx = lax.top_k(score, top_k)
        valid = idx <= q_pos[None, :, None]
        ks = _gather_rows(k, idx)
        vs = _gather_rows(v, idx)
        logits = jnp.einsum('bqhd,bqjd->bqhj', qb, ks).astype(jnp.float32) * hd ** -0.5
        logits = jnp.where(valid[:, :, None, :], logits, -jnp.inf)
        p = jax.nn.softmax(logits, axis=-1).astype(vs.dtype)
        return jnp.einsum('bqhj,bqjd->bqhd', p, vs)

    starts = jnp.arange(seq // Q_BLOCK) * Q_BLOCK
    out = lax.map(block, starts)
    return out.transpose(1, 0, 2, 3, 4).reshape(bsz, seq, n_heads * hd)

def dilated_attention(q, k, v):
    bsz, seq, n_heads, hd = q.shape
    n_kv = k.shape[2]
    qg = q.reshape(bsz, seq, n_kv, n_heads // n_kv, hd)

    def block(start):
        qb = lax.dynamic_slice_in_dim(qg, start, Q_BLOCK, axis=1)
        q_pos = start + jnp.arange(Q_BLOCK)
        lses, outs = [], []
        for window, dilation in DIL_PATTERNS:
            n_keys = window // dilation + 1
            pos = q_pos[:, None] - dilation * jnp.arange(n_keys)[None, :]
            valid = pos >= 0
            pos = jnp.maximum(pos, 0)
            ks = jnp.take(k, pos, axis=1)
            vs = jnp.take(v, pos, axis=1)
            logits = jnp.einsum('bqkgd,bqjkd->bqkgj', qb, ks).astype(jnp.float32) * hd ** -0.5
            logits = jnp.where(valid[None, :, None, None, :], logits, -jnp.inf)
            lse = jax.nn.logsumexp(logits, axis=-1, keepdims=True)
            p = jnp.exp(logits - lse).astype(vs.dtype)
            outs.append(jnp.einsum('bqkgj,bqjkd->bqkgd', p, vs).astype(jnp.float32))
            lses.append(lse)
        wts = jax.nn.softmax(jnp.stack(lses), axis=0)
        return jnp.sum(wts * jnp.stack(outs), axis=0).astype(q.dtype)

    starts = jnp.arange(seq // Q_BLOCK) * Q_BLOCK
    out = lax.map(block, starts)
    return out.transpose(1, 0, 2, 3, 4, 5).reshape(bsz, seq, n_heads * hd)

def grouped_expert_ffn(xt, expert_ids, gates, w_gate, w_up, w_down):
    n_tok, d = xt.shape
    n_assign = n_tok * TOP_K_INNER
    flat_e = expert_ids.reshape(n_assign)
    flat_tok = jnp.arange(n_assign) // TOP_K_INNER
    flat_gate = gates.reshape(n_assign)
    order = jnp.argsort(flat_e)
    sorted_e = flat_e[order]
    counts = jnp.bincount(flat_e, length=N_EXPERTS)
    padded = ((counts + MOE_BLOCK - 1) // MOE_BLOCK) * MOE_BLOCK
    start_sorted = jnp.cumsum(counts) - counts
    pad_end = jnp.cumsum(padded)
    start_pad = pad_end - padded
    rank = jnp.arange(n_assign) - start_sorted[sorted_e]
    dest = start_pad[sorted_e] + rank
    n_blocks = -(-n_assign // MOE_BLOCK) + N_EXPERTS
    n_rows = n_blocks * MOE_BLOCK
    row_tok = jnp.full((n_rows,), n_tok, dtype=jnp.int32).at[dest].set(flat_tok[order].astype(jnp.int32))
    row_gate = jnp.zeros((n_rows,), dtype=flat_gate.dtype).at[dest].set(flat_gate[order])
    block_expert = jnp.clip(jnp.searchsorted(pad_end, jnp.arange(n_blocks) * MOE_BLOCK, side='right'), 0, N_EXPERTS - 1)
    x_pad = jnp.concatenate([xt, jnp.zeros((1, d), xt.dtype)], axis=0)
    xs = x_pad[row_tok].reshape(n_blocks, MOE_BLOCK, d)

    def expert_block(args):
        xb, e = args
        h = jax.nn.silu(xb @ w_gate[e]) * (xb @ w_up[e])
        return h @ w_down[e]

    ys = lax.map(expert_block, (xs, block_expert)).reshape(n_rows, d)
    out = jnp.zeros((n_tok + 1, d), ys.dtype).at[row_tok].add(ys * row_gate[:, None].astype(ys.dtype))
    return out[:n_tok]

def hierarchical_moe(x, w_rg, b_rg, w_re, b_re, w_gate, w_up, w_down):
    bsz, seq, d = x.shape
    xt = x.reshape(bsz * seq, d)
    p_group = jax.nn.softmax((xt @ w_rg + b_rg).astype(jnp.float32), axis=-1)
    pg_top, g_sel = lax.top_k(p_group, 1)
    le = (jnp.einsum('nd,gde->nge', xt, w_re) + b_re).astype(jnp.float32)
    le_sel = jnp.take_along_axis(le, g_sel[:, :, None], axis=1)[:, 0]
    pe_top, e_sel = lax.top_k(jax.nn.softmax(le_sel, axis=-1), TOP_K_INNER)
    pe_top = pe_top / jnp.sum(pe_top, axis=-1, keepdims=True)
    gates = pg_top * pe_top
    expert_ids = g_sel * EXPERTS_PER_GROUP + e_sel
    y = grouped_expert_ffn(xt, expert_ids, gates, w_gate, w_up, w_down)
    return y.reshape(bsz, seq, d)

def even_mixer(x, cos, sin, attn_norm, w_in, conv_w, q_norm, k_norm, w_out):
    bsz, seq, _ = x.shape
    h = rms_norm(x, attn_norm)
    cb, cc, ch, q, k, v, iq, ik, iw = split_cols(h @ w_in, EVEN_SPLITS)
    a_out = short_gated_conv(cb, cc, ch, conv_w)
    q = apply_rope(rms_norm(q.reshape(bsz, seq, DSA_HEADS, HEAD_DIM), q_norm), cos, sin)
    k = apply_rope(rms_norm(k, k_norm)[:, :, None, :], cos, sin)[:, :, 0]
    iq = apply_rope(iq.reshape(bsz, seq, IDX_HEADS, IDX_DIM), cos, sin)
    ik = apply_rope(ik[:, :, None, :], cos, sin)[:, :, 0]
    b_out = dsa_attention(q, k, v, iq, ik, iw * IDX_HEADS ** -0.5)
    return x + jnp.concatenate([a_out, b_out], axis=-1) @ w_out

def odd_mixer(x, cos, sin, attn_norm, w_in, q_norm, k_norm, w_out):
    bsz, seq, _ = x.shape
    h = rms_norm(x, attn_norm)
    q, k, v = split_cols(h @ w_in, ODD_SPLITS)
    q = apply_rope(rms_norm(q.reshape(bsz, seq, DIL_HEADS, HEAD_DIM), q_norm), cos, sin)
    k = apply_rope(rms_norm(k.reshape(bsz, seq, DIL_KV_HEADS, HEAD_DIM), k_norm), cos, sin)
    v = v.reshape(bsz, seq, DIL_KV_HEADS, HEAD_DIM)
    return x + dilated_attention(q, k, v) @ w_out

def moe_sublayer(x, ffn_norm, w_rg, b_rg, w_re, b_re, w_gate, w_up, w_down):
    return x + hierarchical_moe(rms_norm(x, ffn_norm), w_rg, b_rg, w_re, b_re, w_gate, w_up, w_down)

def setup_inputs(seed: int = 0) -> dict:
    key = jax.random.key(seed)
    ks = jax.random.split(key, 32)
    f32 = jnp.float32

    def nrm(k, shape, scale):
        return jax.random.normal(k, shape, f32) * scale

    def gain(k, n):
        return 1.0 + 0.02 * jax.random.normal(k, (n,), f32)

    d = D_MODEL
    inp = {}
    inp['x'] = nrm(ks[0], (BATCH, SEQ, d), 1.0)
    inp['attn_norm_0'] = gain(ks[1], d)
    inp['w_in_0'] = nrm(ks[2], (d, EVEN_IN_WIDTH), d ** -0.5)
    inp['conv_w_0'] = nrm(ks[3], (CONV_CHANNELS, CONV_WIDTH), CONV_WIDTH ** -0.5)
    inp['q_norm_0'] = gain(ks[4], HEAD_DIM)
    inp['k_norm_0'] = gain(ks[5], HEAD_DIM)
    inp['w_out_0'] = nrm(ks[6], (EVEN_MIX_WIDTH, d), EVEN_MIX_WIDTH ** -0.5)
    inp['ffn_norm_0'] = gain(ks[7], d)
    inp['w_rg_0'] = nrm(ks[8], (d, N_GROUPS), d ** -0.5)
    inp['b_rg_0'] = nrm(ks[9], (N_GROUPS,), 0.01)
    inp['w_re_0'] = nrm(ks[10], (N_GROUPS, d, EXPERTS_PER_GROUP), d ** -0.5)
    inp['b_re_0'] = nrm(ks[11], (N_GROUPS, EXPERTS_PER_GROUP), 0.01)
    inp['w_gate_0'] = nrm(ks[12], (N_EXPERTS, d, D_EXPERT), d ** -0.5)
    inp['w_up_0'] = nrm(ks[13], (N_EXPERTS, d, D_EXPERT), d ** -0.5)
    inp['w_down_0'] = nrm(ks[14], (N_EXPERTS, D_EXPERT, d), D_EXPERT ** -0.5)
    inp['attn_norm_1'] = gain(ks[15], d)
    inp['w_in_1'] = nrm(ks[16], (d, ODD_IN_WIDTH), d ** -0.5)
    inp['q_norm_1'] = gain(ks[17], HEAD_DIM)
    inp['k_norm_1'] = gain(ks[18], HEAD_DIM)
    inp['w_out_1'] = nrm(ks[19], (ODD_MIX_WIDTH, d), ODD_MIX_WIDTH ** -0.5)
    inp['ffn_norm_1'] = gain(ks[20], d)
    inp['w_rg_1'] = nrm(ks[21], (d, N_GROUPS), d ** -0.5)
    inp['b_rg_1'] = nrm(ks[22], (N_GROUPS,), 0.01)
    inp['w_re_1'] = nrm(ks[23], (N_GROUPS, d, EXPERTS_PER_GROUP), d ** -0.5)
    inp['b_re_1'] = nrm(ks[24], (N_GROUPS, EXPERTS_PER_GROUP), 0.01)
    inp['w_gate_1'] = nrm(ks[25], (N_EXPERTS, d, D_EXPERT), d ** -0.5)
    inp['w_up_1'] = nrm(ks[26], (N_EXPERTS, d, D_EXPERT), d ** -0.5)
    inp['w_down_1'] = nrm(ks[27], (N_EXPERTS, D_EXPERT, d), D_EXPERT ** -0.5)
    return inp

def reference(x, attn_norm_0, w_in_0, conv_w_0, q_norm_0, k_norm_0, w_out_0, ffn_norm_0,
              w_rg_0, b_rg_0, w_re_0, b_re_0, w_gate_0, w_up_0, w_down_0,
              attn_norm_1, w_in_1, q_norm_1, k_norm_1, w_out_1, ffn_norm_1,
              w_rg_1, b_rg_1, w_re_1, b_re_1, w_gate_1, w_up_1, w_down_1):
    cos, sin = rope_tables(x.shape[1])
    mixer_params = ((attn_norm_0, w_in_0, conv_w_0, q_norm_0, k_norm_0, w_out_0),
                    (attn_norm_1, w_in_1, q_norm_1, k_norm_1, w_out_1))
    moe_params = ((ffn_norm_0, w_rg_0, b_rg_0, w_re_0, b_re_0, w_gate_0, w_up_0, w_down_0),
                  (ffn_norm_1, w_rg_1, b_rg_1, w_re_1, b_re_1, w_gate_1, w_up_1, w_down_1))
    for layer in range(DEPTH):
        if layer % 2 == 0:
            x = even_mixer(x, cos, sin, *mixer_params[layer])
        else:
            x = odd_mixer(x, cos, sin, *mixer_params[layer])
        x = moe_sublayer(x, *moe_params[layer])
    return x


_drawn_inputs = setup_inputs


def setup_inputs(seed=0):
    import zlib

    import numpy as np

    out = dict(_drawn_inputs(seed))
    spreads = {}
    factors = {'q_norm_0': 3.833,
     'k_norm_0': 4.339,
     'b_rg_0': 8.0,
     'b_re_0': 3.687,
     'attn_norm_1': 3.59,
     'q_norm_1': 3.781,
     'k_norm_1': 5.428,
     'b_rg_1': 17.88,
     'b_re_1': 28.432,
     'ffn_norm_1': 7.57}
    for name, (base, spread) in spreads.items():
        noise = np.random.default_rng([zlib.crc32(name.encode()), seed]).standard_normal(out[name].shape)
        drawn = base * np.exp(spread * noise) if base else spread * noise
        out[name] = jnp.asarray(drawn.astype(out[name].dtype))
    for name, factor in factors.items():
        out[name] = (out[name] * factor).astype(out[name].dtype)
    return out
```

```python
import concourse.bass as bass
from concourse import mybir
from contextlib import ExitStack

TOKENS, D_MODEL, PARTS = 512, 1024, 128
TILES = TOKENS // PARTS
CHUNKS = D_MODEL // PARTS
N_GROUPS, PER_GROUP = 4, 8
N_EXPERTS = N_GROUPS * PER_GROUP
N_ROUTER = N_GROUPS + N_EXPERTS
HEAD = 64
HALF = HEAD // 2
ROPE_THETA = 10000.0
CONV = 512
TAPS = 3
N_CONV_COLS = 3 * CONV
DSA_HEADS, IDX_HEADS, DSA_KEEP = 8, 4, 128
N_QKV0 = (DSA_HEADS + 2) * HEAD
N_IDX0 = (IDX_HEADS + 1) * HEAD + IDX_HEADS
DIL_HEADS, DIL_KV = 16, 4
PATTERNS = ((128, 1), (512, 4), (2048, 16))
N_QK1 = (DIL_HEADS + DIL_KV) * HEAD
N_V1 = DIL_KV * HEAD
SCALE = HEAD ** -0.5
D_EXPERT = 512
TOP_K = 2
CAP = 64
LEVELS = TOKENS // CAP
NORM_EPS = 1e-6
BIG = 1e30
TAKEN = -3e38

CONST_WIDTHS = dict(ident=128, ones=128, before=128, iota_slot=128, iota_expert=32, iota_group=4,
                    token=4, half=1, pair_row=8, spare=32, half_less_spare=32, eps_pow=2,
                    rope_cos=256, rope_sin=256, strip=512, causal=128)
CONST_AT, _at = {}, 0
for _name, _width in CONST_WIDTHS.items():
    CONST_AT[_name] = (_at, _at + _width)
    _at += _width
N_CONST = _at


def constant_table():
    import numpy as np
    p = np.arange(PARTS)
    table = np.zeros((PARTS, N_CONST), np.float32)

    def put(name, value):
        a, b = CONST_AT[name]
        table[:, a:b] = value
    put("ident", np.eye(PARTS))
    put("ones", 1.0)
    put("before", p[:, None] < p[None, :])
    put("iota_slot", np.arange(PARTS)[None] % CAP)
    put("iota_expert", np.arange(N_EXPERTS)[None])
    put("iota_group", np.arange(N_GROUPS)[None])
    put("token", p[:, None] + PARTS * np.arange(TILES)[None])
    put("half", (p >= CAP)[:, None])
    put("pair_row", (4 * (p[:, None, None] + PARTS * np.arange(TILES)[None, :, None]) + 2 * np.arange(TOP_K)).reshape(PARTS, -1))
    spare = 2 * (TOP_K * TOKENS + CAP * np.arange(N_EXPERTS)[None] + (p % CAP)[:, None]) + (p >= CAP)[:, None]
    put("spare", spare)
    put("half_less_spare", (p >= CAP)[:, None] - spare)
    angle = np.arange(TOKENS)[:, None].astype(np.float32) * (ROPE_THETA ** (-np.arange(HALF, dtype=np.float32) / HALF)).astype(np.float32)
    by_tile = lambda v: v.reshape(TILES, PARTS, HEAD).transpose(1, 0, 2).reshape(PARTS, -1)
    put("rope_cos", by_tile(np.concatenate([np.cos(angle), np.cos(angle)], 1)))
    put("rope_sin", by_tile(np.concatenate([-np.sin(angle), np.sin(angle)], 1)))
    back = p[:, None] + (TOKENS - PARTS) - np.arange(TOKENS)[None]
    seen = sum(((back >= 0) & (back <= w) & (back % d == 0)).astype(int) for w, d in PATTERNS)
    put("strip", np.where(seen > 0, np.log(np.maximum(seen, 1)) / SCALE, -BIG))
    put("causal", np.where(p[None, :] <= p[:, None], 0.0, -BIG))
    put("eps_pow", [[NORM_EPS, -0.5]])
    return table


def trunk(nc, a, layers=(0, 1), mixers=True, moes=True):
    f32, i32 = mybir.dt.float32, mybir.dt.int32
    ALU, ACT, AX = mybir.AluOpType, mybir.ActivationFunctionType, mybir.AxisListType.X
    ctx = ExitStack()
    with ctx:
        def sb(name, shape, dt=f32):
            return ctx.enter_context(nc.sbuf_tensor(name, shape, dt))

        def sem(name):
            return ctx.enter_context(nc.semaphore(name))

        ring = sb("ring", [PARTS, 6, 4096])
        x_res = sb("x_res", [PARTS, TILES, D_MODEL])
        buf1 = sb("buf1", [PARTS, 4096])
        buf2 = sb("buf2", [PARTS, 4096])
        const = sb("const", [PARTS, N_CONST])
        w_router = sb("w_router", [PARTS, CHUNKS, N_ROUTER])
        b_router = sb("b_router", [PARTS, N_ROUTER])
        gain = sb("gain", [PARTS, 4, CHUNKS])
        w_mix = sb("w_mix", [PARTS, 12288])
        head_gain = sb("head_gain", [PARTS, 4, HEAD])
        rope = sb("rope", [PARTS, 4, TILES, HEAD])
        conv_w = sb("conv_w", [PARTS, CONV // PARTS, TAPS])
        idx_w = sb("idx_w", [PARTS, TILES, IDX_HEADS])
        best8 = sb("best8", [PARTS, 8])
        neg_max = sb("neg_max", [PARTS, 3])
        denom = sb("denom", [PARTS, 2, DIL_HEADS])
        head_ss = sb("head_ss", [PARTS, 2, DIL_HEADS + DIL_KV])
        sumsq = sb("sumsq", [PARTS, TILES])
        gates = sb("gates", [PARTS, TOP_K, TILES])
        fetch = sb("fetch", [PARTS, N_EXPERTS], i32)
        store = sb("store", [PARTS, N_EXPERTS], i32)
        fetch_now = sb("fetch_now", [PARTS, 2], i32)
        store_now = sb("store_now", [PARTS, 2], i32)
        max_count = sb("max_count", [PARTS, 1], i32)
        ps = ctx.enter_context(nc.psum_tensor("ps", [PARTS, 8, 512], f32))
        xn_dram = nc.dram_tensor("xn_dram", (TOKENS, D_MODEL), f32, kind="Internal").ap()
        ys_dram = nc.dram_tensor("ys_dram", (TOP_K * TOKENS + N_EXPERTS * CAP, D_MODEL), f32, kind="Internal").ap()

        def con(name):
            lo, hi = CONST_AT[name]
            return const[:, lo:hi]

        ident, ones, before = con("ident"), con("ones"), con("before")

        xn = buf1[:, :].rearrange("p (t d) -> p t d", t=TILES)
        xnT = buf2[:, :].rearrange("p (c n) -> p c n", c=CHUNKS)
        xg = [buf1[:, 512 * u:512 * u + 512] for u in range(2)]
        xT = [buf1[:, 1024 + 512 * u:1536 + 512 * u] for u in range(2)]
        ysb = [buf1[:, 2048 + 512 * u:2560 + 512 * u] for u in range(2)]
        silu = buf1[:, 3072:3328]
        h = buf1[:, 3328:3584]
        hT = buf1[:, 3584:3840]

        def b2(at, *dims):
            n = 1
            for d in dims:
                n *= d
            v = buf2[:, at:at + n]
            if len(dims) == 1:
                return v
            if len(dims) == 2:
                return v.rearrange("p (a b) -> p a b", a=dims[0])
            return v.rearrange("p (a b c) -> p a b c", a=dims[0], b=dims[1])
        slot_hot = b2(0, TILES, TOP_K, PARTS)
        row_hot = b2(2304, TILES, TOP_K, 3 * N_EXPERTS)
        hot = [b2(1280, TILES, N_EXPERTS), b2(1408, TILES, N_EXPERTS)]
        picked = b2(1536, TILES, N_EXPERTS)
        logit = b2(1664, TILES, N_ROUTER)
        lm = b2(1808, TILES, N_EXPERTS)
        tmp = b2(1936, TILES, N_EXPERTS)
        at4 = b2(2064, TILES, N_GROUPS)
        hot4 = b2(2080, TILES, N_GROUPS)
        exp4 = b2(2096, TILES, N_GROUPS)
        pen4 = b2(2112, TILES, N_GROUPS)
        gmax = b2(2128, TILES)
        gidx = b2(2132, TILES)
        top = [b2(2136, TILES), b2(2140, TILES)]
        eid = b2(2144, TOP_K, TILES)
        rank = b2(2152, TOP_K, TILES)
        storef = b2(2208, N_EXPERTS)
        gap = b2(2176, TILES)
        e21 = b2(2180, TILES)
        inv = b2(2184, TILES)
        p_group = b2(2188, TILES)
        cmax = b2(2192, 1)

        token_major = [buf2, buf1]
        feature_major = [buf1, buf2]
        mixed = buf2[:, :].rearrange("p (c n) -> p c n", c=CHUNKS)
        scratch = ring[:, 3:6, :].rearrange("p j n -> p (j n)")
        w_conv = ring[:, 0:3, :].rearrange("p j n -> p (j n)").rearrange("p (c n) -> p c n", c=CHUNKS)

        def part(buf, at, *dims):
            n = 1
            for d in dims:
                n *= d
            v = buf[:, at:at + n]
            if len(dims) == 2:
                v = v.rearrange("p (a b) -> p a b", a=dims[0])
            if len(dims) == 3:
                v = v.rearrange("p (a b c) -> p a b c", a=dims[0], b=dims[1])
            return v

        qT0 = part(scratch, 0, DSA_HEADS // 2, TOKENS)
        kT0 = part(scratch, 2048, 1, TOKENS)
        idxT = part(scratch, 2560, 3, TOKENS)
        v0 = part(scratch, 4096, TILES, HEAD)
        score = [None] + [part(scratch, at, n) for at, n in ((4352, 256), (4608, 384), (4992, 512))]
        relu = part(scratch, 5504, 2, TOKENS)
        idx_raw = part(scratch, 6528, TILES, N_IDX0)
        idx_sin = part(scratch, 7824, IDX_HEADS + 1, HEAD)
        qk_raw0 = part(scratch, 8144, 2, N_QKV0)
        qk_sq0 = part(scratch, 9424, N_QKV0)
        qk_sin0 = part(scratch, 10064, DSA_HEADS + 1, HEAD)
        conv_in = part(scratch, 6528, 3, TOKENS)
        conv_u = part(scratch, 8064, TOKENS + TAPS - 1)
        conv_y = part(scratch, 8578, 2, TOKENS)
        idx_rot = part(buf2, 0, TILES, 3 * PARTS)
        qk_rot0 = part(buf2, 1536, TILES, 5 * PARTS)
        w_idx = part(w_mix, 0, CHUNKS, N_IDX0)
        w_qkv0 = part(w_mix, CHUNKS * N_IDX0, CHUNKS, N_QKV0)
        qT1 = part(scratch, 0, DIL_HEADS // 2, TOKENS)
        kT1 = part(scratch, 4096, DIL_KV, TOKENS)
        v1 = part(scratch, 6144, TILES, N_V1)
        qk_raw1 = part(scratch, 7168, N_QK1)
        qk_sq1 = part(scratch, 8448, N_QK1)
        qk_rot1 = part(scratch, 9728, DIL_HEADS * HEAD + 2 * DIL_KV * HEAD)
        w_in1 = part(w_mix, 0, CHUNKS, N_QK1 + N_V1)
        w_out = part(w_mix, 0, CHUNKS, D_MODEL)
        prob = part(buf1, 0, 3, TOKENS)
        probT = part(buf1, 1536, 2, TOKENS)
        attn = part(buf1, 2560, DIL_HEADS * HEAD)

        consts_in = sem("consts_in")
        out_stored = sem("out_stored")
        dve_chain = sem("dve_chain")
        pool_chain = sem("pool_chain")
        x_in = [sem(f"x_in{t}") for t in range(TILES)]
        x_ready = [sem(f"x_ready{i}") for i in range(5)]

        params_in = sem("params_in")
        def signals(kind, by_name):
            return type(kind, (), by_name)()

        first_layer, first_norm = layers[0], 2 * layers[0] + (0 if mixers else 1)
        N = []
        shared = {n: sem(n) for n in "ss_done rstd_done xn_done xT_ps xT_act xT_dve".split()}
        for z in range(4):
            s = signals("NormSignals", shared)
            before_it = z - first_norm if mixers else (z - first_norm) // 2
            s.base = {n: before_it * (CHUNKS if n == "xT_ps" else TILES) for n in shared}
            N.append(s)
        units0 = TILES * DSA_HEADS
        mixer0_counts = dict(w_in=16, w_out_in=16, head_gain_in=96, in_ps=TILES, raw_done=TILES, sq_done=TILES, head_ss_done=TILES,
                             head_rstd_done=TILES, normed=TILES, sin_done=TILES, rot_done=TILES, qkT_ps=2 * TILES, qkT_done=2 * TILES,
                             in_over=1, out_over=1, tables_done=1, s_ps=units0, masked_done=units0, exp_done=units0, pT_ps=units0,
                             pT_dve=units0 // 2, pT_act=units0 // 2, pv_done=units0, o_done=TILES, oT_ps=TILES, oT_done=TILES,
                             out_ps=2 * TILES, out_half=2 * TILES)
        shared = {n: sem(n) for n in mixer0_counts}
        M = []
        for l in range(2):
            only = ("w_in_b w_conv_in v_done idx_ps idx_raw_done idx_sin_done idx_rot_done idxT_ps idxT_done "
                    "rel_ps rel_done rel_used idx_w_done conv_ps conv_in_done conv_done conv_over") if l == 0 else ""
            s = signals("MixerSignals", {**shared, **{n: sem(n) for n in only.split()}})
            s.base = {n: count * (l - first_layer) for n, count in mixer0_counts.items()}
            M.append(s)
        L = []
        for l in range(2):
            s = signals("ExpertSignals", {n: sem(f"{n}_{l}") for n in ("router_in xn_stored logits_done exp_in exp_done "
                      "picked_done rank_done hot_ready fetch_ps fetch_done count_done fetch_copied store_copied pool_turn store_done level_stored "
                      "x_transposed xT_done parts_done silu_done h_done h_transposed hT_done y_evac "
                      "all_ys_stored store_steps xn_scaled").split()})
            s.weights_in = [sem(f"weights_in{j}_{l}") for j in range(6)]
            s.xg_in = [sem(f"xg_in{u}_{l}") for u in range(2)]
            s.ys_stored = [sem(f"ys_stored{u}_{l}") for u in range(2)]
            s.combine_in = [sem(f"combine_in{t}_{l}") for t in range(TILES)]
            L.append(s)

        def expert_weights(l, e):
            for name in ("w_gate", "w_up", "w_down"):
                w = a[f"{name}_{l}"][e]
                if name == "w_down":
                    yield w.rearrange("(c p) n -> p c n", p=PARTS)
                else:
                    yield w.rearrange("(c p) n -> p c n", p=PARTS)

        def ring_part(j):
            n = D_EXPERT if j % 3 < 2 else D_MODEL
            return ring[:, j, :].rearrange("p (c n) -> p c n", n=n)

        def comb(t):
            return ring[:, :, :].rearrange("p j n -> p (j n)")[:, TOP_K * D_MODEL * t:TOP_K * D_MODEL * (t + 1)]

        block = ctx.enter_context(nc.Block())

        @block.sync
        def _(sp):
            for t in range(TILES):
                sp.dma_start(x_res[:, t, :], a["x"][PARTS * t:PARTS * t + PARTS, :]).then_inc(x_in[t], 16)
            sp.dma_start(const[:, :], a["consts"]).then_inc(consts_in, 16)
            for z, name in enumerate(("attn_norm_0", "ffn_norm_0", "attn_norm_1", "ffn_norm_1")):
                sp.dma_start(gain[:, z, :], a[name].rearrange("(c p) -> p c", p=PARTS), allow_slow_non_contiguous=True).then_inc(params_in, 16)
            sp.dma_start(conv_w[:, :, :], a["conv_w_0"].rearrange("(c p) j -> p c j", p=PARTS)).then_inc(params_in, 16)

            def head_gains(l):
                for j, name in enumerate((f"q_norm_{l}", f"k_norm_{l}")):
                    row = a[name].rearrange("(o d) -> o d", o=1)
                    sp.dma_start(head_gain[:, 2 * j, :], row.broadcast_to([PARTS, HEAD])).then_inc(M[l].head_gain_in, 16)
                    sp.dma_start(head_gain[:, 2 * j + 1, 0:HALF], row[:, HALF:].broadcast_to([PARTS, HALF])).then_inc(M[l].head_gain_in, 16)
                    sp.dma_start(head_gain[:, 2 * j + 1, HALF:], row[:, 0:HALF].broadcast_to([PARTS, HALF])).then_inc(M[l].head_gain_in, 16)

            def load_w_out(l):
                sp.dma_start(w_out, a[f"w_out_{l}"].rearrange("(c p) n -> p c n", p=PARTS)).then_inc(M[l].w_out_in, 16)

            def load_expert(l, e, u):
                for j, src in enumerate(expert_weights(l, e)):
                    yield j, (ring_part(3 * u + j), src)

            def moe(l):
                s = L[l]
                sp.dma_start(w_router[:, :, 0:N_GROUPS], a[f"w_rg_{l}"].rearrange("(c p) g -> p c g", p=PARTS)).then_inc(s.router_in, 16)
                for g in range(N_GROUPS):
                    sp.dma_start(w_router[:, :, N_GROUPS + g * PER_GROUP:N_GROUPS + (g + 1) * PER_GROUP],
                                 a[f"w_re_{l}"][g].rearrange("(c p) e -> p c e", p=PARTS)).then_inc(s.router_in, 16)
                sp.dma_start(b_router[:, 0:N_GROUPS], a[f"b_rg_{l}"].rearrange("(o g) -> o g", o=1).broadcast_to([PARTS, N_GROUPS])).then_inc(s.router_in, 16)
                sp.dma_start(b_router[:, N_GROUPS:], a[f"b_re_{l}"].rearrange("(o g) e -> o (g e)", o=1).broadcast_to([PARTS, N_EXPERTS])).then_inc(s.router_in, 16)
                for u in range(2):
                    if u and mixers:
                        sp.wait_ge(M[l].out_over, M[l].base["out_over"] + 1)
                    for j, (dst, src) in load_expert(l, u, u):
                        sp.dma_start(dst, src).then_inc(s.weights_in[3 * u + j], 16)
                if l == 0 and mixers:
                    sp.dma_start(w_in1, a["w_in_1"].rearrange("(c p) n -> p c n", p=PARTS)).then_inc(M[1].w_in, 16)
                for t in range(TILES):
                    sp.wait_ge(N[2 * l + 1].xn_done, N[2 * l + 1].base["xn_done"] + t + 1)
                    sp.dma_start(xn_dram[PARTS * t:PARTS * t + PARTS, :], xn[:, t, :]).then_inc(s.xn_stored, 16)

                def steps(first, b):
                    with sp.Fori(first, N_EXPERTS // 2) as i:
                        for u in range(2):
                            for j, (dst, src) in load_expert(l, 2 * i + u, u):
                                sp.wait_ge(s.parts_done, (b * N_EXPERTS + 2 * i + u - 2) * 3 + j + 1)
                                sp.dma_start(dst, src).then_inc(s.weights_in[3 * u + j], 16)
                steps(1, 0)
                sp.wait_ge(s.count_done, 1)
                most = sp.value_load(max_count[0:1, 0:1], min_val=0, max_val=TOKENS)
                with sp.Fori(1, LEVELS) as b:
                    with sp.If(most > b * CAP):
                        steps(0, b)
                sp.wait_ge(s.all_ys_stored, 1)
                for t in range(TILES):
                    sp.dma_start(comb(t), ys_dram[TOP_K * PARTS * t:TOP_K * PARTS * (t + 1), :].rearrange("(p k) d -> p (k d)", k=TOP_K)).then_inc(s.combine_in[t], 16)

            def mixer0():
                w = a["w_in_0"].rearrange("(c p) n -> p c n", p=PARTS)
                sp.dma_start(w_idx, w[:, :, N_CONV_COLS + N_QKV0:]).then_inc(M[0].w_in, 16)
                sp.dma_start(w_qkv0, w[:, :, N_CONV_COLS:N_CONV_COLS + N_QKV0]).then_inc(M[0].w_in_b, 16)
                head_gains(0)
                sp.dma_start(w_conv, w[:, :, 0:N_CONV_COLS]).then_inc(M[0].w_conv_in, 16)
                sp.wait_ge(M[0].in_over, M[0].base["in_over"] + 1)
                load_w_out(0)
                sp.wait_ge(M[0].conv_over, 1)

            def mixer1():
                if first_layer == 0:
                    sp.wait_ge(x_ready[2], TILES)
                else:
                    sp.dma_start(w_in1, a["w_in_1"].rearrange("(c p) n -> p c n", p=PARTS)).then_inc(M[1].w_in, 16)
                head_gains(1)
                sp.wait_ge(M[1].in_over, M[1].base["in_over"] + 1)
                load_w_out(1)

            for l in layers:
                if mixers:
                    (mixer0, mixer1)[l]()
                if moes:
                    moe(l)
            for t in range(TILES):
                sp.wait_ge(x_ready[4], t + 1)
                sp.dma_start(a["out"][PARTS * t:PARTS * t + PARTS, :], x_res[:, t, :]).then_inc(out_stored, 16)
            sp.wait_ge(out_stored, 16 * TILES)

        @block.gpsimd
        def _(pool):
            chain = [0]

            def link(ins):
                chain[0] += 1
                ins.then_inc(pool_chain, 1)
                pool.wait_ge(pool_chain, chain[0])

            G = nc.gpsimd
            pool.wait_ge(consts_in, 16)

            def root(value, width, done, n):
                link(G.tensor_scalar(value, value, 1.0 / width, NORM_EPS, ALU.mult, ALU.add))
                G.tensor_tensor(value, value, con("eps_pow")[:, 1:2].broadcast_to([PARTS, n]), ALU.pow).then_inc(done, 1)

            def norm(z):
                for t in range(TILES):
                    pool.wait_ge(N[z].ss_done, N[z].base["ss_done"] + t + 1)
                    root(sumsq[:, t:t + 1], D_MODEL, N[z].rstd_done, 1)

            def head_norm(l, t, heads):
                pool.wait_ge(M[l].head_ss_done, M[l].base["head_ss_done"] + t + 1)
                root(head_ss[:, t % 2, 0:heads], HEAD, M[l].head_rstd_done, heads)

            def sine_terms(out, raw, sin):
                heads = out.shape[1]
                G.tensor_tensor(out[:, :, 0:HALF], raw[:, :, HALF:], sin[:, 0:HALF].unsqueeze(1).broadcast_to([PARTS, heads, HALF]), ALU.mult)
                return G.tensor_tensor(out[:, :, HALF:], raw[:, :, 0:HALF], sin[:, HALF:].unsqueeze(1).broadcast_to([PARTS, heads, HALF]), ALU.mult)

            def heads_of(v):
                return v.rearrange("p (h d) -> p h d", d=HEAD)

            def mixer0():
                m = M[0]
                norm(0)
                base_sin = con("rope_sin").rearrange("p (t d) -> p t d", d=HEAD)
                for t in range(TILES):
                    pool.wait_ge(m.idx_raw_done, t + 1)
                    if t:
                        pool.wait_ge(m.idx_rot_done, t)
                    sine_terms(idx_sin, heads_of(idx_raw[:, t, 0:(IDX_HEADS + 1) * HEAD]), base_sin[:, t, :]).then_inc(m.idx_sin_done, 1)
                    G.tensor_scalar(idx_w[:, t, :], idx_raw[:, t, (IDX_HEADS + 1) * HEAD:], IDX_HEADS ** -0.5, None, ALU.mult).then_inc(m.idx_w_done, 1)
                pool.wait_ge(m.tables_done, m.base["tables_done"] + 1)
                for t in range(TILES):
                    raw = qk_raw0[:, t % 2, :]
                    pool.wait_ge(m.raw_done, m.base["raw_done"] + t + 1)
                    G.tensor_copy(v0[:, t, :], raw[:, (DSA_HEADS + 1) * HEAD:]).then_inc(m.v_done, 1)
                    head_norm(0, t, DSA_HEADS + 1)
                    pool.wait_ge(m.normed, m.base["normed"] + t + 1)
                    if t:
                        pool.wait_ge(m.rot_done, m.base["rot_done"] + t)
                    sine_terms(qk_sin0[:, 0:DSA_HEADS, :], heads_of(raw[:, 0:DSA_HEADS * HEAD]), rope[:, 1, t, :])
                    sine_terms(qk_sin0[:, DSA_HEADS:, :], heads_of(raw[:, DSA_HEADS * HEAD:(DSA_HEADS + 1) * HEAD]), rope[:, 3, t, :]).then_inc(m.sin_done, 1)
                pool.wait_ge(m.qkT_ps, m.base["qkT_ps"] + 2 * TILES)
                link(G.memset(conv_u[:, 0:TAPS - 1], 0.0))
                for c in range(CONV // PARTS):
                    pool.wait_ge(m.conv_in_done, 3 * c + 2)
                    u = conv_u[:, TAPS - 1:]
                    link(G.tensor_tensor(u, conv_in[:, 0, :], conv_in[:, 1, :], ALU.mult))
                    link(G.tensor_scalar(conv_y[:, 0, :], conv_u[:, 0:TOKENS], conv_w[:, c, 0:1], None, ALU.mult))
                    for j in range(1, TAPS):
                        link(G.tensor_scalar(conv_y[:, 1, :], conv_u[:, j:j + TOKENS], conv_w[:, c, j:j + 1], None, ALU.mult))
                        link(G.tensor_tensor(conv_y[:, 0, :], conv_y[:, 0, :], conv_y[:, 1, :], ALU.add))
                    pool.wait_ge(m.conv_in_done, 3 * c + 3)
                    G.tensor_tensor(mixed[:, c, :], conv_y[:, 0, :], conv_in[:, 2, :], ALU.mult).then_inc(m.conv_done, 1)

            def mixer1():
                m = M[1]
                norm(2)
                pool.wait_ge(m.tables_done, m.base["tables_done"] + 1)
                nq = DIL_HEADS * HEAD
                sin_terms = heads_of(qk_sq1)
                for t in range(TILES):
                    head_norm(1, t, DIL_HEADS + DIL_KV)
                    pool.wait_ge(m.normed, m.base["normed"] + t + 1)
                    sine_terms(sin_terms[:, 0:DIL_HEADS, :], heads_of(qk_raw1[:, 0:nq]), rope[:, 1, t, :])
                    sine_terms(sin_terms[:, DIL_HEADS:, :], heads_of(qk_raw1[:, nq:]), rope[:, 3, t, :]).then_inc(m.sin_done, 1)

            def moe(l):
                s = L[l]
                norm(2 * l + 1)
                pool.wait_ge(s.xn_stored, 16 * TILES)

                def gather(b, i, u):
                    nc.gpsimd.tensor_copy(fetch_now[:, u:u + 1], fetch[:, bass.ds(2 * i + u, 1)]).then_inc(s.fetch_copied, 1)
                    pool.wait_ge(s.fetch_copied, b * N_EXPERTS + 2 * i + u + 1)
                    pool.sem_inc(s.pool_turn, 1)
                    pool.indirect_dma_start(out=xg[u], out_offset=None, in_=xn_dram.rearrange("t (h d) -> (t h) d", h=2),
                                            in_offset=bass.IndirectOffsetOnAxis(ap=fetch_now[:, u:u + 1], axis=0)).then_inc(s.xg_in[u], 16)

                def scatter(b, i, u):
                    nc.gpsimd.tensor_copy(store_now[:, u:u + 1], store[:, bass.ds(2 * i + u, 1)]).then_inc(s.store_copied, 1)
                    pool.wait_ge(s.store_copied, b * N_EXPERTS + 2 * i + u + 1)
                    pool.wait_ge(s.y_evac, b * N_EXPERTS + 2 * i + u + 1)
                    if type(b) is not int or type(i) is not int or b + i + u > 0:
                        pool.wait_ge(s.ys_stored[1 - u], (b * (N_EXPERTS // 2) + i + u) * 16)
                    pool.sem_inc(s.pool_turn, 1)
                    pool.indirect_dma_start(out=ys_dram.rearrange("r (h d) -> (r h) d", h=2),
                                            out_offset=bass.IndirectOffsetOnAxis(ap=store_now[:, u:u + 1], axis=0),
                                            in_=ysb[u], in_offset=None).then_inc(s.ys_stored[u], 16)

                def steps(b):
                    pool.wait_ge(s.fetch_done, b + 1)
                    pool.wait_ge(s.store_done, b + 1)
                    pool.sem_inc(s.pool_turn, 1)
                    for u in range(2):
                        gather(b, 0, u)
                    first = 0
                    if type(b) is int:
                        for u in range(2):
                            scatter(b, 0, u)
                            gather(b, 1, u)
                        first = 1
                    with pool.Fori(first, N_EXPERTS // 2 - 1) as i:
                        for u in range(2):
                            scatter(b, i, u)
                            gather(b, i + 1, u)
                    for u in range(2):
                        scatter(b, N_EXPERTS // 2 - 1, u)
                    for u in range(2):
                        pool.wait_ge(s.ys_stored[u], (b + 1) * (N_EXPERTS // 2) * 16)
                    pool.sem_inc(s.pool_turn, 1)
                steps(0)
                pool.wait_ge(s.count_done, 1)
                most = pool.value_load(max_count[0:1, 0:1], min_val=0, max_val=TOKENS)
                with pool.Fori(1, LEVELS) as b:
                    with pool.If(most > b * CAP):
                        steps(b)
                pool.sem_inc(s.all_ys_stored, 1)
            for l in layers:
                if mixers:
                    (mixer0, mixer1)[l]()
                if moes:
                    moe(l)

        @block.scalar
        def _(act):
            A = nc.scalar

            def norm(z):
                tok = token_major[z % 2][:, :].rearrange("p (t d) -> p t d", t=TILES)
                tr = feature_major[z % 2][:, :].rearrange("p (c n) -> p c n", c=CHUNKS)
                for t in range(TILES):
                    if z == first_norm:
                        act.wait_ge(x_in[t], 16)
                    else:
                        act.wait_ge(x_ready[z], t + 1)
                    A.activation(tok[:, t, :], x_res[:, t, :], ACT.Square, accum_out=sumsq[:, t:t + 1]).then_inc(N[z].ss_done, 1)
                act.wait_ge(params_in, 80)
                for c in range(1, CHUNKS, 2):
                    act.wait_ge(N[z].xT_ps, N[z].base["xT_ps"] + c + 1)
                    A.activation(tr[:, c, :], ps[:, c % 4, :], ACT.Copy, scale=gain[:, z, c:c + 1]).then_inc(N[z].xT_act, 1)

            def attention(l, heads):
                m = M[l]
                units = TILES * heads
                for n in range(units + 4):
                    if n < units:
                        t, hd = divmod(n, heads)
                        keys = PARTS * (t + 1)
                        act.wait_ge(m.masked_done, m.base["masked_done"] + n + 1)
                        if hd == 0 and t >= 2:
                            act.wait_ge(m.o_done, m.base["o_done"] + t - 1)
                        A.activation(prob[:, n % 3, 0:keys], prob[:, n % 3, 0:keys], ACT.Exp, bias=neg_max[:, n % 3:n % 3 + 1], scale=-1.0,
                                     accum_out=denom[:, t % 2, hd:hd + 1]).then_inc(m.exp_done, 1)
                    e = n - 2
                    if 0 <= e < units and e % 2 == 1:
                        keys = PARTS * (e // heads + 1)
                        act.wait_ge(m.pT_ps, m.base["pT_ps"] + e + 1)
                        if e >= 2:
                            act.wait_ge(m.pv_done, m.base["pv_done"] + e - 1)
                        A.activation(probT[:, 1, 0:keys], ps[:, 4, 0:keys], ACT.Copy).then_inc(m.pT_act, 1)
                    if n >= 4 and (n - 3) % heads == 0:
                        t = (n - 4) // heads
                        blocks = heads * HEAD // PARTS
                        for g in range(blocks // 4):
                            act.wait_ge(m.oT_ps, m.base["oT_ps"] + t * (blocks // 4) + g + 1)
                            c0 = CHUNKS - blocks + 4 * g
                            A.activation(mixed[:, c0:c0 + 4, PARTS * t:PARTS * t + PARTS], ps[:, 7, :].rearrange("p (c n) -> p c n", c=4), ACT.Copy).then_inc(m.oT_done, 1)

            def mixer0():
                m = M[0]
                norm(0)
                for t in range(TILES):
                    act.wait_ge(m.idx_ps, t + 1)
                    A.activation(idx_raw[:, t, :], ps[:, t % 2, 0:N_IDX0], ACT.Copy).then_inc(m.idx_raw_done, 1)
                for t in range(TILES):
                    if t >= 2:
                        act.wait_ge(m.rot_done, m.base["rot_done"] + t - 1)
                        act.wait_ge(m.sin_done, m.base["sin_done"] + t - 1)
                        act.wait_ge(m.v_done, t - 1)
                    if t >= 1:
                        act.wait_ge(m.head_ss_done, m.base["head_ss_done"] + t)
                    act.wait_ge(m.in_ps, m.base["in_ps"] + t + 1)
                    b0 = 2 + 2 * (t % 2)
                    src = ps[:, b0:b0 + 2, 0:N_QKV0 // 2]
                    A.activation(qk_sq0.rearrange("p (a n) -> p a n", a=2), src, ACT.Square).then_inc(m.sq_done, 1)
                    A.activation(qk_raw0[:, t % 2, :].rearrange("p (a n) -> p a n", a=2), src, ACT.Copy).then_inc(m.raw_done, 1)
                for t in range(TILES):
                    act.wait_ge(m.idxT_ps, t + 1)
                    A.activation(idxT[:, :, PARTS * t:PARTS * t + PARTS], ps[:, 6 + t % 2, 0:3 * PARTS].rearrange("p (c n) -> p c n", c=3), ACT.Copy).then_inc(m.idxT_done, 1)
                for t in range(1, TILES):
                    keys = PARTS * (t + 1)
                    for hd in range(IDX_HEADS):
                        n = (t - 1) * IDX_HEADS + hd
                        act.wait_ge(m.rel_ps, n + 1)
                        if n >= 2:
                            act.wait_ge(m.rel_used, n - 1)
                        A.activation(relu[:, n % 2, 0:keys], ps[:, hd, 0:keys], ACT.Relu, scale=SCALE).then_inc(m.rel_done, 1)
                for t in range(TILES):
                    for g in range(2):
                        act.wait_ge(m.qkT_ps, m.base["qkT_ps"] + 2 * t + g + 1)
                        dst = qT0[:, :, PARTS * t:PARTS * t + PARTS] if g == 0 else kT0[:, :, PARTS * t:PARTS * t + PARTS]
                        w = 4 if g == 0 else 1
                        A.activation(dst, ps[:, 6 + g, 0:w * PARTS].rearrange("p (c n) -> p c n", c=w), ACT.Copy).then_inc(m.qkT_done, 1)
                for c in range(CONV // PARTS):
                    for g in range(3):
                        act.wait_ge(m.conv_ps, 3 * c + g + 1)
                        if c >= 1:
                            act.wait_ge(m.conv_done, c)
                        A.activation(conv_in[:, g, :], ps[:, 3 * (c % 2) + g, :], ACT.Copy).then_inc(m.conv_in_done, 1)
                attention(0, DSA_HEADS)

            def mixer1():
                m = M[1]
                norm(2)
                for t in range(TILES):
                    act.wait_ge(m.in_ps, m.base["in_ps"] + t + 1)
                    b0 = 3 * (t % 2)
                    if t:
                        act.wait_ge(m.rot_done, m.base["rot_done"] + t)
                    for g, (lo, hi) in enumerate(((0, 512), (512, 1024), (1024, 1280))):
                        last = A.activation(qk_sq1[:, lo:hi], ps[:, b0 + g, 0:hi - lo], ACT.Square)
                    last.then_inc(m.sq_done, 1)
                    for g, (lo, hi) in enumerate(((0, 512), (512, 1024), (1024, 1280))):
                        A.activation(qk_raw1[:, lo:hi], ps[:, b0 + g, 0:hi - lo], ACT.Copy)
                    A.activation(v1[:, t, :], ps[:, b0 + 2, 256:512], ACT.Copy).then_inc(m.raw_done, 1)
                    if t:
                        transposed_out(t - 1)
                transposed_out(TILES - 1)
                attention(1, DIL_HEADS)

            def transposed_out(t):
                m = M[1]
                for g in range(3):
                    act.wait_ge(m.qkT_ps, m.base["qkT_ps"] + 3 * t + g + 1)
                    dst = qT1[:, 4 * g:4 * g + 4, :] if g < 2 else kT1
                    A.activation(dst[:, :, PARTS * t:PARTS * t + PARTS], ps[:, 6 + (3 * t + g) % 2, :].rearrange("p (c n) -> p c n", c=4), ACT.Copy).then_inc(m.qkT_done, 1)

            def moe(l):
                s = L[l]
                norm(2 * l + 1)
                act.wait_ge(s.exp_in, 1)
                nc.scalar.activation(exp4[:, :, :], at4[:, :, :], ACT.Exp).then_inc(s.exp_done, 1)
                act.wait_ge(s.exp_in, 2)
                nc.scalar.activation(e21[:, :], gap[:, :], ACT.Exp).then_inc(s.exp_done, 1)

                def expert_pair(b, i):
                        for u in range(2):
                            n = b * N_EXPERTS + 2 * i + u
                            act.wait_ge(s.parts_done, 3 * n + 1)
                            nc.scalar.activation(silu, ps[:, 1, 0:256], ACT.Silu).then_inc(s.silu_done, 1)
                            act.wait_ge(s.h_transposed, n + 1)
                            nc.scalar.activation(hT, ps[:, 3, 0:256], ACT.Copy).then_inc(s.hT_done, 1)
                            act.wait_ge(s.parts_done, 3 * n + 3)
                            if n >= 2 if type(n) is int else True:
                                act.wait_ge(s.ys_stored[u], (b * (N_EXPERTS // 2) + i) * 16)
                            nc.scalar.activation(ysb[u], ps[:, 4, :], ACT.Copy).then_inc(s.y_evac, 1)

                def steps(b):
                    first = 0
                    if type(b) is int:
                        expert_pair(b, 0)
                        first = 1
                    with act.Fori(first, N_EXPERTS // 2) as i:
                        expert_pair(b, i)
                steps(0)
                act.wait_ge(s.count_done, 1)
                most = act.value_load(max_count[0:1, 0:1], min_val=0, max_val=TOKENS)
                with act.Fori(1, LEVELS) as b:
                    with act.If(most > b * CAP):
                        steps(b)
            for l in layers:
                if mixers:
                    (mixer0, mixer1)[l]()
                if moes:
                    moe(l)

        @block.vector
        def _(dve):
            chain = [0]

            def link(ins):
                chain[0] += 1
                ins.then_inc(dve_chain, 1)
                dve.wait_ge(dve_chain, chain[0])
            V = nc.vector

            def over(v, n):
                return v.unsqueeze(2).broadcast_to([PARTS, v.shape[1], n])

            def norm(z):
                tok = token_major[z % 2][:, :].rearrange("p (t d) -> p t d", t=TILES)
                tr = feature_major[z % 2][:, :].rearrange("p (c n) -> p c n", c=CHUNKS)
                for t in range(TILES):
                    dve.wait_ge(N[z].rstd_done, N[z].base["rstd_done"] + t + 1)
                    V.tensor_scalar(tok[:, t, :], x_res[:, t, :], sumsq[:, t:t + 1], None, ALU.mult).then_inc(N[z].xn_done, 1)
                dve.wait_ge(params_in, 80)
                for c in range(0, CHUNKS, 2):
                    dve.wait_ge(N[z].xT_ps, N[z].base["xT_ps"] + c + 1)
                    V.tensor_scalar(tr[:, c, :], ps[:, c % 4, :], gain[:, z, c:c + 1], None, ALU.mult).then_inc(N[z].xT_dve, 1)

            def heads_of(v):
                return v.rearrange("p (h d) -> p h d", d=HEAD)

            def on_heads(v, heads):
                return v.unsqueeze(1).broadcast_to([PARTS, heads, HEAD])

            def tables(l):
                dve.wait_ge(M[l].head_gain_in, M[l].base["head_gain_in"] + 96)
                for j in range(4):
                    base = con("rope_sin" if j % 2 else "rope_cos").rearrange("p (t d) -> p t d", d=HEAD)
                    last = V.tensor_tensor(rope[:, j, :, :], base, on_heads(head_gain[:, j, :], TILES), ALU.mult)
                link(last)
                dve.sem_inc(M[l].tables_done, 1)

            def rotate(m, t, raw, sin, rot, qh, kh):
                nq, nk = qh * HEAD, kh * HEAD
                dve.wait_ge(m.sq_done, m.base["sq_done"] + t + 1)
                sq = qk_sq0[:, 0:nq + nk] if qh == DSA_HEADS else qk_sq1
                V.tensor_reduce(head_ss[:, t % 2, 0:qh + kh], heads_of(sq), AX, ALU.add).then_inc(m.head_ss_done, 1)
                dve.wait_ge(m.head_rstd_done, m.base["head_rstd_done"] + t + 1)
                dve.wait_ge(m.raw_done, m.base["raw_done"] + t + 1)
                r3 = heads_of(raw[:, 0:nq + nk])
                V.tensor_tensor(r3, r3, head_ss[:, t % 2, 0:qh + kh].unsqueeze(2).broadcast_to([PARTS, qh + kh, HEAD]), ALU.mult).then_inc(m.normed, 1)
                dve.wait_ge(m.normed, m.base["normed"] + t + 1)
                q_rot = heads_of(rot[:, 0:nq])
                k_rot = rot[:, nq:nq + 2 * nk].rearrange("p (h two d) -> p h two d", two=2, d=HEAD)
                V.tensor_tensor(q_rot, r3[:, 0:qh, :], on_heads(rope[:, 0, t, :], qh), ALU.mult)
                link(V.tensor_tensor(k_rot[:, :, 0, :], r3[:, qh:, :], on_heads(rope[:, 2, t, :], kh), ALU.mult))
                dve.wait_ge(m.sin_done, m.base["sin_done"] + t + 1)
                V.tensor_tensor(q_rot, q_rot, sin[:, 0:qh, :], ALU.add)
                link(V.tensor_tensor(k_rot[:, :, 1, :], k_rot[:, :, 0, :], sin[:, qh:, :], ALU.add))
                link(V.tensor_tensor(k_rot[:, :, 0, :], k_rot[:, :, 0, :], sin[:, qh:, :], ALU.add))
                dve.sem_inc(m.rot_done, 1)

            def attention(l, heads, mask_of):
                m = M[l]
                units = TILES * heads
                for n in range(units + 4):
                    if n < units:
                        t, hd = divmod(n, heads)
                        keys = PARTS * (t + 1)
                        dve.wait_ge(m.s_ps, m.base["s_ps"] + n + 1)
                        if n >= 3:
                            dve.wait_ge(m.pT_ps, m.base["pT_ps"] + n - 2)
                        V.tensor_tensor_reduce(out=prob[:, n % 3, 0:keys], in0=ps[:, n % 3, 0:keys], in1=mask_of(t), scale=-SCALE, scalar=-TAKEN,
                                               op0=ALU.add, op1=ALU.min, accum_out=neg_max[:, n % 3:n % 3 + 1]).then_inc(m.masked_done, 1)
                    e = n - 2
                    if 0 <= e < units and e % 2 == 0:
                        keys = PARTS * (e // heads + 1)
                        dve.wait_ge(m.pT_ps, m.base["pT_ps"] + e + 1)
                        if e >= 2:
                            dve.wait_ge(m.pv_done, m.base["pv_done"] + e - 1)
                        V.tensor_copy(probT[:, 0, 0:keys], ps[:, 3, 0:keys]).then_inc(m.pT_dve, 1)
                    if n >= 3 and (n - 2) % heads == 0:
                        t = (n - 3) // heads
                        dve.wait_ge(m.exp_done, m.base["exp_done"] + (t + 1) * heads)
                        link(V.reciprocal(denom[:, t % 2, 0:heads], denom[:, t % 2, 0:heads]))
                        dve.wait_ge(m.pv_done, m.base["pv_done"] + (t + 1) * heads)
                        if t:
                            dve.wait_ge(m.oT_ps, m.base["oT_ps"] + t * (heads // 8))
                        for g in range(heads // 8):
                            bank = 5 + (t % 2 if heads == DSA_HEADS else g)
                            last = V.tensor_tensor(heads_of(attn[:, 512 * g:512 * g + 512]), heads_of(ps[:, bank, :]),
                                                   denom[:, t % 2, 8 * g:8 * g + 8].unsqueeze(2).broadcast_to([PARTS, 8, HEAD]), ALU.mult)
                        last.then_inc(m.o_done, 1)

            def project_out(l):
                m = M[l]
                for t in range(TILES):
                    for hf in range(2):
                        n = 2 * t + hf
                        dve.wait_ge(m.out_ps, m.base["out_ps"] + n + 1)
                        cols = slice(512 * hf, 512 * hf + 512)
                        ins = V.tensor_tensor(x_res[:, t, cols], x_res[:, t, cols], ps[:, n % 4, :], ALU.add)
                        ins.then_inc(m.out_half, 1)
                    dve.wait_ge(m.out_half, m.base["out_half"] + 2 * t + 2)
                    dve.sem_inc(x_ready[2 * l + 1] if moes else x_ready[4], 1)

            def mixer0():
                m = M[0]
                dve.wait_ge(consts_in, 16)
                norm(0)
                tables(0)
                base_cos = con("rope_cos").rearrange("p (t d) -> p t d", d=HEAD)
                n_idx = (IDX_HEADS + 1) * HEAD
                for t in range(TILES):
                    dve.wait_ge(m.idx_raw_done, t + 1)
                    rot = idx_rot[:, t, :]
                    link(V.tensor_tensor(heads_of(rot[:, 0:n_idx]), heads_of(idx_raw[:, t, 0:n_idx]), on_heads(base_cos[:, t, :], IDX_HEADS + 1), ALU.mult))
                    dve.wait_ge(m.idx_sin_done, t + 1)
                    link(V.tensor_tensor(rot[:, n_idx:], rot[:, n_idx - HEAD:n_idx], idx_sin[:, IDX_HEADS, :], ALU.add))
                    link(V.tensor_tensor(heads_of(rot[:, 0:n_idx]), heads_of(rot[:, 0:n_idx]), idx_sin, ALU.add))
                    dve.sem_inc(m.idx_rot_done, 1)
                for t in range(TILES):
                    rotate(m, t, qk_raw0[:, t % 2, :], qk_sin0, qk_rot0[:, t, :], DSA_HEADS, 1)
                dve.wait_ge(m.idx_w_done, TILES)
                for t in range(1, TILES):
                    for hd in range(IDX_HEADS):
                        n = (t - 1) * IDX_HEADS + hd
                        dve.wait_ge(m.rel_done, n + 1)
                        rel = relu[:, n % 2, 0:PARTS * (t + 1)]
                        if hd == 0:
                            V.tensor_scalar(score[t], rel, idx_w[:, t, hd:hd + 1], None, ALU.mult).then_inc(m.rel_used, 1)
                        else:
                            V.scalar_tensor_tensor(score[t], rel, idx_w[:, t, hd:hd + 1], score[t], ALU.mult, ALU.add).then_inc(m.rel_used, 1)
                        dve.wait_ge(m.rel_used, n + 1)
                    own = score[t][:, PARTS * t:]
                    link(V.tensor_tensor(own, own, con("causal"), ALU.add))
                for t in range(1, TILES):
                    for _ in range(DSA_KEEP // 8):
                        link(V.max(best8[:, :], score[t]))
                        link(V.match_replace(score[t], best8[:, :], score[t], TAKEN))
                    link(V.tensor_scalar(score[t], score[t], TAKEN, -BIG, ALU.not_equal, ALU.mult))
                attention(0, DSA_HEADS, lambda t: score[t] if t else con("causal"))
                project_out(0)

            def mixer1():
                m = M[1]
                norm(2)
                tables(1)
                for t in range(TILES):
                    if t:
                        dve.wait_ge(m.qkT_ps, m.base["qkT_ps"] + 3 * t)
                    rotate(m, t, qk_raw1, heads_of(qk_sq1), qk_rot1, DIL_HEADS, DIL_KV)
                attention(1, DIL_HEADS, lambda t: con("strip")[:, TOKENS - PARTS * (t + 1):])
                project_out(1)

            def moe(l):
                s = L[l]
                norm(2 * l + 1)
                dve.wait_ge(s.router_in, 112)
                dve.wait_ge(s.logits_done, 1)
                link(V.tensor_tensor(logit[:, :, :], ps[:, 4, 0:TILES * N_ROUTER].rearrange("p (t n) -> p t n", t=TILES),
                                     b_router[:, :].unsqueeze(1).broadcast_to([PARTS, TILES, N_ROUTER]), ALU.add))
                lg, le = logit[:, :, 0:N_GROUPS], logit[:, :, N_GROUPS:]

                def first_of_max(values, best, index, out, work, n, iota):
                    link(V.tensor_reduce(best, values, AX, ALU.max))
                    link(V.tensor_tensor(work, values, over(best, n), ALU.is_equal))
                    link(V.scalar_tensor_tensor(work, work, -64.0, iota.unsqueeze(1).broadcast_to([PARTS, TILES, n]), ALU.mult, ALU.add))
                    link(V.tensor_reduce(index, work, AX, ALU.min))
                    link(V.tensor_tensor(out, work, over(index, n), ALU.is_equal))
                first_of_max(lg, gmax, gidx, hot4, pen4, N_GROUPS, con("iota_group"))
                V.tensor_tensor(at4, lg, over(gmax, N_GROUPS), ALU.subtract).then_inc(s.exp_in, 1)
                link(V.tensor_scalar(pen4, hot4, -1.0, BIG, ALU.add, ALU.mult))
                link(V.tensor_tensor(lm.rearrange("p t (g e) -> p t g e", g=N_GROUPS), le.rearrange("p t (g e) -> p t g e", g=N_GROUPS),
                                     pen4.unsqueeze(3).broadcast_to([PARTS, TILES, N_GROUPS, PER_GROUP]), ALU.add))
                first_of_max(lm, top[0], eid[:, 0, :], hot[0], tmp, N_EXPERTS, con("iota_expert"))
                link(V.scalar_tensor_tensor(lm, hot[0], -BIG, lm, ALU.mult, ALU.add))
                first_of_max(lm, top[1], eid[:, 1, :], hot[1], tmp, N_EXPERTS, con("iota_expert"))
                V.tensor_tensor(picked, hot[0], hot[1], ALU.add).then_inc(s.picked_done, 1)
                V.tensor_tensor(gap, top[1], top[0], ALU.subtract).then_inc(s.exp_in, 1)
                pair_row = con("pair_row").rearrange("p (t k) -> p t k", k=TOP_K)
                for k in range(TOP_K):
                    V.tensor_tensor(row_hot[:, :, k, 0:N_EXPERTS], hot[k], over(con("token"), N_EXPERTS), ALU.mult)
                    V.tensor_tensor(row_hot[:, :, k, N_EXPERTS:2 * N_EXPERTS], hot[k], over(pair_row[:, :, k], N_EXPERTS), ALU.mult)
                    V.tensor_copy(row_hot[:, :, k, 2 * N_EXPERTS:], hot[k])
                dve.wait_ge(s.rank_done, 1)
                ranks = ps[:, 5, 0:TILES * N_EXPERTS].rearrange("p (t e) -> p t e", t=TILES)
                for k in range(TOP_K):
                    link(V.tensor_tensor(tmp, hot[k], ranks, ALU.mult))
                    link(V.tensor_reduce(rank[:, k, :], tmp, AX, ALU.add))

                def slot_hots():
                    for k in range(TOP_K):
                        last = V.tensor_tensor(slot_hot[:, :, k, :], con("iota_slot").unsqueeze(1).broadcast_to([PARTS, TILES, PARTS]),
                                               over(rank[:, k, :], PARTS), ALU.is_equal)
                    last.then_inc(s.hot_ready, 1)
                slot_hots()
                link(V.tensor_reduce(cmax, ps[:, 6, 0:N_EXPERTS], AX, ALU.max))
                V.tensor_copy(max_count[:, :], cmax).then_inc(s.count_done, 1)
                dve.wait_ge(s.exp_done, 2)
                link(V.tensor_reduce(p_group, exp4, AX, ALU.add))
                link(V.reciprocal(p_group, p_group))
                link(V.tensor_scalar(inv, e21, 1.0, None, ALU.add))
                link(V.reciprocal(inv, inv))
                link(V.tensor_tensor(gates[:, 0, :], p_group, inv, ALU.mult))
                link(V.tensor_tensor(gates[:, 1, :], gates[:, 0, :], e21, ALU.mult))

                def steps(b):
                    dve.wait_ge(s.fetch_ps, b + 1)
                    V.tensor_scalar(fetch[:, :], ps[:, 7, 0:N_EXPERTS], 2.0, con("half"), ALU.mult, ALU.add).then_inc(s.fetch_done, 1)
                    V.tensor_tensor(storef, ps[:, 7, 2 * N_EXPERTS:3 * N_EXPERTS], con("half_less_spare"), ALU.mult).then_inc(s.store_steps, 1)
                    dve.wait_ge(s.store_steps, 3 * b + 1)
                    V.tensor_tensor(storef, storef, con("spare"), ALU.add).then_inc(s.store_steps, 1)
                    dve.wait_ge(s.store_steps, 3 * b + 2)
                    V.tensor_tensor(storef, storef, ps[:, 7, N_EXPERTS:2 * N_EXPERTS], ALU.add).then_inc(s.store_steps, 1)
                    dve.wait_ge(s.store_steps, 3 * b + 3)
                    V.tensor_copy(store[:, :], storef).then_inc(s.store_done, 1)
                    with dve.Fori(0, N_EXPERTS // 2) as i:
                        for u in range(2):
                            n = b * N_EXPERTS + 2 * i + u
                            dve.wait_ge(s.x_transposed, n + 1)
                            V.tensor_tensor(xT[u].rearrange("p (c h s) -> p c h s", h=2, s=CAP),
                                            ps[:, 0, :].rearrange("p (c h s) -> p c h s", h=2, s=CAP),
                                            gain[:, 2 * l + 1, :].rearrange("p (h c) -> p c h", h=2).unsqueeze(3).broadcast_to([PARTS, 4, 2, CAP]),
                                            ALU.mult).then_inc(s.xT_done, 1)
                            dve.wait_ge(s.silu_done, n + 1)
                            dve.wait_ge(s.parts_done, 3 * n + 2)
                            V.tensor_tensor(h, silu, ps[:, 2, 0:256], ALU.mult).then_inc(s.h_done, 1)
                steps(0)
                most = dve.value_load(max_count[0:1, 0:1], min_val=0, max_val=TOKENS)
                with dve.Fori(1, LEVELS) as b:
                    with dve.If(most > b * CAP):
                        V.tensor_scalar(rank, rank, -float(CAP), None, ALU.add).then_inc(s.xn_scaled, 1)
                        dve.wait_ge(s.xn_scaled, b)
                        dve.wait_ge(s.fetch_copied, b * N_EXPERTS)
                        dve.wait_ge(s.store_copied, b * N_EXPERTS)
                        slot_hots()
                        steps(b)
                for t in range(TILES):
                    dve.wait_ge(s.combine_in[t], 16)
                    link(V.scalar_tensor_tensor(x_res[:, t, :], comb(t)[:, 0:D_MODEL], gates[:, 0, t:t + 1], x_res[:, t, :], ALU.mult, ALU.add))
                    V.scalar_tensor_tensor(x_res[:, t, :], comb(t)[:, D_MODEL:], gates[:, 1, t:t + 1], x_res[:, t, :], ALU.mult, ALU.add)\
                        .then_inc(x_ready[2 * l + 2 if not (l == layers[-1]) else 4], 1)
            for l in layers:
                if mixers:
                    (mixer0, mixer1)[l]()
                if moes:
                    moe(l)

        @block.tensor
        def _(pe):
            pe.wait_ge(consts_in, 16)

            T = nc.tensor

            def norm(z):
                tok = token_major[z % 2][:, :].rearrange("p (t d) -> p t d", t=TILES)
                pe.wait_ge(N[z].xn_done, N[z].base["xn_done"] + TILES)
                for c in range(CHUNKS):
                    if c >= 4:
                        pe.wait_ge(N[z].xT_act if c % 2 else N[z].xT_dve, N[z].base["xT_act"] + c // 2 - 1)
                    for t in range(TILES):
                        last = T.transpose(ps[:, c % 4, PARTS * t:PARTS * t + PARTS], tok[:, t, PARTS * c:PARTS * c + PARTS], ident)
                    last.then_inc(N[z].xT_ps, 1)
                pe.wait_ge(N[z].xT_act, N[z].base["xT_act"] + CHUNKS // 2)
                pe.wait_ge(N[z].xT_dve, N[z].base["xT_dve"] + CHUNKS // 2)

            def project(out, src, cols, w, lo, hi):
                for c in range(CHUNKS):
                    last = T.matmul(out, src[:, c, cols], w[:, c, lo:hi], start=c == 0, stop=c == CHUNKS - 1)
                return last

            def attention(l, heads, qT, kT, v, kv_of):
                m = M[l]
                units = TILES * heads
                for n in range(units + 5):
                    if n < units:
                        t, hd = divmod(n, heads)
                        lo = HEAD * (hd % 2)
                        if n >= 3:
                            pe.wait_ge(m.masked_done, m.base["masked_done"] + n - 2)
                        T.matmul(ps[:, n % 3, 0:PARTS * (t + 1)], qT[lo:lo + HEAD, hd // 2, PARTS * t:PARTS * t + PARTS],
                                 kT[lo:lo + HEAD, kv_of(hd), 0:PARTS * (t + 1)], start=True, stop=True).then_inc(m.s_ps, 1)
                    e = n - 2
                    if 0 <= e < units:
                        t = e // heads
                        pe.wait_ge(m.exp_done, m.base["exp_done"] + e + 1)
                        if e >= 2:
                            pe.wait_ge(m.pT_act if e % 2 else m.pT_dve, m.base["pT_act"] + e // 2)
                        for kb in range(t + 1):
                            last = T.transpose(ps[:, 3 + e % 2, PARTS * kb:PARTS * kb + PARTS], prob[:, e % 3, PARTS * kb:PARTS * kb + PARTS], ident)
                        last.then_inc(m.pT_ps, 1)
                    e = n - 3
                    if 0 <= e < units:
                        t, hd = divmod(e, heads)
                        pe.wait_ge(m.pT_act if e % 2 else m.pT_dve, m.base["pT_act"] + e // 2 + 1)
                        if hd == 0 and t:
                            pe.wait_ge(m.o_done, m.base["o_done"] + t)
                        bank = 5 + (t % 2 if heads == DSA_HEADS else hd // 8)
                        for kb in range(t + 1):
                            kv = kv_of(hd)
                            last = T.matmul(ps[:, bank, HEAD * (hd % 8):HEAD * (hd % 8) + HEAD], probT[:, e % 2, PARTS * kb:PARTS * kb + PARTS],
                                            v[:, kb, HEAD * kv:HEAD * kv + HEAD], start=kb == 0, stop=kb == t)
                        last.then_inc(m.pv_done, 1)
                    if n >= 4 and (n - 3) % heads == 0:
                        t = (n - 4) // heads
                        pe.wait_ge(m.o_done, m.base["o_done"] + t + 1)
                        groups = heads // 8
                        for g in range(groups):
                            if t * groups + g:
                                pe.wait_ge(m.oT_done, m.base["oT_done"] + t * groups + g)
                            for j in range(4):
                                last = T.transpose(ps[:, 7, PARTS * j:PARTS * j + PARTS], attn[:, 512 * g + PARTS * j:512 * g + PARTS * j + PARTS], ident)
                            last.then_inc(m.oT_ps, 1)

            def project_out(l):
                m = M[l]
                pe.wait_ge(m.w_out_in, m.base["w_out_in"] + 16)
                pe.wait_ge(m.oT_done, m.base["oT_done"] + TILES * (1 if l == 0 else 2))
                if l == 0:
                    pe.wait_ge(m.conv_done, CONV // PARTS)
                for t in range(TILES):
                    for hf in range(2):
                        n = 2 * t + hf
                        if n >= 4:
                            pe.wait_ge(m.out_half, m.base["out_half"] + n - 3)
                        project(ps[:, n % 4, :], mixed, slice(PARTS * t, PARTS * t + PARTS), w_out, 512 * hf, 512 * hf + 512).then_inc(m.out_ps, 1)
                pe.wait_ge(m.out_half, m.base["out_half"] + 2 * TILES)
                pe.sem_inc(m.out_over, 1)

            def mixer0():
                m = M[0]
                norm(0)
                hT0 = feature_major[0][:, :].rearrange("p (c n) -> p c n", c=CHUNKS)
                pe.wait_ge(m.w_in, m.base["w_in"] + 16)
                for t in range(TILES):
                    if t >= 2:
                        pe.wait_ge(m.idx_raw_done, t - 1)
                    project(ps[:, t % 2, 0:N_IDX0], hT0, slice(PARTS * t, PARTS * t + PARTS), w_idx, 0, N_IDX0).then_inc(m.idx_ps, 1)
                pe.wait_ge(m.w_in_b, 16)
                for t in range(TILES):
                    if t >= 2:
                        pe.wait_ge(m.raw_done, m.base["raw_done"] + t - 1)
                    for hf in range(2):
                        last = project(ps[:, 2 + 2 * (t % 2) + hf, 0:N_QKV0 // 2], hT0, slice(PARTS * t, PARTS * t + PARTS), w_qkv0,
                                       hf * N_QKV0 // 2, (hf + 1) * N_QKV0 // 2)
                    last.then_inc(m.in_ps, 1)
                pe.wait_ge(m.in_ps, m.base["in_ps"] + TILES)
                pe.sem_inc(m.in_over, 1)
                for t in range(TILES):
                    pe.wait_ge(m.idx_rot_done, t + 1)
                    if t >= 2:
                        pe.wait_ge(m.idxT_done, t - 1)
                    for j in range(3):
                        last = T.transpose(ps[:, 6 + t % 2, PARTS * j:PARTS * j + PARTS], idx_rot[:, t, PARTS * j:PARTS * j + PARTS], ident)
                    last.then_inc(m.idxT_ps, 1)
                pe.wait_ge(m.idxT_done, TILES)
                pe.wait_ge(m.raw_done, m.base["raw_done"] + TILES)
                for t in range(1, TILES):
                    for hd in range(IDX_HEADS):
                        n = (t - 1) * IDX_HEADS + hd
                        if n >= IDX_HEADS:
                            pe.wait_ge(m.rel_done, n - IDX_HEADS + 1)
                        lo = HEAD * (hd % 2)
                        T.matmul(ps[:, hd, 0:PARTS * (t + 1)], idxT[lo:lo + HEAD, hd // 2, PARTS * t:PARTS * t + PARTS], idxT[lo:lo + HEAD, 2, 0:PARTS * (t + 1)],
                                 start=True, stop=True).then_inc(m.rel_ps, 1)
                for t in range(TILES):
                    pe.wait_ge(m.rot_done, m.base["rot_done"] + t + 1)
                    for g in range(2):
                        if t:
                            pe.wait_ge(m.qkT_done, m.base["qkT_done"] + 2 * t + g - 1)
                        for j in range(4 if g == 0 else 1):
                            last = T.transpose(ps[:, 6 + g, PARTS * j:PARTS * j + PARTS], qk_rot0[:, t, 512 * g + PARTS * j:512 * g + PARTS * j + PARTS], ident)
                        last.then_inc(m.qkT_ps, 1)
                pe.wait_ge(m.rel_done, 3 * IDX_HEADS)
                pe.wait_ge(m.w_conv_in, 16)
                for c in range(CONV // PARTS):
                    for g, gate in enumerate((1, 2, 0)):
                        if c >= 2:
                            pe.wait_ge(m.conv_in_done, 3 * (c - 2) + g + 1)
                        lo = gate * CONV + PARTS * c
                        for k in range(CHUNKS):
                            last = T.matmul(ps[:, 3 * (c % 2) + g, :], w_conv[:, k, lo:lo + PARTS], hT0[:, k, :], start=k == 0, stop=k == CHUNKS - 1)
                        last.then_inc(m.conv_ps, 1)
                pe.wait_ge(m.conv_ps, 3 * CONV // PARTS)
                pe.sem_inc(m.conv_over, 1)
                pe.wait_ge(m.conv_in_done, 3 * CONV // PARTS)
                pe.wait_ge(m.qkT_done, m.base["qkT_done"] + 2 * TILES)
                pe.wait_ge(m.v_done, TILES)
                attention(0, DSA_HEADS, qT0, kT0, v0, lambda hd: 0)
                project_out(0)

            def mixer1():
                m = M[1]
                norm(2)
                hT1 = feature_major[0][:, :].rearrange("p (c n) -> p c n", c=CHUNKS)
                pe.wait_ge(m.w_in, m.base["w_in"] + 16)

                def transposes(t):
                    pe.wait_ge(m.rot_done, m.base["rot_done"] + t + 1)
                    for g in range(3):
                        if 3 * t + g >= 2:
                            pe.wait_ge(m.qkT_done, m.base["qkT_done"] + 3 * t + g - 1)
                        for j in range(4):
                            at = 512 * g + PARTS * j
                            last = T.transpose(ps[:, 6 + (3 * t + g) % 2, PARTS * j:PARTS * j + PARTS], qk_rot1[:, at:at + PARTS], ident)
                        last.then_inc(m.qkT_ps, 1)
                for t in range(TILES):
                    if t >= 2:
                        pe.wait_ge(m.raw_done, m.base["raw_done"] + t - 1)
                    for g in range(3):
                        last = project(ps[:, 3 * (t % 2) + g, :], hT1, slice(PARTS * t, PARTS * t + PARTS), w_in1, 512 * g, 512 * g + 512)
                    last.then_inc(m.in_ps, 1)
                    if t:
                        transposes(t - 1)
                pe.wait_ge(m.in_ps, m.base["in_ps"] + TILES)
                pe.sem_inc(m.in_over, 1)
                transposes(TILES - 1)
                pe.wait_ge(m.qkT_done, m.base["qkT_done"] + 3 * TILES)
                attention(1, DIL_HEADS, qT1, kT1, v1, lambda hd: hd // (DIL_HEADS // DIL_KV))
                project_out(1)

            def moe(l):
                s = L[l]
                norm(2 * l + 1)
                pe.wait_ge(s.router_in, 112)
                for t in range(TILES):
                    for c in range(CHUNKS):
                        last = nc.tensor.matmul(ps[:, 4, N_ROUTER * t:N_ROUTER * (t + 1)], xnT[:, c, PARTS * t:PARTS * t + PARTS], w_router[:, c, :],
                                                start=c == 0, stop=c == CHUNKS - 1)
                last.then_inc(s.logits_done, 1)
                pe.wait_ge(s.picked_done, 1)
                for t in range(TILES):
                    for t0 in range(t + 1):
                        nc.tensor.matmul(ps[:, 5, N_EXPERTS * t:N_EXPERTS * (t + 1)], before if t0 == t else ones, picked[:, t0, :],
                                         start=t0 == 0, stop=t0 == t)
                for t in range(TILES):
                    last = nc.tensor.matmul(ps[:, 6, 0:N_EXPERTS], ones, picked[:, t, :], start=t == 0, stop=t == TILES - 1)
                last.then_inc(s.rank_done, 1)

                def steps(b):
                    pe.wait_ge(s.hot_ready, b + 1)
                    for t in range(TILES):
                        for k in range(TOP_K):
                            last = nc.tensor.matmul(ps[:, 7, 0:3 * N_EXPERTS], slot_hot[:, t, k, :], row_hot[:, t, k, :],
                                                    start=t + k == 0, stop=t + k == TILES + TOP_K - 2)
                    last.then_inc(s.fetch_ps, 1)
                    with pe.Fori(0, N_EXPERTS // 2) as i:
                        for u in range(2):
                            n = b * N_EXPERTS + 2 * i + u
                            arrived = (b * (N_EXPERTS // 2) + i + 1) * 16
                            pe.wait_ge(s.xg_in[u], arrived)
                            for j in range(4):
                                last = nc.tensor.transpose(ps[:, 0, PARTS * j:PARTS * j + PARTS], xg[u][:, PARTS * j:PARTS * j + PARTS], ident)
                            last.then_inc(s.x_transposed, 1)
                            pe.wait_ge(s.xT_done, n + 1)
                            for part in range(2):
                                w = ring_part(3 * u + part)
                                pe.wait_ge(s.weights_in[3 * u + part], arrived)
                                for c in range(CHUNKS):
                                    x_c = xT[u][:, PARTS * (c % 4) + CAP * (c // 4):PARTS * (c % 4) + CAP * (c // 4) + CAP]
                                    for hf in range(2):
                                        last = nc.tensor.matmul(ps[CAP * hf:CAP * hf + CAP, 1 + part, 0:256], x_c, w[:, c, 256 * hf:256 * hf + 256],
                                                                start=c == 0, stop=c == CHUNKS - 1)
                                last.then_inc(s.parts_done, 1)
                            pe.wait_ge(s.h_done, n + 1)
                            for j in range(2):
                                last = nc.tensor.transpose(ps[:, 3, PARTS * j:PARTS * j + PARTS], h[:, PARTS * j:PARTS * j + PARTS], ident)
                            last.then_inc(s.h_transposed, 1)
                            w = ring_part(3 * u + 2)
                            pe.wait_ge(s.weights_in[3 * u + 2], arrived)
                            pe.wait_ge(s.hT_done, n + 1)
                            for c in range(4):
                                h_c = hT[:, PARTS * (c % 2) + CAP * (c // 2):PARTS * (c % 2) + CAP * (c // 2) + CAP]
                                for hf in range(2):
                                    last = nc.tensor.matmul(ps[CAP * hf:CAP * hf + CAP, 4, :], h_c, w[:, c, 512 * hf:512 * hf + 512],
                                                            start=c == 0, stop=c == 3)
                            last.then_inc(s.parts_done, 1)
                steps(0)
                pe.wait_ge(s.count_done, 1)
                most = pe.value_load(max_count[0:1, 0:1], min_val=0, max_val=TOKENS)
                with pe.Fori(1, LEVELS) as b:
                    with pe.If(most > b * CAP):
                        steps(b)
            for l in layers:
                if mixers:
                    (mixer0, mixer1)[l]()
                if moes:
                    moe(l)


_SHARED = ["x"]
_BY_LAYER = ["attn_norm", "w_in", "q_norm", "k_norm", "w_out", "ffn_norm", "w_rg", "b_rg", "w_re", "b_re", "w_gate", "w_up", "w_down"]
_INS = _SHARED + ["conv_w_0"] + [f"{n}_{l}" for l in range(2) for n in _BY_LAYER]


def kernel(**inputs):
    import numpy as _np
    import concourse.bacc as _bacc
    from concourse import mybir as _mybir
    from concourse.bass_utils import run_bass_kernel_spmd as _run

    nc = _bacc.Bacc("TRN2", target_bir_lowering=False, num_devices=1)
    arrays, aps = {}, {}
    for name in _INS + ["consts"]:
        a = constant_table() if name == "consts" else _np.ascontiguousarray(inputs[name])
        if name == "x":
            a = a.reshape(TOKENS, D_MODEL)
        arrays[f"in_{name}_dram"] = a
        aps[name] = nc.dram_tensor(f"in_{name}_dram", a.shape, _mybir.dt.from_np(a.dtype), kind="ExternalInput").ap()
    aps["out"] = nc.dram_tensor("out_0_dram", (TOKENS, D_MODEL), _mybir.dt.float32, kind="ExternalOutput").ap()
    trunk(nc, aps)
    r = _run(nc, [arrays], core_ids=[0])
    return r.results[0]["out_0_dram"].reshape(1, TOKENS, D_MODEL)
```

```python
import concourse.bass as bass
from concourse import mybir
from contextlib import ExitStack

TOKENS, D_MODEL, PARTS = 512, 1024, 128
TILES = TOKENS // PARTS
CHUNKS = D_MODEL // PARTS
N_GROUPS, PER_GROUP = 4, 8
N_EXPERTS = N_GROUPS * PER_GROUP
N_ROUTER = N_GROUPS + N_EXPERTS
HEAD = 64
HALF = HEAD // 2
ROPE_THETA = 10000.0
CONV = 512
TAPS = 3
N_CONV_COLS = 3 * CONV
DSA_HEADS, IDX_HEADS, DSA_KEEP = 8, 4, 128
N_QKV0 = (DSA_HEADS + 2) * HEAD
N_IDX0 = (IDX_HEADS + 1) * HEAD + IDX_HEADS
DIL_HEADS, DIL_KV = 16, 4
PATTERNS = ((128, 1), (512, 4), (2048, 16))
N_QK1 = (DIL_HEADS + DIL_KV) * HEAD
N_V1 = DIL_KV * HEAD
SCALE = HEAD ** -0.5
D_EXPERT = 512
TOP_K = 2
CAP = 64
AHEAD = 3
ORDER = ((0, 0), (0, 1), (1, 0), (1, 1), (0, 2), (1, 2))
LEVELS = TOKENS // CAP
NORM_EPS = 1e-6
BIG = 1e30
TAKEN = -3e38

CONST_WIDTHS = dict(ident=128, ones=128, before=128, iota_slot=128, iota_expert=32, iota_group=4,
                    token=4, half=1, eps_pow=2,
                    rope_cos=256, rope_sin=256, strip=512, causal=128)
CONST_AT, _at = {}, 0
for _name, _width in CONST_WIDTHS.items():
    CONST_AT[_name] = (_at, _at + _width)
    _at += _width
N_CONST = _at


def constant_table():
    import numpy as np
    p = np.arange(PARTS)
    table = np.zeros((PARTS, N_CONST), np.float32)

    def put(name, value):
        a, b = CONST_AT[name]
        table[:, a:b] = value
    put("ident", np.eye(PARTS))
    put("ones", 1.0)
    put("before", p[:, None] < p[None, :])
    put("iota_slot", np.arange(PARTS)[None] % CAP)
    put("iota_expert", np.arange(N_EXPERTS)[None])
    put("iota_group", np.arange(N_GROUPS)[None])
    put("token", p[:, None] + PARTS * np.arange(TILES)[None])
    put("half", (p >= CAP)[:, None])
    angle = np.arange(TOKENS)[:, None].astype(np.float32) * (ROPE_THETA ** (-np.arange(HALF, dtype=np.float32) / HALF)).astype(np.float32)
    by_tile = lambda v: v.reshape(TILES, PARTS, HEAD).transpose(1, 0, 2).reshape(PARTS, -1)
    put("rope_cos", by_tile(np.concatenate([np.cos(angle), np.cos(angle)], 1)))
    put("rope_sin", by_tile(np.concatenate([-np.sin(angle), np.sin(angle)], 1)))
    back = p[:, None] + (TOKENS - PARTS) - np.arange(TOKENS)[None]
    seen = sum(((back >= 0) & (back <= w) & (back % d == 0)).astype(int) for w, d in PATTERNS)
    put("strip", np.where(seen > 0, np.log(np.maximum(seen, 1)) / SCALE, -BIG))
    put("causal", np.where(p[None, :] <= p[:, None], 0.0, -BIG))
    put("eps_pow", [[NORM_EPS, -0.5]])
    return table


def trunk(nc, a, layers=(0, 1), mixers=True, moes=True):
    f32, i32 = mybir.dt.float32, mybir.dt.int32
    ALU, ACT, AX = mybir.AluOpType, mybir.ActivationFunctionType, mybir.AxisListType.X
    ctx = ExitStack()
    with ctx:
        def sb(name, shape, dt=f32):
            return ctx.enter_context(nc.sbuf_tensor(name, shape, dt))

        def sem(name):
            return ctx.enter_context(nc.semaphore(name))

        ring = sb("ring", [PARTS, 6, 4096])
        x_res = sb("x_res", [PARTS, TILES, D_MODEL])
        buf1 = sb("buf1", [PARTS, 4096])
        buf2 = sb("buf2", [PARTS, 4096])
        const = sb("const", [PARTS, N_CONST])
        w_router = sb("w_router", [PARTS, CHUNKS, N_ROUTER])
        b_router = sb("b_router", [PARTS, N_ROUTER])
        gain = sb("gain", [PARTS, 4, CHUNKS])
        w_mix = sb("w_mix", [PARTS, 12288])
        head_gain = sb("head_gain", [PARTS, 4, HEAD])
        rope = sb("rope", [PARTS, 4, TILES, HEAD])
        logitT = rope[:, :, :, :].rearrange("p a t d -> p (a t d)")[0:N_ROUTER, 0:TOKENS]
        conv_w = sb("conv_w", [PARTS, CONV // PARTS, TAPS])
        idx_w = sb("idx_w", [PARTS, TILES, IDX_HEADS])
        best8 = sb("best8", [PARTS, 8])
        neg_max = sb("neg_max", [PARTS, 4])
        denom = sb("denom", [PARTS, 2, 8])
        head_ss = sb("head_ss", [PARTS, 2, DIL_HEADS + DIL_KV])
        sumsq = sb("sumsq", [PARTS, TILES])
        gates = sb("gates", [PARTS, TOP_K, TILES])
        fetch = sb("fetch", [PARTS, N_EXPERTS], i32)
        fetch_now = sb("fetch_now", [PARTS, 2], i32)
        max_count = sb("max_count", [PARTS, 1], i32)
        ps = ctx.enter_context(nc.psum_tensor("ps", [PARTS, 8, 512], f32))
        xn_dram = nc.dram_tensor("xn_dram", (TOKENS, D_MODEL), f32, kind="Internal").ap()

        def con(name):
            lo, hi = CONST_AT[name]
            return const[:, lo:hi]

        ident, ones, before = con("ident"), con("ones"), con("before")

        xn = buf1[:, :].rearrange("p (t d) -> p t d", t=TILES)
        xnT = buf2[:, :].rearrange("p (c n) -> p c n", c=CHUNKS)
        xg = [buf1[:, 512 * u:512 * u + 512] for u in range(2)]
        xT = [buf1[:, 1024 + 512 * u:1536 + 512 * u] for u in range(2)]
        y = buf1[:, 2048:3072]
        silu = buf1[:, 3072:3328]
        h = buf1[:, 3328:3584]
        hT = [buf1[:, 3584 + 256 * u:3840 + 256 * u] for u in range(2)]

        def b2(at, *dims):
            n = 1
            for d in dims:
                n *= d
            v = buf2[:, at:at + n]
            if len(dims) == 1:
                return v
            if len(dims) == 2:
                return v.rearrange("p (a b) -> p a b", a=dims[0])
            return v.rearrange("p (a b c) -> p a b c", a=dims[0], b=dims[1])
        slot_hot = b2(0, TILES, TOP_K, PARTS)
        row_hot = b2(2304, TILES, TOP_K, N_EXPERTS)
        gate_at = b2(3072, TILES, PARTS)
        gate_at2 = rope[:, :, :, :].rearrange("p a t d -> p (a t d)")[:, 512:1024].rearrange("p (t s) -> p t s", t=TILES)
        gateT = b2(3584, TILES, PARTS)
        hot = [b2(1280, TILES, N_EXPERTS), b2(1408, TILES, N_EXPERTS)]
        picked = b2(1536, TILES, N_EXPERTS)
        logit = b2(1664, TILES, N_ROUTER)
        lm = b2(1808, TILES, N_EXPERTS)
        tmp = b2(1936, TILES, N_EXPERTS)
        at4 = b2(2064, TILES, N_GROUPS)
        hot4 = b2(2080, TILES, N_GROUPS)
        exp4 = b2(2096, TILES, N_GROUPS)
        pen4 = b2(2112, TILES, N_GROUPS)
        gmax = b2(2128, TILES)
        gidx = b2(2132, TILES)
        top = [b2(2136, TILES), b2(2140, TILES)]
        eid = b2(2144, TOP_K, TILES)
        rank = b2(2152, TOP_K, TILES)
        gap = b2(2176, TILES)
        e21 = b2(2180, TILES)
        inv = b2(2184, TILES)
        p_group = b2(2188, TILES)
        cmax = b2(2192, 1)

        token_major = [buf2, buf1]
        feature_major = [buf1, buf2]
        mixed = buf2[:, :].rearrange("p (c n) -> p c n", c=CHUNKS)
        scratch = ring[:, 3:6, :].rearrange("p j n -> p (j n)")
        w_conv = ring[:, 0:3, :].rearrange("p j n -> p (j n)").rearrange("p (c n) -> p c n", c=CHUNKS)

        def part(buf, at, *dims):
            n = 1
            for d in dims:
                n *= d
            v = buf[:, at:at + n]
            if len(dims) == 2:
                v = v.rearrange("p (a b) -> p a b", a=dims[0])
            if len(dims) == 3:
                v = v.rearrange("p (a b c) -> p a b c", a=dims[0], b=dims[1])
            return v

        qT0 = part(scratch, 0, DSA_HEADS // 2, TOKENS)
        kT0 = part(scratch, 10640, 1, 2, TOKENS)
        idx_qT = part(scratch, 2048, IDX_HEADS // 2, TOKENS)
        idx_kT = part(scratch, 3072, 1, 2, TOKENS)
        v0 = part(scratch, 4096, TILES, HEAD)
        score = [None] + [part(scratch, at, n) for at, n in ((4352, 256), (4608, 384), (4992, 512))]
        relu = part(scratch, 5504, 2, TOKENS)
        idx_raw = part(scratch, 6528, TILES, N_IDX0)
        idx_sin = part(scratch, 7824, IDX_HEADS + 1, HEAD)
        qk_raw0 = part(scratch, 8144, 2, N_QKV0)
        qk_sq0 = part(scratch, 9424, N_QKV0)
        qk_sin0 = part(scratch, 10064, DSA_HEADS + 1, HEAD)
        conv_in = part(scratch, 6528, 3, TOKENS)
        conv_u = part(scratch, 8064, TOKENS + TAPS - 1)
        conv_y = part(scratch, 8578, 2, TOKENS)
        idx_rot = part(buf2, 0, TILES, 3 * PARTS)
        qk_rot0 = part(buf2, 1536, TILES, 5 * PARTS)
        w_idx = part(w_mix, 0, CHUNKS, N_IDX0)
        w_qkv0 = part(w_mix, CHUNKS * N_IDX0, CHUNKS, N_QKV0)
        qT1 = part(scratch, 0, DIL_HEADS // 2, TOKENS)
        kT1 = part(scratch, 4096, DIL_KV, 2, TOKENS)
        v1 = part(scratch, 8192, TILES, N_V1)
        qk_raw1 = part(scratch, 9216, N_QK1)
        qk_sq1 = part(scratch, 10496, N_QK1)
        qk_rot1 = part(buf2, 0, 2, DIL_HEADS * HEAD + 2 * DIL_KV * HEAD)
        w_in1 = part(w_mix, 0, CHUNKS, N_QK1 + N_V1)
        w_out = part(w_mix, 0, CHUNKS, D_MODEL)
        prob = part(buf1, 0, 4, TOKENS)
        probT = part(buf1, 2048, 2, TOKENS)

        consts_in = sem("consts_in")
        out_stored = sem("out_stored")
        dve_chain = sem("dve_chain")
        pool_chain = sem("pool_chain")
        x_in = [sem(f"x_in{t}") for t in range(TILES)]
        x_ready = [sem(f"x_ready{i}") for i in range(5)]

        params_in = sem("params_in")
        def signals(kind, by_name):
            return type(kind, (), by_name)()

        first_layer, first_norm = layers[0], 2 * layers[0] + (0 if mixers else 1)
        N = []
        shared = {n: sem(n) for n in "ss_done rstd_done xn_done xT_ps xT_done".split()}
        for z in range(4):
            s = signals("NormSignals", shared)
            before_it = z - first_norm if mixers else (z - first_norm) // 2
            s.base = {n: before_it * (2 * TILES if n[:2] == "xT" else TILES) for n in shared}
            N.append(s)
        pairs0, groups0 = TILES * DSA_HEADS // 2, TILES * DSA_HEADS // 8
        mixer0_counts = dict(w_in_a=16, w_in_b=16, w_in_c=16, w_out_in=16, head_gain_in=96, in_ps=TILES, raw_done=TILES, sq_done=TILES,
                             head_ss_done=TILES, head_rstd_done=TILES, normed=TILES, sin_done=TILES, rot_done=TILES, qkT_ps=2 * TILES,
                             qkT_done=2 * TILES, in_over=1, out_over=1, zeros_done=1, tables_done=1, s_ps=2 * pairs0, masked_done=2 * pairs0,
                             exp_done=2 * pairs0, pT_ps=2 * pairs0, pT_dve=pairs0, pT_act=pairs0, pv_done=pairs0,
                             inv_done=groups0, spread_ps=groups0, o_done=groups0, mixed_done=groups0,
                             out_ps=2 * TILES, out_half=2 * TILES)
        shared = {n: sem(n) for n in mixer0_counts}
        M = []
        for l in range(2):
            only = ("v_done idx_ps idx_raw_done idx_sin_done idx_rot_done idxT_ps idxT_done "
                    "rel_ps rel_done rel_used idx_w_done conv_ps conv_in_done conv_done conv_over") if l == 0 else ""
            s = signals("MixerSignals", {**shared, **{n: sem(n) for n in only.split()}})
            s.base = {n: count * (l - first_layer) for n, count in mixer0_counts.items()}
            M.append(s)
        L = []
        for l in range(2):
            s = signals("ExpertSignals", {n: sem(f"{n}_{l}") for n in ("router_in xn_stored logitT_ps logitT_done logits_done exp_in exp_done "
                      "picked_done rank_done hot_ready fetch_ps fetch_done count_done fetch_copied pool_turn rank_shifted "
                      "x_transposed xT_done parts_done silu_done h_done h_transposed hT_done y_evac "
                      "gate_steps gateT_ps gateT_done added_ps added passes_over").split()})
            s.weights_in = [sem(f"weights_in{j}_{l}") for j in range(6)]
            s.ahead_in = [sem(f"ahead_in{q}_{l}") for q in range(AHEAD)]
            s.xg_in = [sem(f"xg_in{u}_{l}") for u in range(2)]
            L.append(s)

        def expert_weights(l, e):
            for name in ("w_gate", "w_up", "w_down"):
                w = a[f"{name}_{l}"][e]
                if name == "w_down":
                    yield w.rearrange("(c p) n -> p c n", p=PARTS)
                else:
                    yield w.rearrange("(c p) n -> p c n", p=PARTS)

        def ring_part(j):
            n = D_EXPERT if j % 3 < 2 else D_MODEL
            return ring[:, j, :].rearrange("p (c n) -> p c n", n=n)

        def ahead(q):
            return w_mix[:, 4096 * q:4096 * (q + 1)].rearrange("p (c n) -> p c n", n=D_EXPERT)

        def block_of(pair, heads):
            t = pair * 2 // heads
            group = pair // 4
            return t, CHUNKS - heads // 2 + 4 * (group % (heads // 8)), group

        block = ctx.enter_context(nc.Block())

        @block.sync
        def _(sp):
            for t in range(TILES):
                sp.dma_start(x_res[:, t, :], a["x"][PARTS * t:PARTS * t + PARTS, :]).then_inc(x_in[t], 16)
                if t == 0:
                    sp.dma_start(const[:, :], a["consts"]).then_inc(consts_in, 16)
            for z, name in enumerate(("attn_norm_0", "ffn_norm_0", "attn_norm_1", "ffn_norm_1")):
                sp.dma_start(gain[:, z, :], a[name].rearrange("(c p) -> p c", p=PARTS), allow_slow_non_contiguous=True).then_inc(params_in, 16)
            sp.dma_start(conv_w[:, :, :], a["conv_w_0"].rearrange("(c p) j -> p c j", p=PARTS)).then_inc(params_in, 16)

            def head_gains(l):
                for j, name in enumerate((f"q_norm_{l}", f"k_norm_{l}")):
                    row = a[name].rearrange("(o d) -> o d", o=1)
                    sp.dma_start(head_gain[:, 2 * j, :], row.broadcast_to([PARTS, HEAD])).then_inc(M[l].head_gain_in, 16)
                    sp.dma_start(head_gain[:, 2 * j + 1, 0:HALF], row[:, HALF:].broadcast_to([PARTS, HALF])).then_inc(M[l].head_gain_in, 16)
                    sp.dma_start(head_gain[:, 2 * j + 1, HALF:], row[:, 0:HALF].broadcast_to([PARTS, HALF])).then_inc(M[l].head_gain_in, 16)

            def load_w_out(l):
                sp.dma_start(w_out, a[f"w_out_{l}"].rearrange("(c p) n -> p c n", p=PARTS)).then_inc(M[l].w_out_in, 16)

            def load_pair(l, i):
                both = [list(expert_weights(l, 2 * i + u)) for u in range(2)]
                for q, (u, j) in enumerate(ORDER):
                    yield q, 3 * u + j, both[u][j]

            def moe(l):
                s = L[l]
                sp.dma_start(w_router[:, :, 0:N_GROUPS], a[f"w_rg_{l}"].rearrange("(c p) g -> p c g", p=PARTS)).then_inc(s.router_in, 16)
                for g in range(N_GROUPS):
                    sp.dma_start(w_router[:, :, N_GROUPS + g * PER_GROUP:N_GROUPS + (g + 1) * PER_GROUP],
                                 a[f"w_re_{l}"][g].rearrange("(c p) e -> p c e", p=PARTS)).then_inc(s.router_in, 16)
                sp.dma_start(b_router[:, 0:N_GROUPS], a[f"b_rg_{l}"].rearrange("(o g) -> o g", o=1).broadcast_to([PARTS, N_GROUPS])).then_inc(s.router_in, 16)
                sp.dma_start(b_router[:, N_GROUPS:], a[f"b_re_{l}"].rearrange("(o g) e -> o (g e)", o=1).broadcast_to([PARTS, N_EXPERTS])).then_inc(s.router_in, 16)
                for q, j, src in load_pair(l, 0):
                    if j == 3 and mixers:
                        sp.wait_ge(M[l].pv_done, M[l].base["pv_done"] + TILES * (DSA_HEADS if l == 0 else DIL_HEADS) // 2)
                        if l == 0:
                            sp.wait_ge(M[0].conv_done, CONV // PARTS)
                    sp.dma_start(ring_part(j), src).then_inc(s.weights_in[j], 16)
                for t in range(TILES):
                    sp.wait_ge(N[2 * l + 1].xn_done, N[2 * l + 1].base["xn_done"] + t + 1)
                    sp.dma_start(xn_dram[PARTS * t:PARTS * t + PARTS, :], xn[:, t, :]).then_inc(s.xn_stored, 16)

                if mixers:
                    sp.wait_ge(M[l].out_over, M[l].base["out_over"] + 1)
                for q, j, src in list(load_pair(l, 1))[:AHEAD]:
                    sp.dma_start(ahead(q), src).then_inc(s.ahead_in[q], 16)

                def steps(first, b):
                    with sp.Fori(first, N_EXPERTS // 2) as i:
                        for q, j, src in load_pair(l, i):
                            sp.wait_ge(s.parts_done, (b * (N_EXPERTS // 2) + i - 1) * 6 + q + 1)
                            sp.dma_start(ring_part(j), src).then_inc(s.weights_in[j], 16)
                for i, some in ((2, slice(0, AHEAD)), (1, slice(AHEAD, None)), (2, slice(AHEAD, None))):
                    for q, j, src in list(load_pair(l, i))[some]:
                        sp.wait_ge(s.parts_done, q + 1 if q < AHEAD else 6 * (i - 1) + q + 1)
                        sp.dma_start(ring_part(j), src).then_inc(s.weights_in[j], 16)
                steps(3, 0)
                if l == 0 and mixers and 1 in layers:
                    load_w_in1()
                    head_gains(1)
                sp.wait_ge(s.count_done, 1)
                most = sp.value_load(max_count[0:1, 0:1], min_val=0, max_val=TOKENS)
                with sp.Fori(1, LEVELS) as b:
                    with sp.If(most > b * CAP):
                        steps(0, b)

            def load_w_in1():
                for g, arrived in enumerate((M[1].w_in_a, M[1].w_in_b, M[1].w_in_c)):
                    cols = slice(512 * g, 512 * g + 512)
                    sp.dma_start(w_in1[:, :, cols], a["w_in_1"].rearrange("(c p) n -> p c n", p=PARTS)[:, :, cols]).then_inc(arrived, 16)

            def mixer0():
                w = a["w_in_0"].rearrange("(c p) n -> p c n", p=PARTS)
                sp.dma_start(w_idx, w[:, :, N_CONV_COLS + N_QKV0:]).then_inc(M[0].w_in_a, 16)
                sp.dma_start(w_qkv0, w[:, :, N_CONV_COLS:N_CONV_COLS + N_QKV0]).then_inc(M[0].w_in_b, 16)
                head_gains(0)
                sp.dma_start(w_conv, w[:, :, 0:N_CONV_COLS]).then_inc(M[0].w_in_c, 16)
                sp.wait_ge(M[0].in_over, M[0].base["in_over"] + 1)
                load_w_out(0)
                sp.wait_ge(M[0].conv_over, 1)

            def mixer1():
                if first_layer == 1:
                    load_w_in1()
                    head_gains(1)
                sp.wait_ge(M[1].in_over, M[1].base["in_over"] + 1)
                load_w_out(1)

            for l in layers:
                if mixers:
                    (mixer0, mixer1)[l]()
                if moes:
                    moe(l)
            for t in range(TILES):
                sp.wait_ge(x_ready[4], t + 1)
                sp.dma_start(a["out"][PARTS * t:PARTS * t + PARTS, :], x_res[:, t, :]).then_inc(out_stored, 16)
            sp.wait_ge(out_stored, 16 * TILES)

        @block.gpsimd
        def _(pool):
            chain = [0]

            def link(ins):
                chain[0] += 1
                ins.then_inc(pool_chain, 1)
                pool.wait_ge(pool_chain, chain[0])

            G = nc.gpsimd
            pool.wait_ge(consts_in, 16)

            def root(value, width, done, n):
                link(G.tensor_scalar(value, value, 1.0 / width, NORM_EPS, ALU.mult, ALU.add))
                G.tensor_tensor(value, value, con("eps_pow")[:, 1:2].broadcast_to([PARTS, n]), ALU.pow).then_inc(done, 1)

            def norm(z):
                for t in range(TILES):
                    pool.wait_ge(N[z].ss_done, N[z].base["ss_done"] + t + 1)
                    root(sumsq[:, t:t + 1], D_MODEL, N[z].rstd_done, 1)

            def head_norm(l, t, heads):
                pool.wait_ge(M[l].head_ss_done, M[l].base["head_ss_done"] + t + 1)
                root(head_ss[:, t % 2, 0:heads], HEAD, M[l].head_rstd_done, heads)

            def sine_terms(out, raw, sin):
                heads = out.shape[1]
                G.tensor_tensor(out[:, :, 0:HALF], raw[:, :, HALF:], sin[:, 0:HALF].unsqueeze(1).broadcast_to([PARTS, heads, HALF]), ALU.mult)
                return G.tensor_tensor(out[:, :, HALF:], raw[:, :, 0:HALF], sin[:, HALF:].unsqueeze(1).broadcast_to([PARTS, heads, HALF]), ALU.mult)

            def heads_of(v):
                return v.rearrange("p (h d) -> p h d", d=HEAD)

            def mixer0():
                m = M[0]
                norm(0)
                base_sin = con("rope_sin").rearrange("p (t d) -> p t d", d=HEAD)
                for t in range(TILES):
                    pool.wait_ge(m.idx_raw_done, t + 1)
                    if t:
                        pool.wait_ge(m.idx_rot_done, t)
                    sine_terms(idx_sin, heads_of(idx_raw[:, t, 0:(IDX_HEADS + 1) * HEAD]), base_sin[:, t, :]).then_inc(m.idx_sin_done, 1)
                    G.tensor_scalar(idx_w[:, t, :], idx_raw[:, t, (IDX_HEADS + 1) * HEAD:], IDX_HEADS ** -0.5, None, ALU.mult).then_inc(m.idx_w_done, 1)
                pool.wait_ge(m.tables_done, m.base["tables_done"] + 1)
                for t in range(TILES):
                    raw = qk_raw0[:, t % 2, :]
                    pool.wait_ge(m.raw_done, m.base["raw_done"] + t + 1)
                    G.tensor_copy(v0[:, t, :], raw[:, (DSA_HEADS + 1) * HEAD:]).then_inc(m.v_done, 1)
                    head_norm(0, t, DSA_HEADS + 1)
                    pool.wait_ge(m.normed, m.base["normed"] + t + 1)
                    if t:
                        pool.wait_ge(m.rot_done, m.base["rot_done"] + t)
                    sine_terms(qk_sin0[:, 0:DSA_HEADS, :], heads_of(raw[:, 0:DSA_HEADS * HEAD]), rope[:, 1, t, :])
                    sine_terms(qk_sin0[:, DSA_HEADS:, :], heads_of(raw[:, DSA_HEADS * HEAD:(DSA_HEADS + 1) * HEAD]), rope[:, 3, t, :]).then_inc(m.sin_done, 1)
                pool.wait_ge(m.qkT_ps, m.base["qkT_ps"] + 2 * TILES)
                link(G.memset(conv_u[:, 0:TAPS - 1], 0.0))
                for c in range(CONV // PARTS):
                    pool.wait_ge(m.conv_in_done, 3 * c + 2)
                    u = conv_u[:, TAPS - 1:]
                    link(G.tensor_tensor(u, conv_in[:, 0, :], conv_in[:, 1, :], ALU.mult))
                    link(G.tensor_scalar(conv_y[:, 0, :], conv_u[:, 0:TOKENS], conv_w[:, c, 0:1], None, ALU.mult))
                    for j in range(1, TAPS):
                        link(G.tensor_scalar(conv_y[:, 1, :], conv_u[:, j:j + TOKENS], conv_w[:, c, j:j + 1], None, ALU.mult))
                        link(G.tensor_tensor(conv_y[:, 0, :], conv_y[:, 0, :], conv_y[:, 1, :], ALU.add))
                    pool.wait_ge(m.conv_in_done, 3 * c + 3)
                    G.tensor_tensor(mixed[:, c, :], conv_y[:, 0, :], conv_in[:, 2, :], ALU.mult).then_inc(m.conv_done, 1)

            def mixer1():
                m = M[1]
                norm(2)
                pool.wait_ge(m.tables_done, m.base["tables_done"] + 1)
                nq = DIL_HEADS * HEAD
                sin_terms = heads_of(qk_sq1)
                for t in range(TILES):
                    head_norm(1, t, DIL_HEADS + DIL_KV)
                    pool.wait_ge(m.normed, m.base["normed"] + t + 1)
                    sine_terms(sin_terms[:, 0:DIL_HEADS, :], heads_of(qk_raw1[:, 0:nq]), rope[:, 1, t, :])
                    sine_terms(sin_terms[:, DIL_HEADS:, :], heads_of(qk_raw1[:, nq:]), rope[:, 3, t, :]).then_inc(m.sin_done, 1)

            def moe(l):
                s = L[l]
                norm(2 * l + 1)
                pool.wait_ge(s.xn_stored, 16 * TILES)

                def gather(b, i, u):
                    nc.gpsimd.tensor_copy(fetch_now[:, u:u + 1], fetch[:, bass.ds(2 * i + u, 1)]).then_inc(s.fetch_copied, 1)
                    pool.wait_ge(s.fetch_copied, b * N_EXPERTS + 2 * i + u + 1)
                    pool.sem_inc(s.pool_turn, 1)
                    pool.indirect_dma_start(out=xg[u], out_offset=None, in_=xn_dram.rearrange("t (h d) -> (t h) d", h=2),
                                            in_offset=bass.IndirectOffsetOnAxis(ap=fetch_now[:, u:u + 1], axis=0)).then_inc(s.xg_in[u], 16)

                def steps(b):
                    pool.wait_ge(s.fetch_done, b + 1)
                    pool.sem_inc(s.pool_turn, 1)
                    for u in range(2):
                        gather(b, 0, u)
                    with pool.Fori(0, N_EXPERTS // 2 - 1) as i:
                        for u in range(2):
                            pool.wait_ge(s.x_transposed, b * N_EXPERTS + 2 * i + u + 1)
                            gather(b, i + 1, u)
                steps(0)
                pool.wait_ge(s.count_done, 1)
                most = pool.value_load(max_count[0:1, 0:1], min_val=0, max_val=TOKENS)
                with pool.Fori(1, LEVELS) as b:
                    with pool.If(most > b * CAP):
                        steps(b)
            for l in layers:
                if mixers:
                    (mixer0, mixer1)[l]()
                if moes:
                    moe(l)

        @block.scalar
        def _(act):
            A = nc.scalar

            def norm(z):
                tok = token_major[z % 2][:, :].rearrange("p (t d) -> p t d", t=TILES)
                for t in range(TILES):
                    if z == first_norm:
                        act.wait_ge(x_in[t], 16)
                    else:
                        act.wait_ge(x_ready[z], t + 1)
                    A.activation(tok[:, t, :], x_res[:, t, :], ACT.Square, accum_out=sumsq[:, t:t + 1]).then_inc(N[z].ss_done, 1)

            def attention(l, heads):
                m = M[l]
                pairs = TILES * heads // 2
                for n in range(pairs + 4):
                    if n < pairs:
                        t, group = n * 2 // heads, n // 4
                        keys = PARTS * (t + 1)
                        if n % 4 == 0 and group >= 2:
                            act.wait_ge(m.spread_ps, m.base["spread_ps"] + group - 1)
                        for u in range(2):
                            b = 2 * (n % 2) + u
                            act.wait_ge(m.masked_done, m.base["masked_done"] + 2 * n + u + 1)
                            A.activation(prob[:, b, 0:keys], prob[:, b, 0:keys], ACT.Exp, bias=neg_max[:, b:b + 1], scale=-1.0,
                                         accum_out=denom[:, group % 2, 2 * (n % 4) + u:2 * (n % 4) + u + 1]).then_inc(m.exp_done, 1)
                    e = n - 1
                    if 0 <= e < pairs:
                        keys = PARTS * (e * 2 // heads + 1)
                        act.wait_ge(m.pT_ps, m.base["pT_ps"] + 2 * e + 2)
                        if e:
                            act.wait_ge(m.pv_done, m.base["pv_done"] + e)
                        A.activation(probT[:, 1, 0:keys], ps[:, 5, 0:keys], ACT.Copy).then_inc(m.pT_act, 1)
                    e = n - 2
                    if 0 <= e < pairs and e % 4 == 3:
                        t, c0, group = block_of(e, heads)
                        act.wait_ge(m.pv_done, m.base["pv_done"] + e + 1)
                        A.activation(mixed[:, c0:c0 + 4, PARTS * t:PARTS * t + PARTS], ps[:, 6, :].rearrange("p (c n) -> p c n", c=4), ACT.Copy).then_inc(m.o_done, 1)

            def keys_out(kT, t, src):
                src = src.rearrange("p (c n) -> p c n", n=PARTS)
                cols = slice(PARTS * t, PARTS * t + PARTS)
                A.activation(kT[0:HEAD, :, 0, cols], src[0:HEAD], ACT.Copy)
                return A.activation(kT[HEAD:, :, 1, cols], src[HEAD:], ACT.Copy)

            def mixer0():
                m = M[0]
                norm(0)
                for t in range(TILES):
                    act.wait_ge(m.idx_ps, t + 1)
                    A.activation(idx_raw[:, t, :], ps[:, t % 2, 0:N_IDX0], ACT.Copy).then_inc(m.idx_raw_done, 1)
                for t in range(TILES):
                    if t >= 2:
                        act.wait_ge(m.rot_done, m.base["rot_done"] + t - 1)
                        act.wait_ge(m.sin_done, m.base["sin_done"] + t - 1)
                        act.wait_ge(m.v_done, t - 1)
                    if t >= 1:
                        act.wait_ge(m.head_ss_done, m.base["head_ss_done"] + t)
                    act.wait_ge(m.in_ps, m.base["in_ps"] + t + 1)
                    b0 = 2 + 2 * (t % 2)
                    src = ps[:, b0:b0 + 2, 0:N_QKV0 // 2]
                    A.activation(qk_sq0.rearrange("p (a n) -> p a n", a=2), src, ACT.Square).then_inc(m.sq_done, 1)
                    A.activation(qk_raw0[:, t % 2, :].rearrange("p (a n) -> p a n", a=2), src, ACT.Copy).then_inc(m.raw_done, 1)
                for t in range(TILES):
                    act.wait_ge(m.idxT_ps, t + 1)
                    cols = slice(PARTS * t, PARTS * t + PARTS)
                    A.activation(idx_qT[:, :, cols], ps[:, 6 + t % 2, 0:2 * PARTS].rearrange("p (c n) -> p c n", c=2), ACT.Copy)
                    keys_out(idx_kT, t, ps[:, 6 + t % 2, 2 * PARTS:3 * PARTS]).then_inc(m.idxT_done, 1)
                for t in range(1, TILES):
                    keys = PARTS * (t + 1)
                    for hd in range(IDX_HEADS):
                        n = (t - 1) * IDX_HEADS + hd
                        act.wait_ge(m.rel_ps, n + 1)
                        if n >= 2:
                            act.wait_ge(m.rel_used, n - 1)
                        A.activation(relu[:, n % 2, 0:keys], ps[:, hd, 0:keys], ACT.Relu, scale=SCALE).then_inc(m.rel_done, 1)
                for t in range(TILES):
                    for g in range(2):
                        act.wait_ge(m.qkT_ps, m.base["qkT_ps"] + 2 * t + g + 1)
                        if g == 0:
                            A.activation(qT0[:, :, PARTS * t:PARTS * t + PARTS], ps[:, 6, :].rearrange("p (c n) -> p c n", c=4), ACT.Copy).then_inc(m.qkT_done, 1)
                        else:
                            keys_out(kT0, t, ps[:, 7, 0:PARTS]).then_inc(m.qkT_done, 1)
                for c in range(CONV // PARTS):
                    for g in range(3):
                        act.wait_ge(m.conv_ps, 3 * c + g + 1)
                        if c >= 1:
                            act.wait_ge(m.conv_done, c)
                        A.activation(conv_in[:, g, :], ps[:, 3 * (c % 2) + g, :], ACT.Copy).then_inc(m.conv_in_done, 1)
                attention(0, DSA_HEADS)

            def mixer1():
                m = M[1]
                norm(2)
                for t in range(TILES):
                    act.wait_ge(m.in_ps, m.base["in_ps"] + t + 1)
                    b0 = 3 * (t % 2)
                    if t:
                        act.wait_ge(m.rot_done, m.base["rot_done"] + t)
                    for g, (lo, hi) in enumerate(((0, 512), (512, 1024), (1024, 1280))):
                        last = A.activation(qk_sq1[:, lo:hi], ps[:, b0 + g, 0:hi - lo], ACT.Square)
                    last.then_inc(m.sq_done, 1)
                    for g, (lo, hi) in enumerate(((0, 512), (512, 1024), (1024, 1280))):
                        last = A.activation(qk_raw1[:, lo:hi], ps[:, b0 + g, 0:hi - lo], ACT.Copy)
                    last.then_inc(m.raw_done, 1)
                    if t:
                        transposed_out(t - 1)
                act.wait_ge(m.in_ps, m.base["in_ps"] + TILES + 1)
                A.activation(v1.rearrange("p (a t) n -> p a (t n)", a=2), ps[:, 0:2, :], ACT.Copy).then_inc(m.raw_done, 1)
                transposed_out(TILES - 1)
                attention(1, DIL_HEADS)

            def transposed_out(t):
                m = M[1]
                for g in range(3):
                    act.wait_ge(m.qkT_ps, m.base["qkT_ps"] + 3 * t + g + 1)
                    bank = ps[:, 6 + (3 * t + g) % 2, :]
                    if g < 2:
                        A.activation(qT1[:, 4 * g:4 * g + 4, PARTS * t:PARTS * t + PARTS], bank.rearrange("p (c n) -> p c n", c=4), ACT.Copy).then_inc(m.qkT_done, 1)
                    else:
                        keys_out(kT1, t, bank).then_inc(m.qkT_done, 1)

            def moe(l):
                s = L[l]
                norm(2 * l + 1)
                act.wait_ge(s.logitT_ps, TILES)
                A.activation(logitT, ps[0:N_ROUTER, 4, :], ACT.Copy).then_inc(s.logitT_done, 1)
                act.wait_ge(s.exp_in, 1)
                nc.scalar.activation(exp4[:, :, :], at4[:, :, :], ACT.Exp).then_inc(s.exp_done, 1)
                act.wait_ge(s.exp_in, 2)
                nc.scalar.activation(e21[:, :], gap[:, :], ACT.Exp).then_inc(s.exp_done, 1)

                def expert_pair(pair):
                    for u in range(2):
                        act.wait_ge(s.parts_done, 6 * pair + 2 * u + 1)
                        if u:
                            act.wait_ge(s.h_done, 2 * pair + 1)
                        A.activation(silu, ps[:, 1, 0:256], ACT.Silu).then_inc(s.silu_done, 1)
                    for u in range(2):
                        act.wait_ge(s.h_transposed, 2 * pair + u + 1)
                        A.activation(hT[u], ps[:, 3, 0:256], ACT.Copy).then_inc(s.hT_done, 1)
                    act.wait_ge(s.gateT_ps, pair + 1)
                    A.activation(gateT, ps[:, 0, :].rearrange("p (t n) -> p t n", t=TILES), ACT.Copy).then_inc(s.gateT_done, 1)
                    act.wait_ge(s.parts_done, 6 * pair + 6)
                    A.activation(y.rearrange("p (a n) -> p a n", a=2), ps[:, 4:6, :], ACT.Copy).then_inc(s.y_evac, 1)

                def steps(b):
                    with act.Fori(0, N_EXPERTS // 2) as i:
                        expert_pair(b * (N_EXPERTS // 2) + i)
                steps(0)
                act.wait_ge(s.count_done, 1)
                most = act.value_load(max_count[0:1, 0:1], min_val=0, max_val=TOKENS)
                with act.Fori(1, LEVELS) as b:
                    with act.If(most > b * CAP):
                        steps(b)
            for l in layers:
                if mixers:
                    (mixer0, mixer1)[l]()
                if moes:
                    moe(l)

        @block.vector
        def _(dve):
            chain = [0]

            def link(ins):
                chain[0] += 1
                ins.then_inc(dve_chain, 1)
                dve.wait_ge(dve_chain, chain[0])
            V = nc.vector

            def over(v, n):
                return v.unsqueeze(2).broadcast_to([PARTS, v.shape[1], n])

            def norm(z, before=lambda t: None):
                tok = token_major[z % 2][:, :].rearrange("p (t d) -> p t d", t=TILES)
                tr = feature_major[z % 2][:, :].rearrange("p (c n) -> p c n", c=CHUNKS)
                for step in range(TILES + 2):
                    if step < TILES:
                        before(step)
                    t = step - 1
                    if 0 <= t < TILES:
                        dve.wait_ge(N[z].rstd_done, N[z].base["rstd_done"] + t + 1)
                        V.tensor_scalar(tok[:, t, :], x_res[:, t, :], sumsq[:, t:t + 1], None, ALU.mult).then_inc(N[z].xn_done, 1)
                    t = step - 2
                    if 0 <= t < TILES:
                        if t == 0:
                            dve.wait_ge(params_in, 80)
                        for g in range(2):
                            dve.wait_ge(N[z].xT_ps, N[z].base["xT_ps"] + 2 * t + g + 1)
                            V.tensor_tensor(tr[:, 4 * g:4 * g + 4, PARTS * t:PARTS * t + PARTS], ps[:, 6 + g, :].rearrange("p (c n) -> p c n", c=4),
                                            gain[:, z, 4 * g:4 * g + 4].unsqueeze(2).broadcast_to([PARTS, 4, PARTS]), ALU.mult).then_inc(N[z].xT_done, 1)

            def heads_of(v):
                return v.rearrange("p (h d) -> p h d", d=HEAD)

            def on_heads(v, heads):
                return v.unsqueeze(1).broadcast_to([PARTS, heads, HEAD])

            def zero_halves(m, *keys):
                for kT in keys:
                    V.memset(kT[HEAD:, :, 0, :], 0.0)
                    last = V.memset(kT[0:HEAD, :, 1, :], 0.0)
                last.then_inc(m.zeros_done, 1)

            def tables(l):
                dve.wait_ge(M[l].head_gain_in, M[l].base["head_gain_in"] + 96)
                for j in range(4):
                    base = con("rope_sin" if j % 2 else "rope_cos").rearrange("p (t d) -> p t d", d=HEAD)
                    last = V.tensor_tensor(rope[:, j, :, :], base, on_heads(head_gain[:, j, :], TILES), ALU.mult)
                link(last)
                dve.sem_inc(M[l].tables_done, 1)

            def rotate(m, t, raw, sin, rot, qh, kh):
                nq, nk = qh * HEAD, kh * HEAD
                dve.wait_ge(m.sq_done, m.base["sq_done"] + t + 1)
                sq = qk_sq0[:, 0:nq + nk] if qh == DSA_HEADS else qk_sq1
                V.tensor_reduce(head_ss[:, t % 2, 0:qh + kh], heads_of(sq), AX, ALU.add).then_inc(m.head_ss_done, 1)
                dve.wait_ge(m.head_rstd_done, m.base["head_rstd_done"] + t + 1)
                dve.wait_ge(m.raw_done, m.base["raw_done"] + t + 1)
                r3 = heads_of(raw[:, 0:nq + nk])
                V.tensor_tensor(r3, r3, head_ss[:, t % 2, 0:qh + kh].unsqueeze(2).broadcast_to([PARTS, qh + kh, HEAD]), ALU.mult).then_inc(m.normed, 1)
                dve.wait_ge(m.normed, m.base["normed"] + t + 1)
                q_rot = heads_of(rot[:, 0:nq])
                k_rot = rot[:, nq:nq + 2 * nk].rearrange("p (h two d) -> p h two d", two=2, d=HEAD)
                V.tensor_tensor(q_rot, r3[:, 0:qh, :], on_heads(rope[:, 0, t, :], qh), ALU.mult)
                link(V.tensor_tensor(k_rot[:, :, 0, :], r3[:, qh:, :], on_heads(rope[:, 2, t, :], kh), ALU.mult))
                dve.wait_ge(m.sin_done, m.base["sin_done"] + t + 1)
                V.tensor_tensor(q_rot, q_rot, sin[:, 0:qh, :], ALU.add)
                link(V.tensor_tensor(k_rot[:, :, 1, :], k_rot[:, :, 0, :], sin[:, qh:, :], ALU.add))
                link(V.tensor_tensor(k_rot[:, :, 0, :], k_rot[:, :, 0, :], sin[:, qh:, :], ALU.add))
                dve.sem_inc(m.rot_done, 1)

            def attention(l, heads, mask_of):
                m = M[l]
                pairs = TILES * heads // 2
                for n in range(pairs + 4):
                    if n < pairs:
                        t = n * 2 // heads
                        keys = PARTS * (t + 1)
                        for u in range(2):
                            b = 2 * (n % 2) + u
                            dve.wait_ge(m.s_ps, m.base["s_ps"] + 2 * n + u + 1)
                            if n >= 2:
                                dve.wait_ge(m.pT_ps, m.base["pT_ps"] + 2 * n - 3 + u)
                            V.tensor_tensor_reduce(out=prob[:, b, 0:keys], in0=ps[:, b, 0:keys], in1=mask_of(t), scale=-SCALE, scalar=-TAKEN,
                                                   op0=ALU.add, op1=ALU.min, accum_out=neg_max[:, b:b + 1]).then_inc(m.masked_done, 1)
                    e = n - 1
                    if 0 <= e < pairs:
                        keys = PARTS * (e * 2 // heads + 1)
                        if e % 4 == 3:
                            g = e // 4
                            dve.wait_ge(m.exp_done, m.base["exp_done"] + 2 * e + 2)
                            V.reciprocal(denom[:, g % 2, :], denom[:, g % 2, :]).then_inc(m.inv_done, 1)
                        dve.wait_ge(m.pT_ps, m.base["pT_ps"] + 2 * e + 1)
                        if e:
                            dve.wait_ge(m.pv_done, m.base["pv_done"] + e)
                        V.tensor_copy(probT[:, 0, 0:keys], ps[:, 4, 0:keys]).then_inc(m.pT_dve, 1)
                    e = n - 3
                    if 0 <= e < pairs and e % 4 == 3:
                        t, c0, group = block_of(e, heads)
                        dve.wait_ge(m.o_done, m.base["o_done"] + group + 1)
                        dve.wait_ge(m.spread_ps, m.base["spread_ps"] + group + 1)
                        out = mixed[:, c0:c0 + 4, PARTS * t:PARTS * t + PARTS]
                        V.tensor_tensor(out, out, ps[:, 7, :].rearrange("p (c n) -> p c n", c=4), ALU.mult).then_inc(m.mixed_done, 1)

            def project_out(l, t):
                m = M[l]
                for hf in range(2):
                    n = 2 * t + hf
                    dve.wait_ge(m.out_ps, m.base["out_ps"] + n + 1)
                    cols = slice(512 * hf, 512 * hf + 512)
                    V.tensor_tensor(x_res[:, t, cols], x_res[:, t, cols], ps[:, n % 4, :], ALU.add).then_inc(m.out_half, 1)
                dve.wait_ge(m.out_half, m.base["out_half"] + 2 * t + 2)
                dve.sem_inc(x_ready[2 * l + 1] if moes else x_ready[4], 1)

            def mixer0():
                m = M[0]
                zero_halves(m, idx_kT, kT0)
                dve.wait_ge(consts_in, 16)
                norm(0)
                tables(0)
                base_cos = con("rope_cos").rearrange("p (t d) -> p t d", d=HEAD)
                n_idx = (IDX_HEADS + 1) * HEAD
                for t in range(TILES):
                    dve.wait_ge(m.idx_raw_done, t + 1)
                    rot = idx_rot[:, t, :]
                    link(V.tensor_tensor(heads_of(rot[:, 0:n_idx]), heads_of(idx_raw[:, t, 0:n_idx]), on_heads(base_cos[:, t, :], IDX_HEADS + 1), ALU.mult))
                    dve.wait_ge(m.idx_sin_done, t + 1)
                    link(V.tensor_tensor(rot[:, n_idx:], rot[:, n_idx - HEAD:n_idx], idx_sin[:, IDX_HEADS, :], ALU.add))
                    link(V.tensor_tensor(heads_of(rot[:, 0:n_idx]), heads_of(rot[:, 0:n_idx]), idx_sin, ALU.add))
                    dve.sem_inc(m.idx_rot_done, 1)
                for t in range(TILES):
                    rotate(m, t, qk_raw0[:, t % 2, :], qk_sin0, qk_rot0[:, t, :], DSA_HEADS, 1)
                dve.wait_ge(m.idx_w_done, TILES)
                for t in range(1, TILES):
                    for hd in range(IDX_HEADS):
                        n = (t - 1) * IDX_HEADS + hd
                        dve.wait_ge(m.rel_done, n + 1)
                        rel = relu[:, n % 2, 0:PARTS * (t + 1)]
                        if hd == 0:
                            V.tensor_scalar(score[t], rel, idx_w[:, t, hd:hd + 1], None, ALU.mult).then_inc(m.rel_used, 1)
                        else:
                            V.scalar_tensor_tensor(score[t], rel, idx_w[:, t, hd:hd + 1], score[t], ALU.mult, ALU.add).then_inc(m.rel_used, 1)
                        dve.wait_ge(m.rel_used, n + 1)
                    own = score[t][:, PARTS * t:]
                    link(V.tensor_tensor(own, own, con("causal"), ALU.add))
                for t in range(1, TILES):
                    for _ in range(DSA_KEEP // 8):
                        link(V.max(best8[:, :], score[t]))
                        link(V.match_replace(score[t], best8[:, :], score[t], TAKEN))
                    link(V.tensor_scalar(score[t], score[t], TAKEN, -BIG, ALU.not_equal, ALU.mult))
                attention(0, DSA_HEADS, lambda t: score[t] if t else con("causal"))
                if not moes:
                    for t in range(TILES):
                        project_out(0, t)

            def mixer1():
                m = M[1]
                zero_halves(m, kT1)
                norm(2)
                tables(1)
                for t in range(TILES):
                    if t >= 2:
                        dve.wait_ge(m.qkT_ps, m.base["qkT_ps"] + 3 * (t - 1))
                    rotate(m, t, qk_raw1, heads_of(qk_sq1), qk_rot1[:, t % 2, :], DIL_HEADS, DIL_KV)
                attention(1, DIL_HEADS, lambda t: con("strip")[:, TOKENS - PARTS * (t + 1):])
                if not moes:
                    for t in range(TILES):
                        project_out(1, t)

            def moe(l):
                s = L[l]
                norm(2 * l + 1, (lambda t: project_out(l, t)) if mixers else lambda t: None)
                dve.wait_ge(s.router_in, 112)
                dve.wait_ge(s.logits_done, 1)
                link(V.tensor_tensor(logit[:, :, :], ps[:, 5, 0:TILES * N_ROUTER].rearrange("p (t n) -> p t n", t=TILES),
                                     b_router[:, :].unsqueeze(1).broadcast_to([PARTS, TILES, N_ROUTER]), ALU.add))
                lg, le = logit[:, :, 0:N_GROUPS], logit[:, :, N_GROUPS:]

                def first_of_max(values, best, index, out, work, n, iota):
                    link(V.tensor_reduce(best, values, AX, ALU.max))
                    link(V.tensor_tensor(work, values, over(best, n), ALU.is_equal))
                    link(V.scalar_tensor_tensor(work, work, -64.0, iota.unsqueeze(1).broadcast_to([PARTS, TILES, n]), ALU.mult, ALU.add))
                    link(V.tensor_reduce(index, work, AX, ALU.min))
                    link(V.tensor_tensor(out, work, over(index, n), ALU.is_equal))
                first_of_max(lg, gmax, gidx, hot4, pen4, N_GROUPS, con("iota_group"))
                V.tensor_tensor(at4, lg, over(gmax, N_GROUPS), ALU.subtract).then_inc(s.exp_in, 1)
                link(V.tensor_scalar(pen4, hot4, -1.0, BIG, ALU.add, ALU.mult))
                link(V.tensor_tensor(lm.rearrange("p t (g e) -> p t g e", g=N_GROUPS), le.rearrange("p t (g e) -> p t g e", g=N_GROUPS),
                                     pen4.unsqueeze(3).broadcast_to([PARTS, TILES, N_GROUPS, PER_GROUP]), ALU.add))
                first_of_max(lm, top[0], eid[:, 0, :], hot[0], tmp, N_EXPERTS, con("iota_expert"))
                link(V.scalar_tensor_tensor(lm, hot[0], -BIG, lm, ALU.mult, ALU.add))
                first_of_max(lm, top[1], eid[:, 1, :], hot[1], tmp, N_EXPERTS, con("iota_expert"))
                V.tensor_tensor(picked, hot[0], hot[1], ALU.add).then_inc(s.picked_done, 1)
                V.tensor_tensor(gap, top[1], top[0], ALU.subtract).then_inc(s.exp_in, 1)
                for k in range(TOP_K):
                    V.tensor_tensor(row_hot[:, :, k, :], hot[k], over(con("token"), N_EXPERTS), ALU.mult)
                dve.wait_ge(s.rank_done, 1)
                ranks = ps[:, 6, 0:TILES * N_EXPERTS].rearrange("p (t e) -> p t e", t=TILES)
                for k in range(TOP_K):
                    link(V.tensor_tensor(tmp, hot[k], ranks, ALU.mult))
                    link(V.tensor_reduce(rank[:, k, :], tmp, AX, ALU.add))

                def slot_hots():
                    for k in range(TOP_K):
                        last = V.tensor_tensor(slot_hot[:, :, k, :], con("iota_slot").unsqueeze(1).broadcast_to([PARTS, TILES, PARTS]),
                                               over(rank[:, k, :], PARTS), ALU.is_equal)
                    last.then_inc(s.hot_ready, 1)
                slot_hots()
                dve.wait_ge(s.rank_done, 2)
                link(V.tensor_reduce(tmp[:, 0, :], ps[:, 4, 0:TILES * N_EXPERTS].rearrange("p (t e) -> p e t", t=TILES), AX, ALU.add))
                link(V.tensor_reduce(cmax, tmp[:, 0, :], AX, ALU.max))
                V.tensor_copy(max_count[:, :], cmax).then_inc(s.count_done, 1)
                dve.wait_ge(s.exp_done, 2)
                link(V.tensor_reduce(p_group, exp4, AX, ALU.add))
                link(V.reciprocal(p_group, p_group))
                link(V.tensor_scalar(inv, e21, 1.0, None, ALU.add))
                link(V.reciprocal(inv, inv))
                link(V.tensor_tensor(gates[:, 0, :], p_group, inv, ALU.mult))
                link(V.tensor_tensor(gates[:, 1, :], gates[:, 0, :], e21, ALU.mult))
                for k in range(TOP_K):
                    link(V.tensor_tensor(hot[k], hot[k], over(gates[:, k, :], N_EXPERTS), ALU.mult))

                def experts(pair, i):
                    for u in range(2):
                        dve.wait_ge(s.x_transposed, 2 * pair + u + 1)
                        V.tensor_tensor(xT[u].rearrange("p (c h s) -> p c h s", h=2, s=CAP),
                                        ps[:, 0, :].rearrange("p (c h s) -> p c h s", h=2, s=CAP),
                                        gain[:, 2 * l + 1, :].rearrange("p (h c) -> p c h", h=2).unsqueeze(3).broadcast_to([PARTS, 4, 2, CAP]),
                                        ALU.mult).then_inc(s.xT_done, 1)
                        if u == 0:
                            for k, out in enumerate((gate_at, gate_at2)):
                                V.tensor_tensor(out.rearrange("p t (u s) -> p t u s", u=2), slot_hot[:, :, k, :].rearrange("p t (u s) -> p t u s", u=2),
                                                hot[k][:, :, bass.ds(2 * i, 2)].unsqueeze(3).broadcast_to([PARTS, TILES, 2, CAP]), ALU.mult).then_inc(s.gate_steps, 1)
                            dve.wait_ge(s.gate_steps, 3 * pair + 2)
                            V.tensor_tensor(gate_at, gate_at, gate_at2, ALU.add).then_inc(s.gate_steps, 1)
                        dve.wait_ge(s.silu_done, 2 * pair + u + 1)
                        dve.wait_ge(s.parts_done, 6 * pair + 2 * u + 2)
                        if u:
                            dve.wait_ge(s.h_transposed, 2 * pair + 1)
                        V.tensor_tensor(h, silu, ps[:, 2, 0:256], ALU.mult).then_inc(s.h_done, 1)

                def add(pair, wait_before=True):
                    if wait_before:
                        dve.wait_ge(s.added, 2 * TILES * pair)
                    for t in range(TILES):
                        for hf in range(2):
                            dve.wait_ge(s.added_ps, 2 * TILES * pair + 2 * t + hf + 1)
                            cols = slice(512 * hf, 512 * hf + 512)
                            V.tensor_tensor(x_res[:, t, cols], x_res[:, t, cols], ps[:, 6 + hf, :], ALU.add).then_inc(s.added, 1)

                def steps(b):
                    dve.wait_ge(s.fetch_ps, b + 1)
                    V.tensor_scalar(fetch[:, :], ps[:, 7, 0:N_EXPERTS], 2.0, con("half"), ALU.mult, ALU.add).then_inc(s.fetch_done, 1)
                    first = b * (N_EXPERTS // 2)
                    pass_one = type(b) is int
                    experts(first, 0)
                    if pass_one:
                        experts(1, 1)
                        add(0, wait_before=False)
                    with dve.Fori(2 if pass_one else 1, N_EXPERTS // 2) as i:
                        experts(first + i, i)
                        add(first + i - 1)
                    add(first + N_EXPERTS // 2 - 1)
                    dve.wait_ge(s.added, 2 * TILES * (first + N_EXPERTS // 2))
                    dve.sem_inc(s.passes_over, 1)
                steps(0)
                most = dve.value_load(max_count[0:1, 0:1], min_val=0, max_val=TOKENS)
                with dve.Fori(1, LEVELS) as b:
                    with dve.If(most > b * CAP):
                        V.tensor_scalar(rank, rank, -float(CAP), None, ALU.add).then_inc(s.rank_shifted, 1)
                        dve.wait_ge(s.rank_shifted, b)
                        dve.wait_ge(s.fetch_copied, b * N_EXPERTS)
                        slot_hots()
                        steps(b)
                for t in range(TILES):
                    dve.sem_inc(x_ready[2 * l + 2 if l != layers[-1] else 4], 1)

            for l in layers:
                if mixers:
                    (mixer0, mixer1)[l]()
                if moes:
                    moe(l)

        @block.tensor
        def _(pe):
            pe.wait_ge(consts_in, 16)

            T = nc.tensor

            def transpose_x(z, t):
                tok = token_major[z % 2][:, :].rearrange("p (t d) -> p t d", t=TILES)
                pe.wait_ge(N[z].xn_done, N[z].base["xn_done"] + t + 1)
                for g in range(2):
                    if t:
                        pe.wait_ge(N[z].xT_done, N[z].base["xT_done"] + 2 * t + g - 1)
                    for j in range(4):
                        at = 512 * g + PARTS * j
                        last = T.transpose(ps[:, 6 + g, PARTS * j:PARTS * j + PARTS], tok[:, t, at:at + PARTS], ident)
                    last.then_inc(N[z].xT_ps, 1)

            def x_by_features(z, t):
                pe.wait_ge(N[z].xT_done, N[z].base["xT_done"] + 2 * t + 2)

            def project(out, src, cols, w, lo, hi):
                for c in range(CHUNKS):
                    last = T.matmul(out, src[:, c, cols], w[:, c, lo:hi], start=c == 0, stop=c == CHUNKS - 1)
                return last

            def attention(l, heads, qT, kT, v, kv_of):
                m = M[l]
                pairs = TILES * heads // 2
                for n in range(pairs + 4):
                    if n < pairs:
                        t, pair = divmod(n, heads // 2)
                        for u in range(2):
                            if n >= 2:
                                pe.wait_ge(m.masked_done, m.base["masked_done"] + 2 * n - 3 + u)
                            T.matmul(ps[:, 2 * (n % 2) + u, 0:PARTS * (t + 1)], qT[:, pair, PARTS * t:PARTS * t + PARTS],
                                     kT[:, kv_of(2 * pair), u, 0:PARTS * (t + 1)], start=True, stop=True).then_inc(m.s_ps, 1)
                    e = n - 1
                    if 0 <= e < pairs:
                        for u in range(2):
                            pe.wait_ge(m.exp_done, m.base["exp_done"] + 2 * e + u + 1)
                            if e:
                                pe.wait_ge(m.pT_act if u else m.pT_dve, m.base["pT_act"] + e)
                            for kb in range(e * 2 // heads + 1):
                                blk = slice(PARTS * kb, PARTS * kb + PARTS)
                                last = T.transpose(ps[:, 4 + u, blk], prob[:, 2 * (e % 2) + u, blk], ident)
                            last.then_inc(m.pT_ps, 1)
                    e = n - 2
                    if 0 <= e < pairs:
                        t, pair = divmod(e, heads // 2)
                        if e % 4 == 0 and e:
                            pe.wait_ge(m.o_done, m.base["o_done"] + e // 4)
                        pe.wait_ge(m.pT_dve, m.base["pT_dve"] + e + 1)
                        pe.wait_ge(m.pT_act, m.base["pT_act"] + e + 1)
                        kv = kv_of(2 * pair)
                        for kb in range(t + 1):
                            for u in range(2):
                                last = T.matmul(ps[HEAD * u:HEAD * u + HEAD, 6, PARTS * (e % 4):PARTS * (e % 4) + PARTS],
                                                v[:, kb, HEAD * kv:HEAD * kv + HEAD], probT[:, u, PARTS * kb:PARTS * kb + PARTS], start=kb == 0, stop=kb == t)
                        last.then_inc(m.pv_done, 1)
                        if e % 4 == 3:
                            g = e // 4
                            pe.wait_ge(m.inv_done, m.base["inv_done"] + g + 1)
                            if g:
                                pe.wait_ge(m.mixed_done, m.base["mixed_done"] + g)
                            for c in range(4):
                                for u in range(2):
                                    last = T.matmul(ps[HEAD * u:HEAD * u + HEAD, 7, PARTS * c:PARTS * c + PARTS],
                                                    denom[:, g % 2, 2 * c + u:2 * c + u + 1].broadcast_to([PARTS, HEAD]), ident, start=True, stop=True)
                            last.then_inc(m.spread_ps, 1)

            def project_out(l, t):
                m = M[l]
                if t == 0:
                    pe.wait_ge(m.w_out_in, m.base["w_out_in"] + 16)
                    pe.wait_ge(m.mixed_done, m.base["mixed_done"] + TILES * (DSA_HEADS if l == 0 else DIL_HEADS) // 8)
                    if l == 0:
                        pe.wait_ge(m.conv_done, CONV // PARTS)
                for hf in range(2):
                    n = 2 * t + hf
                    if n >= 4:
                        pe.wait_ge(m.out_half, m.base["out_half"] + n - 3)
                    project(ps[:, n % 4, :], mixed, slice(PARTS * t, PARTS * t + PARTS), w_out, 512 * hf, 512 * hf + 512).then_inc(m.out_ps, 1)
                if t == TILES - 1:
                    pe.wait_ge(m.out_ps, m.base["out_ps"] + 2 * TILES)
                    pe.sem_inc(m.out_over, 1)

            def mixer0():
                m = M[0]
                hT0 = feature_major[0][:, :].rearrange("p (c n) -> p c n", c=CHUNKS)
                transpose_x(0, 0)
                for t in range(TILES):
                    if t < TILES - 1:
                        transpose_x(0, t + 1)
                    x_by_features(0, t)
                    if t == 0:
                        pe.wait_ge(m.w_in_a, 16)
                    if t >= 2:
                        pe.wait_ge(m.idx_raw_done, t - 1)
                    project(ps[:, t % 2, 0:N_IDX0], hT0, slice(PARTS * t, PARTS * t + PARTS), w_idx, 0, N_IDX0).then_inc(m.idx_ps, 1)
                pe.wait_ge(m.w_in_b, m.base["w_in_b"] + 16)
                for t in range(TILES):
                    if t >= 2:
                        pe.wait_ge(m.raw_done, m.base["raw_done"] + t - 1)
                    for hf in range(2):
                        last = project(ps[:, 2 + 2 * (t % 2) + hf, 0:N_QKV0 // 2], hT0, slice(PARTS * t, PARTS * t + PARTS), w_qkv0,
                                       hf * N_QKV0 // 2, (hf + 1) * N_QKV0 // 2)
                    last.then_inc(m.in_ps, 1)
                pe.wait_ge(m.in_ps, m.base["in_ps"] + TILES)
                pe.sem_inc(m.in_over, 1)
                for t in range(TILES):
                    pe.wait_ge(m.idx_rot_done, t + 1)
                    if t >= 2:
                        pe.wait_ge(m.idxT_done, t - 1)
                    for j in range(3):
                        last = T.transpose(ps[:, 6 + t % 2, PARTS * j:PARTS * j + PARTS], idx_rot[:, t, PARTS * j:PARTS * j + PARTS], ident)
                    last.then_inc(m.idxT_ps, 1)
                pe.wait_ge(m.zeros_done, m.base["zeros_done"] + 1)
                pe.wait_ge(m.idxT_done, TILES)
                pe.wait_ge(m.raw_done, m.base["raw_done"] + TILES)
                for t in range(1, TILES):
                    for hd in range(IDX_HEADS):
                        n = (t - 1) * IDX_HEADS + hd
                        if n >= IDX_HEADS:
                            pe.wait_ge(m.rel_done, n - IDX_HEADS + 1)
                        T.matmul(ps[:, hd, 0:PARTS * (t + 1)], idx_qT[:, hd // 2, PARTS * t:PARTS * t + PARTS], idx_kT[:, 0, hd % 2, 0:PARTS * (t + 1)],
                                 start=True, stop=True).then_inc(m.rel_ps, 1)
                for t in range(TILES):
                    pe.wait_ge(m.rot_done, m.base["rot_done"] + t + 1)
                    for g in range(2):
                        if t:
                            pe.wait_ge(m.qkT_done, m.base["qkT_done"] + 2 * t + g - 1)
                        for j in range(4 if g == 0 else 1):
                            last = T.transpose(ps[:, 6 + g, PARTS * j:PARTS * j + PARTS], qk_rot0[:, t, 512 * g + PARTS * j:512 * g + PARTS * j + PARTS], ident)
                        last.then_inc(m.qkT_ps, 1)
                pe.wait_ge(m.rel_done, 3 * IDX_HEADS)
                pe.wait_ge(m.w_in_c, m.base["w_in_c"] + 16)
                for c in range(CONV // PARTS):
                    for g, gate in enumerate((1, 2, 0)):
                        if c >= 2:
                            pe.wait_ge(m.conv_in_done, 3 * (c - 2) + g + 1)
                        lo = gate * CONV + PARTS * c
                        for k in range(CHUNKS):
                            last = T.matmul(ps[:, 3 * (c % 2) + g, :], w_conv[:, k, lo:lo + PARTS], hT0[:, k, :], start=k == 0, stop=k == CHUNKS - 1)
                        last.then_inc(m.conv_ps, 1)
                pe.wait_ge(m.conv_ps, 3 * CONV // PARTS)
                pe.sem_inc(m.conv_over, 1)
                pe.wait_ge(m.conv_in_done, 3 * CONV // PARTS)
                pe.wait_ge(m.qkT_done, m.base["qkT_done"] + 2 * TILES)
                pe.wait_ge(m.v_done, TILES)
                attention(0, DSA_HEADS, qT0, kT0, v0, lambda hd: 0)
                if not moes:
                    for t in range(TILES):
                        project_out(0, t)

            def mixer1():
                m = M[1]
                hT1 = feature_major[0][:, :].rearrange("p (c n) -> p c n", c=CHUNKS)
                transpose_x(2, 0)

                def transposes(t):
                    pe.wait_ge(m.rot_done, m.base["rot_done"] + t + 1)
                    for g in range(3):
                        if 3 * t + g >= 2:
                            pe.wait_ge(m.qkT_done, m.base["qkT_done"] + 3 * t + g - 1)
                        for j in range(4):
                            at = 512 * g + PARTS * j
                            last = T.transpose(ps[:, 6 + (3 * t + g) % 2, PARTS * j:PARTS * j + PARTS], qk_rot1[:, t % 2, at:at + PARTS], ident)
                        last.then_inc(m.qkT_ps, 1)
                for t in range(TILES):
                    if t < TILES - 1:
                        transpose_x(2, t + 1)
                    x_by_features(2, t)
                    if t >= 2:
                        pe.wait_ge(m.raw_done, m.base["raw_done"] + t - 1)
                    for g, arrived in enumerate(("w_in_a", "w_in_b", "w_in_c")):
                        if t == 0:
                            pe.wait_ge((m.w_in_a, m.w_in_b, m.w_in_c)[g], m.base[arrived] + 16)
                        hi = min(512 * g + 512, N_QK1)
                        last = project(ps[:, 3 * (t % 2) + g, 0:hi - 512 * g], hT1, slice(PARTS * t, PARTS * t + PARTS), w_in1, 512 * g, hi)
                    last.then_inc(m.in_ps, 1)
                    if t >= 2:
                        if t == 2:
                            x_by_features(2, TILES - 1)
                        transposes(t - 2)
                pe.wait_ge(m.raw_done, m.base["raw_done"] + TILES - 1)
                for t in range(TILES):
                    last = project(ps[:, t // 2, N_V1 * (t % 2):N_V1 * (t % 2 + 1)], hT1, slice(PARTS * t, PARTS * t + PARTS), w_in1, N_QK1, N_QK1 + N_V1)
                    if t == TILES // 2:
                        transposes(TILES - 2)
                last.then_inc(m.in_ps, 1)
                pe.wait_ge(m.in_ps, m.base["in_ps"] + TILES + 1)
                pe.sem_inc(m.in_over, 1)
                transposes(TILES - 1)
                pe.wait_ge(m.raw_done, m.base["raw_done"] + TILES + 1)
                pe.wait_ge(m.qkT_done, m.base["qkT_done"] + 3 * TILES)
                pe.wait_ge(m.zeros_done, m.base["zeros_done"] + 1)
                attention(1, DIL_HEADS, qT1, kT1, v1, lambda hd: hd // (DIL_HEADS // DIL_KV))
                if not moes:
                    for t in range(TILES):
                        project_out(1, t)

            def moe(l):
                s = L[l]
                z = 2 * l + 1

                def route(t):
                    if t == 0:
                        pe.wait_ge(s.router_in, 112)
                    x_by_features(z, t)
                    for c in range(CHUNKS):
                        last = T.matmul(ps[0:N_ROUTER, 4, PARTS * t:PARTS * t + PARTS], w_router[:, c, :], xnT[:, c, PARTS * t:PARTS * t + PARTS],
                                        start=c == 0, stop=c == CHUNKS - 1)
                    last.then_inc(s.logitT_ps, 1)
                if mixers:
                    project_out(l, 0)
                    project_out(l, 1)
                    project_out(l, 2)
                transpose_x(z, 0)
                if mixers:
                    project_out(l, 3)
                route(0)
                transpose_x(z, 1)
                transpose_x(z, 2)
                route(1)
                transpose_x(z, 3)
                route(2)
                route(3)
                pe.wait_ge(s.logitT_done, 1)
                for t in range(TILES):
                    last = T.transpose(ps[:, 5, N_ROUTER * t:N_ROUTER * (t + 1)], logitT[:, PARTS * t:PARTS * t + PARTS], ident[0:N_ROUTER, 0:N_ROUTER])
                last.then_inc(s.logits_done, 1)
                pe.wait_ge(s.picked_done, 1)
                both = picked.rearrange("p t e -> p (t e)")
                T.matmul(ps[:, 6, 0:TILES * N_EXPERTS], before, both, start=True, stop=False)
                for back in range(1, TILES):
                    n = (TILES - back) * N_EXPERTS
                    last = T.matmul(ps[:, 6, N_EXPERTS * back:TILES * N_EXPERTS], ones, both[:, 0:n], start=False, stop=back == TILES - 1)
                last.then_inc(s.rank_done, 1)
                T.matmul(ps[:, 4, 0:TILES * N_EXPERTS], ones, both, start=True, stop=True).then_inc(s.rank_done, 1)

                def transpose_rows(pair, u, arrived):
                    pe.wait_ge(s.xg_in[u], arrived)
                    for j in range(4):
                        last = T.transpose(ps[:, 0, PARTS * j:PARTS * j + PARTS], xg[u][:, PARTS * j:PARTS * j + PARTS], ident)
                    last.then_inc(s.x_transposed, 1)
                    pe.wait_ge(s.xT_done, 2 * pair + u + 1)

                def weights(pair, u, part):
                    q, j = ORDER.index((u, part)), 3 * u + part
                    if q < AHEAD and type(pair) is int and pair == 1:
                        pe.wait_ge(s.ahead_in[q], 16)
                        return ahead(q)
                    skipped = 1 if q < AHEAD and not (type(pair) is int and pair == 0) else 0
                    pe.wait_ge(s.weights_in[j], (pair + 1 - skipped) * 16)
                    return ring_part(j)

                def hidden(pair, u, part):
                    w = weights(pair, u, part)
                    for c in range(CHUNKS):
                        x_c = xT[u][:, PARTS * (c % 4) + CAP * (c // 4):PARTS * (c % 4) + CAP * (c // 4) + CAP]
                        for hf in range(2):
                            last = T.matmul(ps[CAP * hf:CAP * hf + CAP, 1 + part, 0:256], x_c, w[:, c, 256 * hf:256 * hf + 256],
                                            start=c == 0, stop=c == CHUNKS - 1)
                    last.then_inc(s.parts_done, 1)

                def transpose_h(pair, u):
                    pe.wait_ge(s.h_done, 2 * pair + u + 1)
                    if u:
                        pe.wait_ge(s.hT_done, 2 * pair + 1)
                    for j in range(2):
                        last = T.transpose(ps[:, 3, PARTS * j:PARTS * j + PARTS], h[:, PARTS * j:PARTS * j + PARTS], ident)
                    last.then_inc(s.h_transposed, 1)

                def gated(pair, tiles, first=False):
                    for t in tiles:
                        for hf in range(2):
                            n = 2 * t + hf
                            if not first or n >= 2:
                                pe.wait_ge(s.added, 2 * TILES * pair + n - 1)
                            T.matmul(ps[:, 6 + hf, :], gateT[:, t, :], y[:, 512 * hf:512 * hf + 512], start=True, stop=True).then_inc(s.added_ps, 1)

                def experts(pair, before=False, first=False):
                    arrived = (pair + 1) * 16
                    if type(pair) is not int or pair > 0:
                        pe.wait_ge(s.gateT_done, pair)
                    transpose_rows(pair, 0, arrived)
                    hidden(pair, 0, 0)
                    hidden(pair, 0, 1)
                    transpose_rows(pair, 1, arrived)
                    pe.wait_ge(s.silu_done, 2 * pair + 1)
                    hidden(pair, 1, 0)
                    transpose_h(pair, 0)
                    hidden(pair, 1, 1)
                    if before:
                        pe.wait_ge(s.y_evac, pair)
                        gated(pair - 1, range(0, TILES // 2), first)
                    transpose_h(pair, 1)
                    if before:
                        gated(pair - 1, range(TILES // 2, TILES), first)
                    pe.wait_ge(s.gate_steps, 3 * pair + 3)
                    for t in range(TILES):
                        last = T.transpose(ps[:, 0, PARTS * t:PARTS * t + PARTS], gate_at[:, t, :], ident)
                    last.then_inc(s.gateT_ps, 1)
                    w = [weights(pair, u, 2) for u in range(2)]
                    pe.wait_ge(s.hT_done, 2 * pair + 2)
                    for c in range(4):
                        for hf in range(2):
                            for u in range(2):
                                h_c = hT[u][:, PARTS * (c % 2) + CAP * (c // 2):PARTS * (c % 2) + CAP * (c // 2) + CAP]
                                last = T.matmul(ps[CAP * u:CAP * u + CAP, 4 + hf, :], h_c, w[u][:, c, 512 * hf:512 * hf + 512],
                                                start=c == 0, stop=c == 3)
                                if c == 3 and hf == 1:
                                    last.then_inc(s.parts_done, 1)

                def steps(b):
                    pe.wait_ge(s.hot_ready, b + 1)
                    for t in range(TILES):
                        for k in range(TOP_K):
                            last = T.matmul(ps[:, 7, 0:N_EXPERTS], slot_hot[:, t, k, :], row_hot[:, t, k, :],
                                            start=t + k == 0, stop=t + k == TILES + TOP_K - 2)
                    last.then_inc(s.fetch_ps, 1)
                    first = b * (N_EXPERTS // 2)
                    pass_one = type(b) is int
                    experts(first)
                    if pass_one:
                        experts(1, before=True, first=True)
                    with pe.Fori(2 if pass_one else 1, N_EXPERTS // 2) as i:
                        experts(first + i, before=True)
                    pe.wait_ge(s.y_evac, first + N_EXPERTS // 2)
                    gated(first + N_EXPERTS // 2 - 1, range(TILES))
                steps(0)
                pe.wait_ge(s.count_done, 1)
                most = pe.value_load(max_count[0:1, 0:1], min_val=0, max_val=TOKENS)
                with pe.Fori(1, LEVELS) as b:
                    with pe.If(most > b * CAP):
                        steps(b)
            for l in layers:
                if mixers:
                    (mixer0, mixer1)[l]()
                if moes:
                    moe(l)


_SHARED = ["x"]
_BY_LAYER = ["attn_norm", "w_in", "q_norm", "k_norm", "w_out", "ffn_norm", "w_rg", "b_rg", "w_re", "b_re", "w_gate", "w_up", "w_down"]
_INS = _SHARED + ["conv_w_0"] + [f"{n}_{l}" for l in range(2) for n in _BY_LAYER]


def kernel(**inputs):
    import numpy as _np
    import concourse.bacc as _bacc
    from concourse import mybir as _mybir
    from concourse.bass_utils import run_bass_kernel_spmd as _run

    nc = _bacc.Bacc("TRN2", target_bir_lowering=False, num_devices=1)
    arrays, aps = {}, {}
    for name in _INS + ["consts"]:
        a = constant_table() if name == "consts" else _np.ascontiguousarray(inputs[name])
        if name == "x":
            a = a.reshape(TOKENS, D_MODEL)
        arrays[f"in_{name}_dram"] = a
        aps[name] = nc.dram_tensor(f"in_{name}_dram", a.shape, _mybir.dt.from_np(a.dtype), kind="ExternalInput").ap()
    aps["out"] = nc.dram_tensor("out_0_dram", (TOKENS, D_MODEL), _mybir.dt.float32, kind="ExternalOutput").ap()
    trunk(nc, aps)
    r = _run(nc, [arrays], core_ids=[0])
    return r.results[0]["out_0_dram"].reshape(1, TOKENS, D_MODEL)
```

```python
import concourse.bass as bass
from concourse import mybir
from contextlib import ExitStack

TOKENS, D_MODEL, PARTS = 512, 1024, 128
TILES = TOKENS // PARTS
CHUNKS = D_MODEL // PARTS
N_GROUPS, PER_GROUP = 4, 8
N_EXPERTS = N_GROUPS * PER_GROUP
N_ROUTER = N_GROUPS + N_EXPERTS
HEAD = 64
HALF = HEAD // 2
ROPE_THETA = 10000.0
CONV = 512
TAPS = 3
N_CONV_COLS = 3 * CONV
DSA_HEADS, IDX_HEADS, DSA_KEEP = 8, 4, 128
N_QKV0 = (DSA_HEADS + 2) * HEAD
N_IDX0 = (IDX_HEADS + 1) * HEAD + IDX_HEADS
DIL_HEADS, DIL_KV = 16, 4
PATTERNS = ((128, 1), (512, 4), (2048, 16))
N_QK1 = (DIL_HEADS + DIL_KV) * HEAD
N_V1 = DIL_KV * HEAD
SCALE = HEAD ** -0.5
D_EXPERT = 512
TOP_K = 2
CAP = 64
AHEAD = 3
ORDER = ((0, 0), (0, 1), (1, 0), (1, 1), (0, 2), (1, 2))
LEVELS = TOKENS // CAP
NORM_EPS = 1e-6
BIG = 1e30
TAKEN = -3e38

CONST_WIDTHS = dict(ident=128, ones=128, before=128, iota_slot=128, iota_expert=32, iota_group=4,
                    row=1, tile_row=4, half=1, eps_pow=2,
                    rope_cos=256, rope_sin=256, causal=128, strip=512)
CONST_AT, _at = {}, 0
for _name, _width in CONST_WIDTHS.items():
    CONST_AT[_name] = (_at, _at + _width)
    _at += _width
N_CONST = _at
N_CONST_0 = CONST_AT["strip"][0]


def constant_table():
    import numpy as np
    p = np.arange(PARTS)
    table = np.zeros((PARTS, N_CONST), np.float32)

    def put(name, value):
        a, b = CONST_AT[name]
        table[:, a:b] = value
    put("ident", np.eye(PARTS))
    put("ones", 1.0)
    put("before", p[:, None] < p[None, :])
    put("iota_slot", np.arange(PARTS)[None] % CAP)
    put("iota_expert", np.arange(N_EXPERTS)[None])
    put("iota_group", np.arange(N_GROUPS)[None])
    put("row", 2 * p[:, None])
    put("tile_row", 2 * PARTS * np.arange(TILES)[None])
    put("half", (p >= CAP)[:, None])
    angle = np.arange(TOKENS)[:, None].astype(np.float32) * (ROPE_THETA ** (-np.arange(HALF, dtype=np.float32) / HALF)).astype(np.float32)
    by_tile = lambda v: v.reshape(TILES, PARTS, HEAD).transpose(1, 0, 2).reshape(PARTS, -1)
    put("rope_cos", by_tile(np.concatenate([np.cos(angle), np.cos(angle)], 1)))
    put("rope_sin", by_tile(np.concatenate([-np.sin(angle), np.sin(angle)], 1)))
    back = p[:, None] + (TOKENS - PARTS) - np.arange(TOKENS)[None]
    seen = sum(((back >= 0) & (back <= w) & (back % d == 0)).astype(int) for w, d in PATTERNS)
    put("strip", np.where(seen > 0, np.log(np.maximum(seen, 1)) / SCALE, -BIG))
    put("causal", np.where(p[None, :] <= p[:, None], 0.0, -BIG))
    put("eps_pow", [[NORM_EPS, -0.5]])
    return table


def trunk(nc, a):
    f32, i32, bf16 = mybir.dt.float32, mybir.dt.int32, mybir.dt.bfloat16
    ALU, ACT, AX = mybir.AluOpType, mybir.ActivationFunctionType, mybir.AxisListType.X
    ctx = ExitStack()
    with ctx:
        def sb(name, shape, dt=f32):
            return ctx.enter_context(nc.sbuf_tensor(name, shape, dt))

        def sem(name):
            return ctx.enter_context(nc.semaphore(name))

        ring = sb("ring", [PARTS, 6, 4096])
        x_res = sb("x_res", [PARTS, TILES, D_MODEL])
        buf1 = sb("buf1", [PARTS, 4096])
        buf2 = sb("buf2", [PARTS, 4096])
        const = sb("const", [PARTS, N_CONST])
        w_router = sb("w_router", [PARTS, CHUNKS, N_ROUTER])
        b_router = sb("b_router", [PARTS, N_ROUTER])
        gain = sb("gain", [PARTS, 4, CHUNKS])
        gain_of4 = sb("gain_of4", [PARTS, 2, CHUNKS])
        order = sb("order", [PARTS, 2, PARTS], bf16)
        w_mix = sb("w_mix", [PARTS, 12288])
        head_gain = sb("head_gain", [PARTS, 4, HEAD])
        rope = sb("rope", [PARTS, 4, TILES, HEAD])
        logitT = rope[:, :, :, :].rearrange("p a t d -> p (a t d)")[0:N_ROUTER, 0:TOKENS]
        conv_w = sb("conv_w", [PARTS, CONV // PARTS, TAPS])
        idx_w = sb("idx_w", [PARTS, TILES, IDX_HEADS])
        best8 = sb("best8", [PARTS, 8])
        neg_max = sb("neg_max", [PARTS, 4])
        denom = sb("denom", [PARTS, 2, 8])
        head_ss = sb("head_ss", [PARTS, 2, DIL_HEADS + DIL_KV])
        sumsq = sb("sumsq", [PARTS, TILES])
        gates = sb("gates", [PARTS, TOP_K, TILES])
        fetch = sb("fetch", [PARTS, N_EXPERTS], i32)
        fetch_now = sb("fetch_now", [PARTS, 2], i32)
        max_count = sb("max_count", [PARTS, 1], i32)
        ps = ctx.enter_context(nc.psum_tensor("ps", [PARTS, 8, 512], f32))
        xn_dram = nc.dram_tensor("xn_dram", (TOKENS, D_MODEL), f32, kind="Internal").ap()

        def con(name):
            lo, hi = CONST_AT[name]
            return const[:, lo:hi]

        ident = con("ident")
        ones, before = order[:, 0, :], order[:, 1, :]

        xn = buf1[:, :].rearrange("p (t d) -> p t d", t=TILES)
        xnT = buf2[:, :].rearrange("p (c n) -> p c n", c=CHUNKS)
        xg = [buf1[:, 512 * u:512 * u + 512] for u in range(2)]
        xT = [buf1[:, 1024 + 512 * u:1536 + 512 * u] for u in range(2)]
        y = buf1[:, 2048:3072]
        silu = buf1[:, 3072:3328]
        h = buf1[:, 3328:3584]
        hT = [buf1[:, 3584 + 256 * u:3840 + 256 * u] for u in range(2)]

        def b2(at, *dims):
            n = 1
            for d in dims:
                n *= d
            v = buf2[:, at:at + n]
            if len(dims) == 1:
                return v
            if len(dims) == 2:
                return v.rearrange("p (a b) -> p a b", a=dims[0])
            return v.rearrange("p (a b c) -> p a b c", a=dims[0], b=dims[1])
        slot_hot = b2(0, 512).bitcast(bf16).rearrange("p (t k s) -> p t k s", t=TILES, k=TOP_K)
        row_hot = b2(2304, 256).bitcast(bf16).rearrange("p (t k e) -> p t k e", t=TILES, k=TOP_K)
        gate_at = b2(3072, TILES, PARTS)
        gate_at2 = rope[:, :, :, :].rearrange("p a t d -> p (a t d)")[:, 512:1024].rearrange("p (t s) -> p t s", t=TILES)
        gateT = b2(3584, TILES, PARTS)
        hot = [b2(1280, TILES, N_EXPERTS), b2(1408, TILES, N_EXPERTS)]
        picked = b2(1536, 64).bitcast(bf16).rearrange("p (t e) -> p t e", t=TILES)
        logit = b2(1664, TILES, N_ROUTER)
        lm = b2(1808, TILES, N_EXPERTS)
        tmp = b2(1936, TILES, N_EXPERTS)
        at4 = b2(2064, TILES, N_GROUPS)
        hot4 = b2(2080, TILES, N_GROUPS)
        exp4 = b2(2096, TILES, N_GROUPS)
        pen4 = b2(2112, TILES, N_GROUPS)
        gmax = b2(2128, TILES)
        gidx = b2(2132, TILES)
        top = [b2(2136, TILES), b2(2140, TILES)]
        eid = b2(2144, TOP_K, TILES)
        rank = b2(2152, TOP_K, TILES)
        row_of = b2(2208, N_EXPERTS)
        gap = b2(2176, TILES)
        e21 = b2(2180, TILES)
        inv = b2(2184, TILES)
        p_group = b2(2188, TILES)
        cmax = b2(2192, 1)

        token_major = [buf2, buf1]
        feature_major = [buf1, buf2]
        mixed = buf2[:, :].rearrange("p (c n) -> p c n", c=CHUNKS)
        scratch = ring[:, 3:6, :].rearrange("p j n -> p (j n)")
        w_conv = ring[:, 0:3, :].rearrange("p j n -> p (j n)").rearrange("p (c n) -> p c n", c=CHUNKS)

        def part(buf, at, *dims):
            n = 1
            for d in dims:
                n *= d
            v = buf[:, at:at + n]
            if len(dims) == 2:
                v = v.rearrange("p (a b) -> p a b", a=dims[0])
            if len(dims) == 3:
                v = v.rearrange("p (a b c) -> p a b c", a=dims[0], b=dims[1])
            return v

        qT0 = part(scratch, 0, DSA_HEADS // 2, TOKENS)
        kT0 = part(scratch, 10640, 1, 2, TOKENS)
        idx_qT = part(scratch, 2048, IDX_HEADS // 2, TOKENS)
        idx_kT = part(scratch, 3072, 1, 2, TOKENS)
        v0 = part(scratch, 4096, TILES, HEAD)
        score = [None] + [part(scratch, at, n) for at, n in ((4352, 256), (4608, 384), (4992, 512))]
        relu = part(scratch, 5504, 2, TOKENS)
        idx_raw = part(scratch, 6528, TILES, N_IDX0)
        idx_sin = part(scratch, 7824, IDX_HEADS + 1, HEAD)
        qk_raw0 = part(scratch, 8144, 2, N_QKV0)
        qk_sq0 = part(scratch, 9424, N_QKV0)
        qk_sin0 = part(scratch, 10064, DSA_HEADS + 1, HEAD)
        conv_in = part(scratch, 6528, 3, TOKENS)
        conv_u = part(scratch, 8064, TOKENS + TAPS - 1)
        conv_y = part(scratch, 8578, 2, TOKENS)
        idx_rot = part(buf2, 0, TILES, 3 * PARTS)
        qk_rot0 = part(buf2, 1536, TILES, 5 * PARTS)
        w_idx = part(w_mix, 0, CHUNKS, N_IDX0)
        w_qkv0 = part(w_mix, CHUNKS * N_IDX0, CHUNKS, N_QKV0)
        gain_rows = part(scratch, 11664, PARTS)[0:4 * CHUNKS, :]
        qT1 = part(scratch, 0, DIL_HEADS // 2, TOKENS)
        kT1 = part(scratch, 4096, DIL_KV, 2, TOKENS)
        v1 = part(scratch, 8192, TILES, N_V1)
        qk_raw1 = [part(scratch, 9216, N_QK1), ring[:, 2, 0:N_QK1]]
        qk_sq1 = [part(scratch, 10496, N_QK1), ring[:, 2, N_QK1:2 * N_QK1]]
        qk_rot1 = part(buf2, 0, 2, DIL_HEADS * HEAD + 2 * DIL_KV * HEAD)
        w_in1 = part(w_mix, 0, CHUNKS, N_QK1 + N_V1)
        w_out = part(w_mix, 0, CHUNKS, D_MODEL)
        prob = part(buf1, 0, 4, TOKENS)
        probT = part(buf1, 2048, 2, TOKENS)

        consts_in = sem("consts_in")
        out_stored = sem("out_stored")
        dve_chain = sem("dve_chain")
        pool_chain = sem("pool_chain")
        x_in = [sem(f"x_in{t}") for t in range(TILES)]
        x_ready = [sem(f"x_ready{i}") for i in range(5)]

        params_in = sem("params_in")
        gain_ps = sem("gain_ps")
        def signals(kind, by_name):
            return type(kind, (), by_name)()

        N = []
        shared = {n: sem(n) for n in "ss_done rstd_done xn_done xT_ps xT_done".split()}
        for z in range(4):
            s = signals("NormSignals", shared)
            s.base = {n: z * (2 * TILES if n[:2] == "xT" else TILES) for n in shared}
            N.append(s)
        pairs0, groups0 = TILES * DSA_HEADS // 2, TILES * DSA_HEADS // 8
        mixer0_counts = dict(w_in_a=16, w_in_b=16, w_in_c=16, w_out_in=16, head_gain_in=96, in_ps=TILES, raw_done=TILES, sq_done=TILES,
                             head_ss_done=TILES, head_rstd_done=TILES, normed=TILES, sin_done=TILES, rot_done=TILES, qkT_ps=2 * TILES,
                             qkT_done=2 * TILES, in_over=1, out_over=1, zeros_done=1, tables_done=1, s_ps=2 * pairs0, masked_done=2 * pairs0,
                             exp_done=2 * pairs0, pT_ps=2 * pairs0, pT_dve=pairs0, pT_act=pairs0, pv_done=pairs0,
                             inv_done=groups0, spread_ps=groups0, o_done=groups0, mixed_done=groups0,
                             out_ps=2 * TILES, out_half=2 * TILES)
        shared = {n: sem(n) for n in mixer0_counts}
        M = []
        for l in range(2):
            only = ("v_done idx_ps idx_raw_done idx_sin_done idx_rot_done idxT_ps idxT_done "
                    "rel_ps rel_done rel_used idx_w_done conv_w_in conv_ps conv_in_done conv_done conv_over") if l == 0 else ""
            s = signals("MixerSignals", {**shared, **{n: sem(n) for n in only.split()}})
            s.base = {n: count * l for n, count in mixer0_counts.items()}
            M.append(s)
        L = []
        for l in range(2):
            s = signals("ExpertSignals", {n: sem(f"{n}_{l}") for n in ("router_in xn_stored logitT_ps logitT_done logits_done exp_in exp_done "
                      "picked_done rank_done hot_ready fetch_ps fetch_done count_done fetch_copied pool_turn rank_shifted "
                      "x_transposed xT_done parts_done silu_done h_done h_transposed hT_done y_evac "
                      "y_half_ps gate_steps gateT_ps gateT_done added_ps added passes_over").split()})
            s.weights_in = [sem(f"weights_in{j}_{l}") for j in range(6)]
            s.ahead_in = [sem(f"ahead_in{q}_{l}") for q in range(AHEAD)]
            s.xg_in = [sem(f"xg_in{u}_{l}") for u in range(2)]
            L.append(s)

        def expert_weights(l, e):
            halves = [a[f"{name}_{l}"][e].rearrange("(h p j) n -> p h (j n)", h=2, p=PARTS) for name in ("w_gate", "w_up")]
            return halves + [a[f"w_down_{l}"][e].rearrange("(c p) n -> p c n", p=PARTS)]

        def in_runs(part, j):
            return part if j % 3 == 2 else part.rearrange("p (h j) n -> p h (j n)", h=2)

        def ring_part(j):
            n = D_EXPERT if j % 3 < 2 else D_MODEL
            return ring[:, j, :].rearrange("p (c n) -> p c n", n=n)

        def ahead(q):
            return w_mix[:, 4096 * q:4096 * (q + 1)].rearrange("p (c n) -> p c n", n=D_EXPERT)

        def conv_bank(c, g):
            return (4 + 3 * c + g) % 6

        def block_of(pair, heads):
            t = pair * 2 // heads
            group = pair // 4
            return t, CHUNKS - heads // 2 + 4 * (group % (heads // 8)), group

        block = ctx.enter_context(nc.Block())

        @block.sync
        def _(sp):
            for t in range(TILES):
                sp.dma_start(x_res[:, t, :], a["x"][PARTS * t:PARTS * t + PARTS, :]).then_inc(x_in[t], 16)
                if t == 0:
                    sp.dma_start(const[:, 0:N_CONST_0], a["consts"][:, 0:N_CONST_0]).then_inc(consts_in, 16)
                    for z, name in enumerate(("attn_norm_0", "ffn_norm_0", "attn_norm_1", "ffn_norm_1")):
                        sp.dma_start(gain_rows[CHUNKS * z:CHUNKS * (z + 1), :], a[name].rearrange("(c p) -> c p", p=PARTS)).then_inc(params_in, 16)
                    sp.dma_start(w_idx, a["w_in_0"].rearrange("(c p) n -> p c n", p=PARTS)[:, :, N_CONV_COLS + N_QKV0:]).then_inc(M[0].w_in_a, 16)

            def head_gains(l):
                for j, name in enumerate((f"q_norm_{l}", f"k_norm_{l}")):
                    row = a[name].rearrange("(o d) -> o d", o=1)
                    sp.dma_start(head_gain[:, 2 * j, :], row.broadcast_to([PARTS, HEAD])).then_inc(M[l].head_gain_in, 16)
                    sp.dma_start(head_gain[:, 2 * j + 1, 0:HALF], row[:, HALF:].broadcast_to([PARTS, HALF])).then_inc(M[l].head_gain_in, 16)
                    sp.dma_start(head_gain[:, 2 * j + 1, HALF:], row[:, 0:HALF].broadcast_to([PARTS, HALF])).then_inc(M[l].head_gain_in, 16)

            def load_w_out(l):
                sp.dma_start(w_out, a[f"w_out_{l}"].rearrange("(c p) n -> p c n", p=PARTS)).then_inc(M[l].w_out_in, 16)

            def load_pair(l, i):
                both = [expert_weights(l, 2 * i + u) for u in range(2)]
                for q, (u, j) in enumerate(ORDER):
                    yield q, 3 * u + j, both[u][j]

            def moe(l):
                s = L[l]
                sp.dma_start(w_router[:, :, 0:N_GROUPS], a[f"w_rg_{l}"].rearrange("(c p) g -> p c g", p=PARTS)).then_inc(s.router_in, 16)
                for g in range(N_GROUPS):
                    sp.dma_start(w_router[:, :, N_GROUPS + g * PER_GROUP:N_GROUPS + (g + 1) * PER_GROUP],
                                 a[f"w_re_{l}"][g].rearrange("(c p) e -> p c e", p=PARTS)).then_inc(s.router_in, 16)
                sp.dma_start(b_router[:, 0:N_GROUPS], a[f"b_rg_{l}"].rearrange("(o g) -> o g", o=1).broadcast_to([PARTS, N_GROUPS])).then_inc(s.router_in, 16)
                sp.dma_start(b_router[:, N_GROUPS:], a[f"b_re_{l}"].rearrange("(o g) e -> o (g e)", o=1).broadcast_to([PARTS, N_EXPERTS])).then_inc(s.router_in, 16)
                sp.dma_start(gain_of4[:, l, :].rearrange("p (h j) -> p h j", h=2), a[f"ffn_norm_{l}"].rearrange("(h p j) -> p h j", h=2, p=PARTS)).then_inc(s.router_in, 16)
                for q, j, src in load_pair(l, 0):
                    if j == 3:
                        sp.wait_ge(M[l].pv_done, M[l].base["pv_done"] + TILES * (DSA_HEADS if l == 0 else DIL_HEADS) // 2)
                        if l == 0:
                            sp.wait_ge(M[0].conv_done, CONV // PARTS)
                    if j == 2 and l == 1:
                        sp.wait_ge(M[1].rot_done, M[1].base["rot_done"] + TILES)
                    sp.dma_start(in_runs(ring_part(j), j), src).then_inc(s.weights_in[j], 16)
                for t in range(TILES):
                    sp.wait_ge(N[2 * l + 1].xn_done, N[2 * l + 1].base["xn_done"] + t + 1)
                    sp.dma_start(xn_dram[PARTS * t:PARTS * t + PARTS, :], xn[:, t, :]).then_inc(s.xn_stored, 16)

                sp.wait_ge(M[l].out_over, M[l].base["out_over"] + 1)
                for q, j, src in list(load_pair(l, 1))[:AHEAD]:
                    sp.dma_start(in_runs(ahead(q), j), src).then_inc(s.ahead_in[q], 16)

                def steps(first, b):
                    with sp.Fori(first, N_EXPERTS // 2) as i:
                        for q, j, src in load_pair(l, i):
                            sp.wait_ge(s.parts_done, (b * (N_EXPERTS // 2) + i - 1) * 6 + q + 1)
                            sp.dma_start(in_runs(ring_part(j), j), src).then_inc(s.weights_in[j], 16)
                for i, some in ((2, slice(0, AHEAD)), (1, slice(AHEAD, None)), (2, slice(AHEAD, None))):
                    for q, j, src in list(load_pair(l, i))[some]:
                        sp.wait_ge(s.parts_done, q + 1 if q < AHEAD else 6 * (i - 1) + q + 1)
                        sp.dma_start(in_runs(ring_part(j), j), src).then_inc(s.weights_in[j], 16)
                steps(3, 0)
                if l == 0:
                    load_w_in1()
                    head_gains(1)
                sp.wait_ge(s.count_done, 1)
                most = sp.value_load(max_count[0:1, 0:1], min_val=0, max_val=TOKENS)
                with sp.If(most > CAP):
                    with sp.Fori(1, LEVELS) as b:
                        with sp.If(most > b * CAP):
                            steps(0, b)

            def load_w_in1():
                for g, arrived in enumerate((M[1].w_in_a, M[1].w_in_b, M[1].w_in_c)):
                    cols = slice(512 * g, 512 * g + 512)
                    sp.dma_start(w_in1[:, :, cols], a["w_in_1"].rearrange("(c p) n -> p c n", p=PARTS)[:, :, cols]).then_inc(arrived, 16)

            def mixer0():
                w = a["w_in_0"].rearrange("(c p) n -> p c n", p=PARTS)
                sp.dma_start(w_qkv0, w[:, :, N_CONV_COLS:N_CONV_COLS + N_QKV0]).then_inc(M[0].w_in_b, 16)
                head_gains(0)
                sp.dma_start(conv_w[:, :, :], a["conv_w_0"].rearrange("(c p) j -> p c j", p=PARTS)).then_inc(M[0].conv_w_in, 16)
                sp.dma_start(const[:, N_CONST_0:], a["consts"][:, N_CONST_0:]).then_inc(M[0].conv_w_in, 16)
                sp.dma_start(w_conv, w[:, :, 0:N_CONV_COLS]).then_inc(M[0].w_in_c, 16)
                sp.wait_ge(M[0].in_over, M[0].base["in_over"] + 1)
                load_w_out(0)
                sp.wait_ge(M[0].conv_over, 1)

            def mixer1():
                sp.wait_ge(M[1].in_over, M[1].base["in_over"] + 1)
                load_w_out(1)

            mixer0()
            moe(0)
            mixer1()
            moe(1)
            for t in range(TILES):
                sp.wait_ge(x_ready[4], t + 1)
                sp.dma_start(a["out"][PARTS * t:PARTS * t + PARTS, :], x_res[:, t, :]).then_inc(out_stored, 16)
            sp.wait_ge(out_stored, 16 * TILES)

        @block.gpsimd
        def _(pool):
            chain = [0]

            def link(ins):
                chain[0] += 1
                ins.then_inc(pool_chain, 1)
                pool.wait_ge(pool_chain, chain[0])

            G = nc.gpsimd
            pool.wait_ge(consts_in, 16)

            def root(value, width, done, n):
                link(G.tensor_scalar(value, value, 1.0 / width, NORM_EPS, ALU.mult, ALU.add))
                G.tensor_tensor(value, value, con("eps_pow")[:, 1:2].broadcast_to([PARTS, n]), ALU.pow).then_inc(done, 1)

            def norm(z):
                for t in range(TILES):
                    pool.wait_ge(N[z].ss_done, N[z].base["ss_done"] + t + 1)
                    root(sumsq[:, t:t + 1], D_MODEL, N[z].rstd_done, 1)

            def head_norm(l, t, heads):
                pool.wait_ge(M[l].head_ss_done, M[l].base["head_ss_done"] + t + 1)
                root(head_ss[:, t % 2, 0:heads], HEAD, M[l].head_rstd_done, heads)

            def sine_terms(out, raw, sin):
                heads = out.shape[1]
                G.tensor_tensor(out[:, :, 0:HALF], raw[:, :, HALF:], sin[:, 0:HALF].unsqueeze(1).broadcast_to([PARTS, heads, HALF]), ALU.mult)
                return G.tensor_tensor(out[:, :, HALF:], raw[:, :, 0:HALF], sin[:, HALF:].unsqueeze(1).broadcast_to([PARTS, heads, HALF]), ALU.mult)

            def heads_of(v):
                return v.rearrange("p (h d) -> p h d", d=HEAD)

            def mixer0():
                m = M[0]
                norm(0)
                base_sin = con("rope_sin").rearrange("p (t d) -> p t d", d=HEAD)
                for t in range(TILES):
                    pool.wait_ge(m.idx_raw_done, t + 1)
                    if t:
                        pool.wait_ge(m.idx_rot_done, t)
                    sine_terms(idx_sin, heads_of(idx_raw[:, t, 0:(IDX_HEADS + 1) * HEAD]), base_sin[:, t, :]).then_inc(m.idx_sin_done, 1)
                    G.tensor_scalar(idx_w[:, t, :], idx_raw[:, t, (IDX_HEADS + 1) * HEAD:], IDX_HEADS ** -0.5, None, ALU.mult).then_inc(m.idx_w_done, 1)
                pool.wait_ge(m.tables_done, m.base["tables_done"] + 1)
                for t in range(TILES):
                    raw = qk_raw0[:, t % 2, :]
                    pool.wait_ge(m.raw_done, m.base["raw_done"] + t + 1)
                    G.tensor_copy(v0[:, t, :], raw[:, (DSA_HEADS + 1) * HEAD:]).then_inc(m.v_done, 1)
                    head_norm(0, t, DSA_HEADS + 1)
                    pool.wait_ge(m.normed, m.base["normed"] + t + 1)
                    if t:
                        pool.wait_ge(m.rot_done, m.base["rot_done"] + t)
                    sine_terms(qk_sin0[:, 0:DSA_HEADS, :], heads_of(raw[:, 0:DSA_HEADS * HEAD]), rope[:, 1, t, :])
                    sine_terms(qk_sin0[:, DSA_HEADS:, :], heads_of(raw[:, DSA_HEADS * HEAD:(DSA_HEADS + 1) * HEAD]), rope[:, 3, t, :]).then_inc(m.sin_done, 1)
                pool.wait_ge(m.qkT_ps, m.base["qkT_ps"] + 2 * TILES)
                link(G.memset(conv_u[:, 0:TAPS - 1], 0.0))
                pool.wait_ge(m.conv_w_in, 32)
                for c in range(CONV // PARTS):
                    pool.wait_ge(m.conv_in_done, 3 * c + 2)
                    u = conv_u[:, TAPS - 1:]
                    link(G.tensor_tensor(u, conv_in[:, 0, :], conv_in[:, 1, :], ALU.mult))
                    link(G.tensor_scalar(conv_y[:, 0, :], conv_u[:, 0:TOKENS], conv_w[:, c, 0:1], None, ALU.mult))
                    for j in range(1, TAPS):
                        link(G.tensor_scalar(conv_y[:, 1, :], conv_u[:, j:j + TOKENS], conv_w[:, c, j:j + 1], None, ALU.mult))
                        link(G.tensor_tensor(conv_y[:, 0, :], conv_y[:, 0, :], conv_y[:, 1, :], ALU.add))
                    pool.wait_ge(m.conv_in_done, 3 * c + 3)
                    G.tensor_tensor(mixed[:, c, :], conv_y[:, 0, :], conv_in[:, 2, :], ALU.mult).then_inc(m.conv_done, 1)

            def mixer1():
                m = M[1]
                norm(2)
                pool.wait_ge(m.tables_done, m.base["tables_done"] + 1)
                nq = DIL_HEADS * HEAD
                for t in range(TILES):
                    raw, sin_terms = qk_raw1[t % 2], heads_of(qk_sq1[t % 2])
                    head_norm(1, t, DIL_HEADS + DIL_KV)
                    pool.wait_ge(m.normed, m.base["normed"] + t + 1)
                    sine_terms(sin_terms[:, 0:DIL_HEADS, :], heads_of(raw[:, 0:nq]), rope[:, 1, t, :])
                    sine_terms(sin_terms[:, DIL_HEADS:, :], heads_of(raw[:, nq:]), rope[:, 3, t, :]).then_inc(m.sin_done, 1)

            def moe(l):
                s = L[l]
                norm(2 * l + 1)
                pool.wait_ge(s.xn_stored, 16 * TILES)

                def gather(b, i, u):
                    nc.gpsimd.tensor_copy(fetch_now[:, u:u + 1], fetch[:, bass.ds(2 * i + u, 1)]).then_inc(s.fetch_copied, 1)
                    pool.wait_ge(s.fetch_copied, b * N_EXPERTS + 2 * i + u + 1)
                    pool.sem_inc(s.pool_turn, 1)
                    pool.indirect_dma_start(out=xg[u], out_offset=None, in_=xn_dram.rearrange("t (h d) -> (t h) d", h=2),
                                            in_offset=bass.IndirectOffsetOnAxis(ap=fetch_now[:, u:u + 1], axis=0)).then_inc(s.xg_in[u], 16)

                def steps(b):
                    pool.wait_ge(s.fetch_done, 2 * b + 2)
                    pool.sem_inc(s.pool_turn, 1)
                    for u in range(2):
                        gather(b, 0, u)
                    with pool.Fori(0, N_EXPERTS // 2 - 1) as i:
                        for u in range(2):
                            pool.wait_ge(s.x_transposed, b * N_EXPERTS + 2 * i + u + 1)
                            gather(b, i + 1, u)
                steps(0)
                pool.wait_ge(s.count_done, 1)
                most = pool.value_load(max_count[0:1, 0:1], min_val=0, max_val=TOKENS)
                with pool.If(most > CAP):
                    with pool.Fori(1, LEVELS) as b:
                        with pool.If(most > b * CAP):
                            steps(b)
            mixer0()
            moe(0)
            mixer1()
            moe(1)

        @block.scalar
        def _(act):
            A = nc.scalar

            def norm(z):
                tok = token_major[z % 2][:, :].rearrange("p (t d) -> p t d", t=TILES)
                for t in range(TILES):
                    if z == 0:
                        act.wait_ge(x_in[t], 16)
                    else:
                        act.wait_ge(x_ready[z], t + 1)
                    A.activation(tok[:, t, :], x_res[:, t, :], ACT.Square, accum_out=sumsq[:, t:t + 1]).then_inc(N[z].ss_done, 1)

            def attention(l, heads):
                m = M[l]
                pairs = TILES * heads // 2
                for n in range(pairs + 4):
                    if n < pairs:
                        t, group = n * 2 // heads, n // 4
                        keys = PARTS * (t + 1)
                        if n % 4 == 0 and group >= 2:
                            act.wait_ge(m.spread_ps, m.base["spread_ps"] + group - 1)
                        for u in range(2):
                            b = 2 * (n % 2) + u
                            act.wait_ge(m.masked_done, m.base["masked_done"] + 2 * n + u + 1)
                            A.activation(prob[:, b, 0:keys], prob[:, b, 0:keys], ACT.Exp, bias=neg_max[:, b:b + 1], scale=-1.0,
                                         accum_out=denom[:, group % 2, 2 * (n % 4) + u:2 * (n % 4) + u + 1]).then_inc(m.exp_done, 1)
                    e = n - 1
                    if 0 <= e < pairs:
                        keys = PARTS * (e * 2 // heads + 1)
                        act.wait_ge(m.pT_ps, m.base["pT_ps"] + 2 * e + 2)
                        if e:
                            act.wait_ge(m.pv_done, m.base["pv_done"] + e)
                        A.activation(probT[:, 1, 0:keys], ps[:, 5, 0:keys], ACT.Copy).then_inc(m.pT_act, 1)
                    e = n - 2
                    if 0 <= e < pairs and e % 4 == 3:
                        t, c0, group = block_of(e, heads)
                        act.wait_ge(m.pv_done, m.base["pv_done"] + e + 1)
                        A.activation(mixed[:, c0:c0 + 4, PARTS * t:PARTS * t + PARTS], ps[:, 6, :].rearrange("p (c n) -> p c n", c=4), ACT.Copy).then_inc(m.o_done, 1)

            def keys_out(kT, t, src):
                src = src.rearrange("p (c n) -> p c n", n=PARTS)
                cols = slice(PARTS * t, PARTS * t + PARTS)
                A.activation(kT[0:HEAD, :, 0, cols], src[0:HEAD], ACT.Copy)
                return A.activation(kT[HEAD:, :, 1, cols], src[HEAD:], ACT.Copy)

            def mixer0():
                m = M[0]
                norm(0)
                for t in range(TILES):
                    act.wait_ge(m.idx_ps, t + 1)
                    A.activation(idx_raw[:, t, :], ps[:, t % 2, 0:N_IDX0], ACT.Copy).then_inc(m.idx_raw_done, 1)
                for t in range(TILES):
                    if t >= 2:
                        act.wait_ge(m.rot_done, m.base["rot_done"] + t - 1)
                        act.wait_ge(m.sin_done, m.base["sin_done"] + t - 1)
                        act.wait_ge(m.v_done, t - 1)
                    if t >= 1:
                        act.wait_ge(m.head_ss_done, m.base["head_ss_done"] + t)
                    act.wait_ge(m.in_ps, m.base["in_ps"] + t + 1)
                    b0 = 2 + 2 * (t % 2)
                    src = ps[:, b0:b0 + 2, 0:N_QKV0 // 2]
                    A.activation(qk_sq0.rearrange("p (a n) -> p a n", a=2), src, ACT.Square).then_inc(m.sq_done, 1)
                    A.activation(qk_raw0[:, t % 2, :].rearrange("p (a n) -> p a n", a=2), src, ACT.Copy).then_inc(m.raw_done, 1)
                for t in range(TILES):
                    act.wait_ge(m.idxT_ps, t + 1)
                    cols = slice(PARTS * t, PARTS * t + PARTS)
                    A.activation(idx_qT[:, :, cols], ps[:, 6 + t % 2, 0:2 * PARTS].rearrange("p (c n) -> p c n", c=2), ACT.Copy)
                    keys_out(idx_kT, t, ps[:, 6 + t % 2, 2 * PARTS:3 * PARTS]).then_inc(m.idxT_done, 1)
                for t in range(1, TILES):
                    keys = PARTS * (t + 1)
                    for hd in range(IDX_HEADS):
                        n = (t - 1) * IDX_HEADS + hd
                        act.wait_ge(m.rel_ps, n + 1)
                        if n >= 2:
                            act.wait_ge(m.rel_used, n - 1)
                        A.activation(relu[:, n % 2, 0:keys], ps[:, hd, 0:keys], ACT.Relu, scale=SCALE).then_inc(m.rel_done, 1)
                for t in range(TILES):
                    for g in range(2):
                        act.wait_ge(m.qkT_ps, m.base["qkT_ps"] + 2 * t + g + 1)
                        if g == 0:
                            A.activation(qT0[:, :, PARTS * t:PARTS * t + PARTS], ps[:, 6, :].rearrange("p (c n) -> p c n", c=4), ACT.Copy).then_inc(m.qkT_done, 1)
                        else:
                            keys_out(kT0, t, ps[:, 7, 0:PARTS]).then_inc(m.qkT_done, 1)
                for c in range(CONV // PARTS):
                    for g in range(3):
                        act.wait_ge(m.conv_ps, 3 * c + g + 1)
                        if c >= 1:
                            act.wait_ge(m.conv_done, c)
                        A.activation(conv_in[:, g, :], ps[:, conv_bank(c, g), :], ACT.Copy).then_inc(m.conv_in_done, 1)
                attention(0, DSA_HEADS)

            def mixer1():
                m = M[1]
                norm(2)
                for t in range(TILES):
                    act.wait_ge(m.in_ps, m.base["in_ps"] + t + 1)
                    b0 = 3 * (t % 2)
                    if t >= 2:
                        act.wait_ge(m.rot_done, m.base["rot_done"] + t - 1)
                    for g, (lo, hi) in enumerate(((0, 512), (512, 1024), (1024, 1280))):
                        last = A.activation(qk_sq1[t % 2][:, lo:hi], ps[:, b0 + g, 0:hi - lo], ACT.Square)
                    last.then_inc(m.sq_done, 1)
                    for g, (lo, hi) in enumerate(((0, 512), (512, 1024), (1024, 1280))):
                        last = A.activation(qk_raw1[t % 2][:, lo:hi], ps[:, b0 + g, 0:hi - lo], ACT.Copy)
                    last.then_inc(m.raw_done, 1)
                    if t:
                        transposed_out(t - 1)
                act.wait_ge(m.in_ps, m.base["in_ps"] + TILES + 1)
                A.activation(v1.rearrange("p (a t) n -> p a (t n)", a=2), ps[:, 0:2, :], ACT.Copy).then_inc(m.raw_done, 1)
                transposed_out(TILES - 1)
                attention(1, DIL_HEADS)

            def transposed_out(t):
                m = M[1]
                for g in range(3):
                    act.wait_ge(m.qkT_ps, m.base["qkT_ps"] + 3 * t + g + 1)
                    bank = ps[:, 6 + (3 * t + g) % 2, :]
                    if g < 2:
                        A.activation(qT1[:, 4 * g:4 * g + 4, PARTS * t:PARTS * t + PARTS], bank.rearrange("p (c n) -> p c n", c=4), ACT.Copy).then_inc(m.qkT_done, 1)
                    else:
                        keys_out(kT1, t, bank).then_inc(m.qkT_done, 1)

            def moe(l):
                s = L[l]
                norm(2 * l + 1)
                act.wait_ge(s.logitT_ps, TILES)
                A.activation(logitT, ps[0:N_ROUTER, 4, :], ACT.Copy).then_inc(s.logitT_done, 1)
                act.wait_ge(s.exp_in, 1)
                nc.scalar.activation(exp4[:, :, :], at4[:, :, :], ACT.Exp).then_inc(s.exp_done, 1)
                act.wait_ge(s.exp_in, 2)
                nc.scalar.activation(e21[:, :], gap[:, :], ACT.Exp).then_inc(s.exp_done, 1)

                def expert_pair(pair):
                    for u in range(2):
                        act.wait_ge(s.parts_done, 6 * pair + 2 * u + 1)
                        if u:
                            act.wait_ge(s.h_done, 2 * pair + 1)
                        A.activation(silu, ps[:, 1, 0:256], ACT.Silu).then_inc(s.silu_done, 1)
                    for u in range(2):
                        act.wait_ge(s.h_transposed, 2 * pair + u + 1)
                        A.activation(hT[u], ps[:, 3, 0:256], ACT.Copy).then_inc(s.hT_done, 1)
                    act.wait_ge(s.gateT_ps, pair + 1)
                    A.activation(gateT, ps[:, 0, :].rearrange("p (t n) -> p t n", t=TILES), ACT.Copy).then_inc(s.gateT_done, 1)
                    act.wait_ge(s.y_half_ps, pair + 1)
                    A.activation(y[:, 0:512], ps[:, 4, :], ACT.Copy).then_inc(s.y_evac, 1)
                    act.wait_ge(s.parts_done, 6 * pair + 6)
                    A.activation(y[:, 512:1024], ps[:, 5, :], ACT.Copy).then_inc(s.y_evac, 1)

                def steps(b):
                    with act.Fori(0, N_EXPERTS // 2) as i:
                        expert_pair(b * (N_EXPERTS // 2) + i)
                steps(0)
                act.wait_ge(s.count_done, 1)
                most = act.value_load(max_count[0:1, 0:1], min_val=0, max_val=TOKENS)
                with act.If(most > CAP):
                    with act.Fori(1, LEVELS) as b:
                        with act.If(most > b * CAP):
                            steps(b)
            mixer0()
            moe(0)
            mixer1()
            moe(1)

        @block.vector
        def _(dve):
            chain = [0]

            def link(ins):
                chain[0] += 1
                ins.then_inc(dve_chain, 1)
                dve.wait_ge(dve_chain, chain[0])
            V = nc.vector

            def over(v, n):
                return v.unsqueeze(2).broadcast_to([PARTS, v.shape[1], n])

            dve.wait_ge(consts_in, 16)
            V.tensor_copy(ones, con("ones"))
            V.tensor_copy(before, con("before"))
            dve.wait_ge(gain_ps, 1)
            link(V.tensor_copy(gain[:, :, :], ps[:, 5, 0:4 * CHUNKS].rearrange("p (z c) -> p z c", z=4)))

            def norm(z, before=lambda t: None):
                tok = token_major[z % 2][:, :].rearrange("p (t d) -> p t d", t=TILES)
                tr = feature_major[z % 2][:, :].rearrange("p (c n) -> p c n", c=CHUNKS)
                for step in range(TILES + 2):
                    if step < TILES:
                        before(step)
                    t = step - 1
                    if 0 <= t < TILES:
                        dve.wait_ge(N[z].rstd_done, N[z].base["rstd_done"] + t + 1)
                        V.tensor_scalar(tok[:, t, :], x_res[:, t, :], sumsq[:, t:t + 1], None, ALU.mult).then_inc(N[z].xn_done, 1)
                    t = step - 2
                    if 0 <= t < TILES:
                        for g in range(2):
                            dve.wait_ge(N[z].xT_ps, N[z].base["xT_ps"] + 2 * t + g + 1)
                            V.tensor_tensor(tr[:, 4 * g:4 * g + 4, PARTS * t:PARTS * t + PARTS], ps[:, 6 + g, :].rearrange("p (c n) -> p c n", c=4),
                                            gain[:, z, 4 * g:4 * g + 4].unsqueeze(2).broadcast_to([PARTS, 4, PARTS]), ALU.mult).then_inc(N[z].xT_done, 1)

            def heads_of(v):
                return v.rearrange("p (h d) -> p h d", d=HEAD)

            def on_heads(v, heads):
                return v.unsqueeze(1).broadcast_to([PARTS, heads, HEAD])

            def zero_halves(m, *keys):
                for kT in keys:
                    V.memset(kT[HEAD:, :, 0, :], 0.0)
                    last = V.memset(kT[0:HEAD, :, 1, :], 0.0)
                last.then_inc(m.zeros_done, 1)

            def tables(l):
                dve.wait_ge(M[l].head_gain_in, M[l].base["head_gain_in"] + 96)
                for j in range(4):
                    base = con("rope_sin" if j % 2 else "rope_cos").rearrange("p (t d) -> p t d", d=HEAD)
                    last = V.tensor_tensor(rope[:, j, :, :], base, on_heads(head_gain[:, j, :], TILES), ALU.mult)
                link(last)
                dve.sem_inc(M[l].tables_done, 1)

            def rotate(m, t, raw, sin, rot, qh, kh):
                nq, nk = qh * HEAD, kh * HEAD
                dve.wait_ge(m.sq_done, m.base["sq_done"] + t + 1)
                sq = qk_sq0[:, 0:nq + nk] if qh == DSA_HEADS else qk_sq1[t % 2]
                V.tensor_reduce(head_ss[:, t % 2, 0:qh + kh], heads_of(sq), AX, ALU.add).then_inc(m.head_ss_done, 1)
                dve.wait_ge(m.head_rstd_done, m.base["head_rstd_done"] + t + 1)
                dve.wait_ge(m.raw_done, m.base["raw_done"] + t + 1)
                r3 = heads_of(raw[:, 0:nq + nk])
                V.tensor_tensor(r3, r3, head_ss[:, t % 2, 0:qh + kh].unsqueeze(2).broadcast_to([PARTS, qh + kh, HEAD]), ALU.mult).then_inc(m.normed, 1)
                dve.wait_ge(m.normed, m.base["normed"] + t + 1)
                q_rot = heads_of(rot[:, 0:nq])
                k_rot = rot[:, nq:nq + 2 * nk].rearrange("p (h two d) -> p h two d", two=2, d=HEAD)
                V.tensor_tensor(q_rot, r3[:, 0:qh, :], on_heads(rope[:, 0, t, :], qh), ALU.mult)
                link(V.tensor_tensor(k_rot[:, :, 0, :], r3[:, qh:, :], on_heads(rope[:, 2, t, :], kh), ALU.mult))
                dve.wait_ge(m.sin_done, m.base["sin_done"] + t + 1)
                V.tensor_tensor(q_rot, q_rot, sin[:, 0:qh, :], ALU.add)
                link(V.tensor_tensor(k_rot[:, :, 1, :], k_rot[:, :, 0, :], sin[:, qh:, :], ALU.add))
                link(V.tensor_tensor(k_rot[:, :, 0, :], k_rot[:, :, 0, :], sin[:, qh:, :], ALU.add))
                dve.sem_inc(m.rot_done, 1)

            def attention(l, heads, mask_of):
                m = M[l]
                pairs = TILES * heads // 2
                for n in range(pairs + 4):
                    if n < pairs:
                        t = n * 2 // heads
                        keys = PARTS * (t + 1)
                        for u in range(2):
                            b = 2 * (n % 2) + u
                            dve.wait_ge(m.s_ps, m.base["s_ps"] + 2 * n + u + 1)
                            if n >= 2:
                                dve.wait_ge(m.pT_ps, m.base["pT_ps"] + 2 * n - 3 + u)
                            V.tensor_tensor_reduce(out=prob[:, b, 0:keys], in0=ps[:, b, 0:keys], in1=mask_of(t), scale=-SCALE, scalar=-TAKEN,
                                                   op0=ALU.add, op1=ALU.min, accum_out=neg_max[:, b:b + 1]).then_inc(m.masked_done, 1)
                    e = n - 1
                    if 0 <= e < pairs:
                        keys = PARTS * (e * 2 // heads + 1)
                        if e % 4 == 3:
                            g = e // 4
                            dve.wait_ge(m.exp_done, m.base["exp_done"] + 2 * e + 2)
                            V.reciprocal(denom[:, g % 2, :], denom[:, g % 2, :]).then_inc(m.inv_done, 1)
                        dve.wait_ge(m.pT_ps, m.base["pT_ps"] + 2 * e + 1)
                        if e:
                            dve.wait_ge(m.pv_done, m.base["pv_done"] + e)
                        V.tensor_copy(probT[:, 0, 0:keys], ps[:, 4, 0:keys]).then_inc(m.pT_dve, 1)
                    e = n - 3
                    if 0 <= e < pairs and e % 4 == 3:
                        t, c0, group = block_of(e, heads)
                        dve.wait_ge(m.o_done, m.base["o_done"] + group + 1)
                        dve.wait_ge(m.spread_ps, m.base["spread_ps"] + group + 1)
                        out = mixed[:, c0:c0 + 4, PARTS * t:PARTS * t + PARTS]
                        V.tensor_tensor(out, out, ps[:, 7, :].rearrange("p (c n) -> p c n", c=4), ALU.mult).then_inc(m.mixed_done, 1)

            def project_out(l, t):
                m = M[l]
                for hf in range(2):
                    n = 2 * t + hf
                    dve.wait_ge(m.out_ps, m.base["out_ps"] + n + 1)
                    cols = slice(512 * hf, 512 * hf + 512)
                    V.tensor_tensor(x_res[:, t, cols], x_res[:, t, cols], ps[:, n % 4, :], ALU.add).then_inc(m.out_half, 1)
                dve.wait_ge(m.out_half, m.base["out_half"] + 2 * t + 2)
                dve.sem_inc(x_ready[2 * l + 1], 1)

            def mixer0():
                m = M[0]
                dve.wait_ge(consts_in, 16)
                norm(0)
                zero_halves(m, idx_kT, kT0)
                tables(0)
                base_cos = con("rope_cos").rearrange("p (t d) -> p t d", d=HEAD)
                n_idx = (IDX_HEADS + 1) * HEAD
                for t in range(TILES):
                    dve.wait_ge(m.idx_raw_done, t + 1)
                    rot = idx_rot[:, t, :]
                    link(V.tensor_tensor(heads_of(rot[:, 0:n_idx]), heads_of(idx_raw[:, t, 0:n_idx]), on_heads(base_cos[:, t, :], IDX_HEADS + 1), ALU.mult))
                    dve.wait_ge(m.idx_sin_done, t + 1)
                    link(V.tensor_tensor(rot[:, n_idx:], rot[:, n_idx - HEAD:n_idx], idx_sin[:, IDX_HEADS, :], ALU.add))
                    link(V.tensor_tensor(heads_of(rot[:, 0:n_idx]), heads_of(rot[:, 0:n_idx]), idx_sin, ALU.add))
                    dve.sem_inc(m.idx_rot_done, 1)
                for t in range(TILES):
                    rotate(m, t, qk_raw0[:, t % 2, :], qk_sin0, qk_rot0[:, t, :], DSA_HEADS, 1)
                dve.wait_ge(m.idx_w_done, TILES)
                for t in range(1, TILES):
                    for hd in range(IDX_HEADS):
                        n = (t - 1) * IDX_HEADS + hd
                        dve.wait_ge(m.rel_done, n + 1)
                        rel = relu[:, n % 2, 0:PARTS * (t + 1)]
                        if hd == 0:
                            V.tensor_scalar(score[t], rel, idx_w[:, t, hd:hd + 1], None, ALU.mult).then_inc(m.rel_used, 1)
                        else:
                            V.scalar_tensor_tensor(score[t], rel, idx_w[:, t, hd:hd + 1], score[t], ALU.mult, ALU.add).then_inc(m.rel_used, 1)
                        dve.wait_ge(m.rel_used, n + 1)
                    own = score[t][:, PARTS * t:]
                    link(V.tensor_tensor(own, own, con("causal"), ALU.add))
                for t in range(1, TILES):
                    for _ in range(DSA_KEEP // 8):
                        link(V.max(best8[:, :], score[t]))
                        link(V.match_replace(score[t], best8[:, :], score[t], TAKEN))
                    link(V.tensor_scalar(score[t], score[t], TAKEN, -BIG, ALU.not_equal, ALU.mult))
                attention(0, DSA_HEADS, lambda t: score[t] if t else con("causal"))

            def mixer1():
                m = M[1]
                norm(2)
                zero_halves(m, kT1)
                tables(1)
                for t in range(TILES):
                    if t >= 2:
                        dve.wait_ge(m.qkT_ps, m.base["qkT_ps"] + 3 * (t - 1))
                    rotate(m, t, qk_raw1[t % 2], heads_of(qk_sq1[t % 2]), qk_rot1[:, t % 2, :], DIL_HEADS, DIL_KV)
                attention(1, DIL_HEADS, lambda t: con("strip")[:, TOKENS - PARTS * (t + 1):])

            def moe(l):
                s = L[l]
                norm(2 * l + 1, lambda t: project_out(l, t))
                dve.wait_ge(s.router_in, 128)
                dve.wait_ge(s.logits_done, 1)
                link(V.tensor_tensor(logit[:, :, :], ps[:, 5, 0:TILES * N_ROUTER].rearrange("p (t n) -> p t n", t=TILES),
                                     b_router[:, :].unsqueeze(1).broadcast_to([PARTS, TILES, N_ROUTER]), ALU.add))
                lg, le = logit[:, :, 0:N_GROUPS], logit[:, :, N_GROUPS:]

                def first_of_max(values, best, index, out, work, n, iota):
                    link(V.tensor_reduce(best, values, AX, ALU.max))
                    link(V.tensor_tensor(work, values, over(best, n), ALU.is_equal))
                    link(V.scalar_tensor_tensor(work, work, -64.0, iota.unsqueeze(1).broadcast_to([PARTS, TILES, n]), ALU.mult, ALU.add))
                    link(V.tensor_reduce(index, work, AX, ALU.min))
                    link(V.tensor_tensor(out, work, over(index, n), ALU.is_equal))
                first_of_max(lg, gmax, gidx, hot4, pen4, N_GROUPS, con("iota_group"))
                V.tensor_tensor(at4, lg, over(gmax, N_GROUPS), ALU.subtract).then_inc(s.exp_in, 1)
                link(V.tensor_scalar(pen4, hot4, -1.0, BIG, ALU.add, ALU.mult))
                link(V.tensor_tensor(lm.rearrange("p t (g e) -> p t g e", g=N_GROUPS), le.rearrange("p t (g e) -> p t g e", g=N_GROUPS),
                                     pen4.unsqueeze(3).broadcast_to([PARTS, TILES, N_GROUPS, PER_GROUP]), ALU.add))
                first_of_max(lm, top[0], eid[:, 0, :], hot[0], tmp, N_EXPERTS, con("iota_expert"))
                link(V.scalar_tensor_tensor(lm, hot[0], -BIG, lm, ALU.mult, ALU.add))
                first_of_max(lm, top[1], eid[:, 1, :], hot[1], tmp, N_EXPERTS, con("iota_expert"))
                V.tensor_tensor(picked, hot[0], hot[1], ALU.add).then_inc(s.picked_done, 1)
                V.tensor_tensor(gap, top[1], top[0], ALU.subtract).then_inc(s.exp_in, 1)
                for k in range(TOP_K):
                    V.tensor_scalar(row_hot[:, :, k, 0:N_EXPERTS], hot[k], con("row"), None, ALU.mult)
                    V.tensor_tensor(row_hot[:, :, k, N_EXPERTS:], hot[k], over(con("tile_row"), N_EXPERTS), ALU.mult)
                dve.wait_ge(s.rank_done, 1)
                ranks = ps[:, 6, 0:TILES * N_EXPERTS].rearrange("p (t e) -> p t e", t=TILES)
                for k in range(TOP_K):
                    link(V.tensor_tensor(tmp, hot[k], ranks, ALU.mult))
                    link(V.tensor_reduce(rank[:, k, :], tmp, AX, ALU.add))

                def slot_hots():
                    for k in range(TOP_K):
                        last = V.tensor_tensor(slot_hot[:, :, k, :], con("iota_slot").unsqueeze(1).broadcast_to([PARTS, TILES, PARTS]),
                                               over(rank[:, k, :], PARTS), ALU.is_equal)
                    last.then_inc(s.hot_ready, 1)
                slot_hots()

                def counts_and_gates():
                    dve.wait_ge(s.rank_done, 2)
                    link(V.tensor_reduce(tmp[:, 0, :], ps[:, 4, 0:TILES * N_EXPERTS].rearrange("p (t e) -> p e t", t=TILES), AX, ALU.add))
                    link(V.tensor_reduce(cmax, tmp[:, 0, :], AX, ALU.max))
                    V.tensor_copy(max_count[:, :], cmax).then_inc(s.count_done, 1)
                    dve.wait_ge(s.exp_done, 2)
                    link(V.tensor_reduce(p_group, exp4, AX, ALU.add))
                    link(V.reciprocal(p_group, p_group))
                    link(V.tensor_scalar(inv, e21, 1.0, None, ALU.add))
                    link(V.reciprocal(inv, inv))
                    link(V.tensor_tensor(gates[:, 0, :], p_group, inv, ALU.mult))
                    link(V.tensor_tensor(gates[:, 1, :], gates[:, 0, :], e21, ALU.mult))
                    for k in range(TOP_K):
                        link(V.tensor_tensor(hot[k], hot[k], over(gates[:, k, :], N_EXPERTS), ALU.mult))

                def experts(pair, i):
                    for u in range(2):
                        dve.wait_ge(s.x_transposed, 2 * pair + u + 1)
                        V.tensor_tensor(xT[u].rearrange("p (c h s) -> p c h s", h=2, s=CAP),
                                        ps[:, 0, :].rearrange("p (c h s) -> p c h s", h=2, s=CAP),
                                        gain_of4[:, l, :].rearrange("p (h c) -> p c h", h=2).unsqueeze(3).broadcast_to([PARTS, 4, 2, CAP]),
                                        ALU.mult).then_inc(s.xT_done, 1)
                        if u == 0:
                            for k, out in enumerate((gate_at, gate_at2)):
                                V.tensor_tensor(out.rearrange("p t (u s) -> p t u s", u=2), slot_hot[:, :, k, :].rearrange("p t (u s) -> p t u s", u=2),
                                                hot[k][:, :, bass.ds(2 * i, 2)].unsqueeze(3).broadcast_to([PARTS, TILES, 2, CAP]), ALU.mult).then_inc(s.gate_steps, 1)
                            dve.wait_ge(s.gate_steps, 3 * pair + 2)
                            V.tensor_tensor(gate_at, gate_at, gate_at2, ALU.add).then_inc(s.gate_steps, 1)
                        dve.wait_ge(s.silu_done, 2 * pair + u + 1)
                        dve.wait_ge(s.parts_done, 6 * pair + 2 * u + 2)
                        if u:
                            dve.wait_ge(s.h_transposed, 2 * pair + 1)
                        V.tensor_tensor(h, silu, ps[:, 2, 0:256], ALU.mult).then_inc(s.h_done, 1)

                def add(pair, wait_before=True, x_over=False):
                    if wait_before:
                        dve.wait_ge(s.added, 2 * TILES * pair)
                    for n in range(2 * TILES):
                        hf, t = divmod(n, TILES)
                        dve.wait_ge(s.added_ps, 2 * TILES * pair + n + 1)
                        cols = slice(512 * hf, 512 * hf + 512)
                        V.tensor_tensor(x_res[:, t, cols], x_res[:, t, cols], ps[:, 6 + n % 2, :], ALU.add).then_inc(s.added, 1)
                        if x_over and hf == 1:
                            dve.wait_ge(s.added, 2 * TILES * pair + n + 1)
                            dve.sem_inc(x_ready[2 * l + 2], 1)

                def steps(b, first_pass=False):
                    dve.wait_ge(s.fetch_ps, b + 1)
                    V.tensor_reduce(row_of, ps[:, 7, 0:2 * N_EXPERTS].rearrange("p (a e) -> p e a", a=2), AX, ALU.add).then_inc(s.fetch_done, 1)
                    dve.wait_ge(s.fetch_done, 2 * b + 1)
                    V.tensor_scalar(fetch[:, :], row_of, con("half"), None, ALU.add).then_inc(s.fetch_done, 1)
                    if first_pass:
                        counts_and_gates()
                    first = b * (N_EXPERTS // 2)
                    experts(first, 0)
                    if first_pass:
                        experts(1, 1)
                        add(0, wait_before=False)
                    with dve.Fori(2 if first_pass else 1, N_EXPERTS // 2) as i:
                        experts(first + i, i)
                        add(first + i - 1)
                    if not first_pass:
                        add(first + N_EXPERTS // 2 - 1)
                        dve.wait_ge(s.added, 2 * TILES * (first + N_EXPERTS // 2))
                        dve.sem_inc(s.passes_over, 1)
                steps(0, first_pass=True)
                most = dve.value_load(max_count[0:1, 0:1], min_val=0, max_val=TOKENS)
                with dve.If(most <= CAP):
                    add(N_EXPERTS // 2 - 1, x_over=True)
                with dve.If(most > CAP):
                    add(N_EXPERTS // 2 - 1)
                    dve.wait_ge(s.added, TILES * N_EXPERTS)
                    dve.sem_inc(s.passes_over, 1)
                    with dve.Fori(1, LEVELS) as b:
                        with dve.If(most > b * CAP):
                            V.tensor_scalar(rank, rank, -float(CAP), None, ALU.add).then_inc(s.rank_shifted, 1)
                            dve.wait_ge(s.rank_shifted, b)
                            dve.wait_ge(s.fetch_copied, b * N_EXPERTS)
                            slot_hots()
                            steps(b)
                    for t in range(TILES):
                        dve.sem_inc(x_ready[2 * l + 2], 1)

            mixer0()
            moe(0)
            mixer1()
            moe(1)

        @block.tensor
        def _(pe):
            pe.wait_ge(consts_in, 16)

            T = nc.tensor
            pe.wait_ge(params_in, 64)
            T.transpose(ps[:, 5, 0:4 * CHUNKS], gain_rows, ident[0:4 * CHUNKS, 0:4 * CHUNKS]).then_inc(gain_ps, 1)

            def transpose_x(z, t):
                tok = token_major[z % 2][:, :].rearrange("p (t d) -> p t d", t=TILES)
                pe.wait_ge(N[z].xn_done, N[z].base["xn_done"] + t + 1)
                for g in range(2):
                    if t:
                        pe.wait_ge(N[z].xT_done, N[z].base["xT_done"] + 2 * t + g - 1)
                    for j in range(4):
                        at = 512 * g + PARTS * j
                        last = T.transpose(ps[:, 6 + g, PARTS * j:PARTS * j + PARTS], tok[:, t, at:at + PARTS], ident)
                    last.then_inc(N[z].xT_ps, 1)

            def x_by_features(z, t):
                pe.wait_ge(N[z].xT_done, N[z].base["xT_done"] + 2 * t + 2)

            def project(out, src, cols, w, lo, hi):
                for c in range(CHUNKS):
                    last = T.matmul(out, src[:, c, cols], w[:, c, lo:hi], start=c == 0, stop=c == CHUNKS - 1)
                return last

            def attention(l, heads, qT, kT, v, kv_of):
                m = M[l]
                pairs = TILES * heads // 2
                for n in range(pairs + 4):
                    if n < pairs:
                        t, pair = divmod(n, heads // 2)
                        for u in range(2):
                            if n >= 2:
                                pe.wait_ge(m.masked_done, m.base["masked_done"] + 2 * n - 3 + u)
                            T.matmul(ps[:, 2 * (n % 2) + u, 0:PARTS * (t + 1)], qT[:, pair, PARTS * t:PARTS * t + PARTS],
                                     kT[:, kv_of(2 * pair), u, 0:PARTS * (t + 1)], start=True, stop=True).then_inc(m.s_ps, 1)
                    e = n - 1
                    if 0 <= e < pairs:
                        for u in range(2):
                            pe.wait_ge(m.exp_done, m.base["exp_done"] + 2 * e + u + 1)
                            if e:
                                pe.wait_ge(m.pT_act if u else m.pT_dve, m.base["pT_act"] + e)
                            for kb in range(e * 2 // heads + 1):
                                blk = slice(PARTS * kb, PARTS * kb + PARTS)
                                last = T.transpose(ps[:, 4 + u, blk], prob[:, 2 * (e % 2) + u, blk], ident)
                            last.then_inc(m.pT_ps, 1)
                    e = n - 2
                    if 0 <= e < pairs:
                        t, pair = divmod(e, heads // 2)
                        if e % 4 == 0 and e:
                            pe.wait_ge(m.o_done, m.base["o_done"] + e // 4)
                        pe.wait_ge(m.pT_dve, m.base["pT_dve"] + e + 1)
                        pe.wait_ge(m.pT_act, m.base["pT_act"] + e + 1)
                        kv = kv_of(2 * pair)
                        for kb in range(t + 1):
                            for u in range(2):
                                last = T.matmul(ps[HEAD * u:HEAD * u + HEAD, 6, PARTS * (e % 4):PARTS * (e % 4) + PARTS],
                                                v[:, kb, HEAD * kv:HEAD * kv + HEAD], probT[:, u, PARTS * kb:PARTS * kb + PARTS], start=kb == 0, stop=kb == t)
                        last.then_inc(m.pv_done, 1)
                        if e % 4 == 3:
                            g = e // 4
                            pe.wait_ge(m.inv_done, m.base["inv_done"] + g + 1)
                            if g:
                                pe.wait_ge(m.mixed_done, m.base["mixed_done"] + g)
                            for c in range(4):
                                for u in range(2):
                                    last = T.matmul(ps[HEAD * u:HEAD * u + HEAD, 7, PARTS * c:PARTS * c + PARTS],
                                                    denom[:, g % 2, 2 * c + u:2 * c + u + 1].broadcast_to([PARTS, HEAD]), ident, start=True, stop=True)
                            last.then_inc(m.spread_ps, 1)

            def project_out(l, t):
                m = M[l]
                if t == 0:
                    pe.wait_ge(m.w_out_in, m.base["w_out_in"] + 16)
                    if l == 0:
                        pe.wait_ge(m.conv_done, CONV // PARTS)
                pe.wait_ge(m.mixed_done, m.base["mixed_done"] + (t + 1) * (DSA_HEADS if l == 0 else DIL_HEADS) // 8)
                for hf in range(2):
                    n = 2 * t + hf
                    if n >= 4:
                        pe.wait_ge(m.out_half, m.base["out_half"] + n - 3)
                    project(ps[:, n % 4, :], mixed, slice(PARTS * t, PARTS * t + PARTS), w_out, 512 * hf, 512 * hf + 512).then_inc(m.out_ps, 1)
                if t == TILES - 1:
                    pe.wait_ge(m.out_ps, m.base["out_ps"] + 2 * TILES)
                    pe.sem_inc(m.out_over, 1)

            def mixer0():
                m = M[0]
                hT0 = feature_major[0][:, :].rearrange("p (c n) -> p c n", c=CHUNKS)

                def conv(c, g):
                    if c >= 2:
                        pe.wait_ge(m.conv_in_done, 3 * (c - 2) + g + 1)
                    lo = (1, 2, 0)[g] * CONV + PARTS * c
                    for k in range(CHUNKS):
                        last = T.matmul(ps[:, conv_bank(c, g), :], w_conv[:, k, lo:lo + PARTS], hT0[:, k, :], start=k == 0, stop=k == CHUNKS - 1)
                    last.then_inc(m.conv_ps, 1)
                transpose_x(0, 0)
                for t in range(TILES):
                    if t < TILES - 1:
                        transpose_x(0, t + 1)
                    x_by_features(0, t)
                    if t == 0:
                        pe.wait_ge(m.w_in_a, 16)
                    if t >= 2:
                        pe.wait_ge(m.idx_raw_done, t - 1)
                    project(ps[:, t % 2, 0:N_IDX0], hT0, slice(PARTS * t, PARTS * t + PARTS), w_idx, 0, N_IDX0).then_inc(m.idx_ps, 1)
                pe.wait_ge(m.w_in_b, m.base["w_in_b"] + 16)
                for t in range(TILES):
                    if t >= 2:
                        pe.wait_ge(m.raw_done, m.base["raw_done"] + t - 1)
                    for hf in range(2):
                        last = project(ps[:, 2 + 2 * (t % 2) + hf, 0:N_QKV0 // 2], hT0, slice(PARTS * t, PARTS * t + PARTS), w_qkv0,
                                       hf * N_QKV0 // 2, (hf + 1) * N_QKV0 // 2)
                    last.then_inc(m.in_ps, 1)
                pe.wait_ge(m.in_ps, m.base["in_ps"] + TILES)
                pe.sem_inc(m.in_over, 1)
                for t in range(TILES):
                    pe.wait_ge(m.idx_rot_done, t + 1)
                    if t >= 2:
                        pe.wait_ge(m.idxT_done, t - 1)
                    for j in range(3):
                        last = T.transpose(ps[:, 6 + t % 2, PARTS * j:PARTS * j + PARTS], idx_rot[:, t, PARTS * j:PARTS * j + PARTS], ident)
                    last.then_inc(m.idxT_ps, 1)
                pe.wait_ge(m.zeros_done, m.base["zeros_done"] + 1)
                pe.wait_ge(m.raw_done, m.base["raw_done"] + TILES)
                pe.wait_ge(m.w_in_c, m.base["w_in_c"] + 16)
                conv(0, 0)
                pe.wait_ge(m.idxT_done, TILES)
                for t in range(1, TILES):
                    for hd in range(IDX_HEADS):
                        n = (t - 1) * IDX_HEADS + hd
                        if n >= IDX_HEADS:
                            pe.wait_ge(m.rel_done, n - IDX_HEADS + 1)
                        T.matmul(ps[:, hd, 0:PARTS * (t + 1)], idx_qT[:, hd // 2, PARTS * t:PARTS * t + PARTS], idx_kT[:, 0, hd % 2, 0:PARTS * (t + 1)],
                                 start=True, stop=True).then_inc(m.rel_ps, 1)
                conv(0, 1)
                for t in range(TILES):
                    pe.wait_ge(m.rot_done, m.base["rot_done"] + t + 1)
                    for g in range(2):
                        if t:
                            pe.wait_ge(m.qkT_done, m.base["qkT_done"] + 2 * t + g - 1)
                        for j in range(4 if g == 0 else 1):
                            last = T.transpose(ps[:, 6 + g, PARTS * j:PARTS * j + PARTS], qk_rot0[:, t, 512 * g + PARTS * j:512 * g + PARTS * j + PARTS], ident)
                        last.then_inc(m.qkT_ps, 1)
                pe.wait_ge(m.rel_done, 3 * IDX_HEADS)
                for c in range(CONV // PARTS):
                    for g in range(3):
                        if 3 * c + g >= 2:
                            conv(c, g)
                pe.wait_ge(m.conv_ps, 3 * CONV // PARTS)
                pe.sem_inc(m.conv_over, 1)
                pe.wait_ge(m.conv_in_done, 3 * CONV // PARTS)
                pe.wait_ge(m.qkT_done, m.base["qkT_done"] + 2 * TILES)
                pe.wait_ge(m.v_done, TILES)
                attention(0, DSA_HEADS, qT0, kT0, v0, lambda hd: 0)

            def mixer1():
                m = M[1]
                hT1 = feature_major[0][:, :].rearrange("p (c n) -> p c n", c=CHUNKS)
                transpose_x(2, 0)

                def transposes(t):
                    pe.wait_ge(m.rot_done, m.base["rot_done"] + t + 1)
                    for g in range(3):
                        if 3 * t + g >= 2:
                            pe.wait_ge(m.qkT_done, m.base["qkT_done"] + 3 * t + g - 1)
                        for j in range(4):
                            at = 512 * g + PARTS * j
                            last = T.transpose(ps[:, 6 + (3 * t + g) % 2, PARTS * j:PARTS * j + PARTS], qk_rot1[:, t % 2, at:at + PARTS], ident)
                        last.then_inc(m.qkT_ps, 1)
                for t in range(TILES):
                    if t < TILES - 1:
                        transpose_x(2, t + 1)
                    x_by_features(2, t)
                    if t >= 2:
                        pe.wait_ge(m.raw_done, m.base["raw_done"] + t - 1)
                    for g, arrived in enumerate(("w_in_a", "w_in_b", "w_in_c")):
                        if t == 0:
                            pe.wait_ge((m.w_in_a, m.w_in_b, m.w_in_c)[g], m.base[arrived] + 16)
                        hi = min(512 * g + 512, N_QK1)
                        last = project(ps[:, 3 * (t % 2) + g, 0:hi - 512 * g], hT1, slice(PARTS * t, PARTS * t + PARTS), w_in1, 512 * g, hi)
                    last.then_inc(m.in_ps, 1)
                    if t >= 2:
                        if t == 2:
                            x_by_features(2, TILES - 1)
                        transposes(t - 2)
                pe.wait_ge(m.raw_done, m.base["raw_done"] + TILES - 1)
                for t in range(TILES):
                    last = project(ps[:, t // 2, N_V1 * (t % 2):N_V1 * (t % 2 + 1)], hT1, slice(PARTS * t, PARTS * t + PARTS), w_in1, N_QK1, N_QK1 + N_V1)
                    if t == TILES // 2:
                        transposes(TILES - 2)
                last.then_inc(m.in_ps, 1)
                pe.wait_ge(m.in_ps, m.base["in_ps"] + TILES + 1)
                pe.sem_inc(m.in_over, 1)
                transposes(TILES - 1)
                pe.wait_ge(m.raw_done, m.base["raw_done"] + TILES + 1)
                pe.wait_ge(m.qkT_done, m.base["qkT_done"] + 3 * TILES)
                pe.wait_ge(m.zeros_done, m.base["zeros_done"] + 1)
                attention(1, DIL_HEADS, qT1, kT1, v1, lambda hd: hd // (DIL_HEADS // DIL_KV))

            def moe(l):
                s = L[l]
                z = 2 * l + 1

                def route(t):
                    if t == 0:
                        pe.wait_ge(s.router_in, 128)
                    x_by_features(z, t)
                    for c in range(CHUNKS):
                        last = T.matmul(ps[0:N_ROUTER, 4, PARTS * t:PARTS * t + PARTS], w_router[:, c, :], xnT[:, c, PARTS * t:PARTS * t + PARTS],
                                        start=c == 0, stop=c == CHUNKS - 1)
                    last.then_inc(s.logitT_ps, 1)
                for t in range(TILES - 1):
                    project_out(l, t)
                transpose_x(z, 0)
                project_out(l, TILES - 1)
                route(0)
                transpose_x(z, 1)
                transpose_x(z, 2)
                route(1)
                transpose_x(z, 3)
                route(2)
                route(3)
                pe.wait_ge(s.logitT_done, 1)
                for t in range(TILES):
                    last = T.transpose(ps[:, 5, N_ROUTER * t:N_ROUTER * (t + 1)], logitT[:, PARTS * t:PARTS * t + PARTS], ident[0:N_ROUTER, 0:N_ROUTER])
                last.then_inc(s.logits_done, 1)
                pe.wait_ge(s.picked_done, 1)
                both = picked.rearrange("p t e -> p (t e)")
                T.matmul(ps[:, 6, 0:TILES * N_EXPERTS], before, both, start=True, stop=False)
                for back in range(1, TILES):
                    n = (TILES - back) * N_EXPERTS
                    last = T.matmul(ps[:, 6, N_EXPERTS * back:TILES * N_EXPERTS], ones, both[:, 0:n], start=False, stop=back == TILES - 1)
                last.then_inc(s.rank_done, 1)
                T.matmul(ps[:, 4, 0:TILES * N_EXPERTS], ones, both, start=True, stop=True).then_inc(s.rank_done, 1)

                FIRST, SECOND, LATER = range(3)

                def transpose_rows(pair, u, arrived):
                    pe.wait_ge(s.xg_in[u], arrived)
                    for j in range(4):
                        last = T.transpose(ps[:, 0, PARTS * j:PARTS * j + PARTS], xg[u].rearrange("s (p j) -> s j p", j=4)[:, j, :], ident)
                    last.then_inc(s.x_transposed, 1)
                    pe.wait_ge(s.xT_done, 2 * pair + u + 1)

                def weights(pair, u, part, place):
                    q, j = ORDER.index((u, part)), 3 * u + part
                    if q < AHEAD and place == SECOND:
                        pe.wait_ge(s.ahead_in[q], 16)
                        return ahead(q)
                    loads = pair if q < AHEAD and place == LATER else pair + 1
                    pe.wait_ge(s.weights_in[j], loads * 16)
                    return ring_part(j)

                def hidden(pair, u, part, place):
                    w = weights(pair, u, part, place)
                    for c in range(CHUNKS):
                        x_c = xT[u][:, PARTS * (c % 4) + CAP * (c // 4):PARTS * (c % 4) + CAP * (c // 4) + CAP]
                        for hf in range(2):
                            last = T.matmul(ps[CAP * hf:CAP * hf + CAP, 1 + part, 0:256], x_c, w[:, c, 256 * hf:256 * hf + 256],
                                            start=c == 0, stop=c == CHUNKS - 1)
                    last.then_inc(s.parts_done, 1)

                def transpose_h(pair, u):
                    pe.wait_ge(s.h_done, 2 * pair + u + 1)
                    if u:
                        pe.wait_ge(s.hT_done, 2 * pair + 1)
                    for j in range(2):
                        last = T.transpose(ps[:, 3, PARTS * j:PARTS * j + PARTS], h[:, PARTS * j:PARTS * j + PARTS], ident)
                    last.then_inc(s.h_transposed, 1)

                def gated(pair, hf, first=False):
                    pe.wait_ge(s.y_evac, 2 * pair + hf + 1)
                    for t in range(TILES):
                        n = TILES * hf + t
                        if not first or n >= 2:
                            pe.wait_ge(s.added, 2 * TILES * pair + n - 1)
                        T.matmul(ps[:, 6 + n % 2, :], gateT[:, t, :], y[:, 512 * hf:512 * hf + 512], start=True, stop=True).then_inc(s.added_ps, 1)

                def experts(pair, place, gates_before=True):
                    arrived = (pair + 1) * 16
                    if place != FIRST:
                        pe.wait_ge(s.gateT_done, pair)
                    transpose_rows(pair, 0, arrived)
                    hidden(pair, 0, 0, place)
                    hidden(pair, 0, 1, place)
                    transpose_rows(pair, 1, arrived)
                    pe.wait_ge(s.silu_done, 2 * pair + 1)
                    hidden(pair, 1, 0, place)
                    transpose_h(pair, 0)
                    hidden(pair, 1, 1, place)
                    if gates_before:
                        gated(pair - 1, 0, place == SECOND)
                    transpose_h(pair, 1)
                    if gates_before:
                        gated(pair - 1, 1, place == SECOND)
                    pe.wait_ge(s.gate_steps, 3 * pair + 3)
                    for t in range(TILES):
                        last = T.transpose(ps[:, 0, PARTS * t:PARTS * t + PARTS], gate_at[:, t, :], ident)
                    last.then_inc(s.gateT_ps, 1)
                    w = [weights(pair, u, 2, place) for u in range(2)]
                    pe.wait_ge(s.hT_done, 2 * pair + 2)
                    for hf in range(2):
                        for c in range(4):
                            for u in range(2):
                                h_c = hT[u][:, PARTS * (c % 2) + CAP * (c // 2):PARTS * (c % 2) + CAP * (c // 2) + CAP]
                                last = T.matmul(ps[CAP * u:CAP * u + CAP, 4 + hf, :], h_c, w[u][:, c, 512 * hf:512 * hf + 512],
                                                start=c == 0, stop=c == 3)
                                if c == 3 and hf == 1:
                                    last.then_inc(s.parts_done, 1)
                        if hf == 0:
                            last.then_inc(s.y_half_ps, 1)

                def steps(b, first_pass=False):
                    pe.wait_ge(s.hot_ready, b + 1)
                    for t in range(TILES):
                        for k in range(TOP_K):
                            last = T.matmul(ps[:, 7, 0:2 * N_EXPERTS], slot_hot[:, t, k, :], row_hot[:, t, k, :],
                                            start=t + k == 0, stop=t + k == TILES + TOP_K - 2)
                    last.then_inc(s.fetch_ps, 1)
                    first = b * (N_EXPERTS // 2)
                    experts(first, FIRST if first_pass else LATER, gates_before=False)
                    if first_pass:
                        experts(1, SECOND)
                    with pe.Fori(2 if first_pass else 1, N_EXPERTS // 2) as i:
                        experts(first + i, LATER)
                    for hf in range(2):
                        gated(first + N_EXPERTS // 2 - 1, hf)
                steps(0, first_pass=True)
                pe.wait_ge(s.count_done, 1)
                most = pe.value_load(max_count[0:1, 0:1], min_val=0, max_val=TOKENS)
                with pe.If(most > CAP):
                    with pe.Fori(1, LEVELS) as b:
                        with pe.If(most > b * CAP):
                            steps(b)
            mixer0()
            moe(0)
            mixer1()
            moe(1)


_SHARED = ["x"]
_BY_LAYER = ["attn_norm", "w_in", "q_norm", "k_norm", "w_out", "ffn_norm", "w_rg", "b_rg", "w_re", "b_re", "w_gate", "w_up", "w_down"]
_INS = _SHARED + ["conv_w_0"] + [f"{n}_{l}" for l in range(2) for n in _BY_LAYER]


def kernel(**inputs):
    import numpy as _np
    import concourse.bacc as _bacc
    from concourse import mybir as _mybir
    from concourse.bass_utils import run_bass_kernel_spmd as _run

    nc = _bacc.Bacc("TRN2", target_bir_lowering=False, num_devices=1)
    arrays, aps = {}, {}
    for name in _INS + ["consts"]:
        a = constant_table() if name == "consts" else _np.ascontiguousarray(inputs[name])
        if name == "x":
            a = a.reshape(TOKENS, D_MODEL)
        arrays[f"in_{name}_dram"] = a
        aps[name] = nc.dram_tensor(f"in_{name}_dram", a.shape, _mybir.dt.from_np(a.dtype), kind="ExternalInput").ap()
    aps["out"] = nc.dram_tensor("out_0_dram", (TOKENS, D_MODEL), _mybir.dt.float32, kind="ExternalOutput").ap()
    trunk(nc, aps)
    r = _run(nc, [arrays], core_ids=[0])
    return r.results[0]["out_0_dram"].reshape(1, TOKENS, D_MODEL)
```
